# Optimizing a Trainium2 kernel written in Bass

```python
import jax, jax.numpy as jnp
from jax import lax
import numpy as np
import math

D_MODEL = 1024
BATCH = 1
SEQ = 512
DEPTH = 1

CHUNK = 64
Q_BLOCK = 128
HEAD_DIM = 64
N_HEADS_SB = 8
N_HEADS_FOX = 8
D_SB = N_HEADS_SB * HEAD_DIM
D_FOX = N_HEADS_FOX * HEAD_DIM
N_BRANCH = 2
IN_SIZES = (D_SB, D_SB, D_SB, D_SB,
            D_FOX, D_FOX, D_FOX, D_FOX,
            N_HEADS_FOX,
            N_BRANCH * D_MODEL)
D_IN = sum(IN_SIZES)
EPS = 1e-6
NEG_BIG = -1e30


def _rmsnorm(x, g):
    xf = x.astype(jnp.float32)
    inv = lax.rsqrt(jnp.mean(xf * xf, axis=-1, keepdims=True) + EPS)
    return (xf * inv).astype(x.dtype) * g

def _to_heads(t, n_heads):
    b, s, _ = t.shape
    return t.reshape(b, s, n_heads, HEAD_DIM).transpose(0, 2, 1, 3)

def _from_heads(t):
    b, h, s, d = t.shape
    return t.transpose(0, 2, 1, 3).reshape(b, s, h * d)

def _stick_breaking(q, k, v):
    s_len = q.shape[2]
    scale = HEAD_DIM ** -0.5
    outs = []
    for start in range(0, s_len, Q_BLOCK):
        end = start + Q_BLOCK
        qb, kb, vb = q[:, :, start:end], k[:, :, :end], v[:, :, :end]
        z = jnp.einsum('bhtd,bhsd->bhts', qb, kb).astype(jnp.float32) * scale
        t_idx = start + jnp.arange(Q_BLOCK)[:, None]
        s_idx = jnp.arange(end)[None, :]
        mask = s_idx < t_idx
        log_1m = jnp.where(mask, jax.nn.log_sigmoid(-z), 0.0)
        after = lax.cumsum(log_1m, axis=3, reverse=True) - log_1m
        w = jnp.where(mask, jnp.exp(jax.nn.log_sigmoid(z) + after), 0.0)
        outs.append(jnp.einsum('bhts,bhsd->bhtd', w.astype(vb.dtype), vb))
    return jnp.concatenate(outs, axis=2)

def _forgetting_attention(q, k, v, cum_log_f):
    s_len = q.shape[2]
    scale = HEAD_DIM ** -0.5
    outs = []
    for start in range(0, s_len, Q_BLOCK):
        end = start + Q_BLOCK
        qb, kb, vb = q[:, :, start:end], k[:, :, :end], v[:, :, :end]
        z = jnp.einsum('bhtd,bhsd->bhts', qb, kb).astype(jnp.float32) * scale
        z = z + cum_log_f[:, :, start:end, None] - cum_log_f[:, :, None, :end]
        t_idx = start + jnp.arange(Q_BLOCK)[:, None]
        s_idx = jnp.arange(end)[None, :]
        z = jnp.where(s_idx <= t_idx, z, NEG_BIG)
        p = jax.nn.softmax(z, axis=-1)
        outs.append(jnp.einsum('bhts,bhsd->bhtd', p.astype(vb.dtype), vb))
    return jnp.concatenate(outs, axis=2)

def first_inputs(seed: int = 0) -> dict:
    key = jax.random.key(seed)
    ks = jax.random.split(key, 12)
    f32 = jnp.float32
    d = D_MODEL
    x = jax.random.normal(ks[0], (BATCH, SEQ, d), f32)
    c = jax.random.normal(ks[1], (BATCH, d), f32)
    w_ada = jax.random.normal(ks[2], (DEPTH, d, 3 * d), f32) * (0.5 * d ** -0.5)
    b_ada = 0.02 * jax.random.normal(ks[3], (DEPTH, 3 * d), f32)
    norm_g = 1.0 + 0.02 * jax.random.normal(ks[4], (DEPTH, d), f32)
    w_in = jax.random.normal(ks[5], (DEPTH, d, D_IN), f32) * d ** -0.5
    b_forget = jax.random.uniform(ks[6], (DEPTH, N_HEADS_FOX), f32, 1.0, 4.0)
    w_o_sb = jax.random.normal(ks[7], (DEPTH, D_SB, d), f32) * D_SB ** -0.5
    w_o_fox = jax.random.normal(ks[8], (DEPTH, D_FOX, d), f32) * D_FOX ** -0.5
    b_gate = 0.02 * jax.random.normal(ks[9], (DEPTH, N_BRANCH * d), f32)
    w_out = jax.random.normal(ks[10], (DEPTH, d, d), f32) * d ** -0.5
    final_g = 1.0 + 0.02 * jax.random.normal(ks[11], (d,), f32)
    return {"x": x, "c": c, "w_ada": w_ada, "b_ada": b_ada, "norm_g": norm_g,
            "w_in": w_in, "b_forget": b_forget, "w_o_sb": w_o_sb, "w_o_fox": w_o_fox,
            "b_gate": b_gate, "w_out": w_out, "final_g": final_g}

def first_block(x, c, w_ada, b_ada, norm_g, w_in, b_forget, w_o_sb, w_o_fox, b_gate, w_out, final_g):
    b, s, d = x.shape
    split_points = list(np.cumsum(IN_SIZES)[:-1])
    for l in range(DEPTH):
        mod = c @ w_ada[l] + b_ada[l]
        shift, scale, gate = jnp.split(mod, 3, axis=-1)
        h = _rmsnorm(x, norm_g[l]) * (1.0 + scale[:, None, :]) + shift[:, None, :]

        proj = h @ w_in[l]
        (q_a, k_a, v_a, z_a, q_b, k_b, v_b, z_b,
         f_logit, g_logit) = jnp.split(proj, split_points, axis=-1)

        y_a = _from_heads(_stick_breaking(_to_heads(q_a, N_HEADS_SB), _to_heads(k_a, N_HEADS_SB),
                                          _to_heads(v_a, N_HEADS_SB)))
        y_a = (y_a * jax.nn.silu(z_a)) @ w_o_sb[l]

        log_f = jax.nn.log_sigmoid((f_logit + b_forget[l]).astype(jnp.float32))
        cum_log_f = jnp.cumsum(log_f, axis=1).transpose(0, 2, 1)
        y_b = _from_heads(_forgetting_attention(_to_heads(q_b, N_HEADS_FOX), _to_heads(k_b, N_HEADS_FOX),
                                                _to_heads(v_b, N_HEADS_FOX), cum_log_f))
        y_b = (y_b * jax.nn.silu(z_b)) @ w_o_fox[l]

        gates = jax.nn.sigmoid(g_logit + b_gate[l]).reshape(b, s, N_BRANCH, d)
        merged = gates[:, :, 0, :] * y_a + gates[:, :, 1, :] * y_b
        x = x + gate[:, None, :] * (merged @ w_out[l])
    return _rmsnorm(x, final_g)


N_MEM = 256
MIX_WIDTH = D_MODEL
DA_WIDTH = MIX_WIDTH // 2
CV_WIDTH = MIX_WIDTH - DA_WIDTH
DA_HEADS = 4
DA_VDIM = DA_WIDTH // DA_HEADS
DA_QKDIM = DA_VDIM // 2
ROT_DIM = DA_QKDIM // 4
ROPE_THETA = 500000.0
CV_KERNEL = 31
X_HEADS = 4
X_HEAD_DIM = D_MODEL // X_HEADS
D_FF = 2816
FFN_KERNEL = 3

Q_COLS = DA_HEADS * 2 * DA_QKDIM
K_COLS = DA_HEADS * 2 * DA_QKDIM
V_COLS = DA_HEADS * DA_VDIM
CV_COLS = 2 * CV_WIDTH
IN_COLS = Q_COLS + K_COLS + V_COLS + CV_COLS


def rmsnorm(x, g):
    xf = x.astype(jnp.float32)
    y = xf * lax.rsqrt(jnp.mean(xf * xf, axis=-1, keepdims=True) + EPS)
    return (y * g.astype(jnp.float32)).astype(x.dtype)

def layernorm(x, g, b):
    xf = x.astype(jnp.float32)
    mu = jnp.mean(xf, axis=-1, keepdims=True)
    var = jnp.mean(jnp.square(xf - mu), axis=-1, keepdims=True)
    y = (xf - mu) * lax.rsqrt(var + EPS)
    return (y * g.astype(jnp.float32) + b.astype(jnp.float32)).astype(x.dtype)

def causal_dwconv(x, w):
    k, c = w.shape
    return lax.conv_general_dilated(
        x, w[:, None, :].astype(x.dtype), window_strides=(1,),
        padding=[(k - 1, 0)], dimension_numbers=("NWC", "WIO", "NWC"),
        feature_group_count=c)

def partial_rope(t, positions):
    half = ROT_DIM // 2
    inv_freq = ROPE_THETA ** (-jnp.arange(0, ROT_DIM, 2, dtype=jnp.float32) / ROT_DIM)
    ang = positions.astype(jnp.float32)[..., None] * inv_freq
    cos = jnp.cos(ang)[:, :, None, None, :]
    sin = jnp.sin(ang)[:, :, None, None, :]
    tf = t.astype(jnp.float32)
    t1, t2, rest = tf[..., :half], tf[..., half:ROT_DIM], tf[..., ROT_DIM:]
    out = jnp.concatenate([t1 * cos - t2 * sin, t2 * cos + t1 * sin, rest], axis=-1)
    return out.astype(t.dtype)

def diff_attention(q, k, v, lam):
    b, h, _, s, d = q.shape
    dv = v.shape[-1]
    nblk = s // Q_BLOCK
    scale = 1.0 / math.sqrt(d)
    qb = q.reshape(b, h, 2, nblk, Q_BLOCK, d).transpose(3, 0, 1, 2, 4, 5)
    kpos = jnp.arange(s)

    def one_block(args):
        q_blk, i = args
        sc = jnp.einsum("bhcqd,bhckd->bhcqk", q_blk, k).astype(jnp.float32) * scale
        qpos = i * Q_BLOCK + jnp.arange(Q_BLOCK)
        mask = kpos[None, :] <= qpos[:, None]
        sc = jnp.where(mask, sc, -jnp.inf)
        p = jax.nn.softmax(sc, axis=-1)
        a = p[:, :, 0] - lam * p[:, :, 1]
        return jnp.einsum("bhqk,bhkv->bhqv", a.astype(v.dtype), v)

    out = lax.map(one_block, (qb, jnp.arange(nblk)))
    return out.transpose(1, 0, 3, 2, 4).reshape(b, s, h, dv)

def hybrid_mixer(h, positions, layer_idx, w_in, lam_q1, lam_k1, lam_q2, lam_k2,
                 subln_g, cv_dw_w, cv_dw_b, cv_ln_g, cv_ln_b, w_out):
    b, s, _ = h.shape
    proj = jnp.einsum("bsd,dc->bsc", h, w_in)
    o1 = Q_COLS
    o2 = o1 + K_COLS
    o3 = o2 + V_COLS
    q = proj[..., :o1].reshape(b, s, DA_HEADS, 2, DA_QKDIM)
    k = proj[..., o1:o2].reshape(b, s, DA_HEADS, 2, DA_QKDIM)
    v = proj[..., o2:o3].reshape(b, s, DA_HEADS, DA_VDIM)
    u = proj[..., o3:]

    q = partial_rope(q, positions).transpose(0, 2, 3, 1, 4)
    k = partial_rope(k, positions).transpose(0, 2, 3, 1, 4)
    v = v.transpose(0, 2, 1, 3)
    lam_init = 0.8 - 0.6 * math.exp(-0.3 * layer_idx)
    lam = (jnp.exp(jnp.sum(lam_q1.astype(jnp.float32) * lam_k1.astype(jnp.float32)))
           - jnp.exp(jnp.sum(lam_q2.astype(jnp.float32) * lam_k2.astype(jnp.float32)))
           + lam_init)
    a = diff_attention(q, k, v, lam)
    a = rmsnorm(a, subln_g) * (1.0 - lam_init)
    a = a.reshape(b, s, DA_WIDTH)

    c = u[..., :CV_WIDTH] * jax.nn.sigmoid(u[..., CV_WIDTH:])
    c = causal_dwconv(c, cv_dw_w) + cv_dw_b.astype(c.dtype)
    c = jax.nn.silu(layernorm(c, cv_ln_g, cv_ln_b))

    y = jnp.concatenate([a, c], axis=-1)
    return jnp.einsum("bsc,cd->bsd", y, w_out)

def cross_attention(h, m, w_cq, w_ckv, w_co):
    b, s, _ = h.shape
    q = jnp.einsum("bsd,de->bse", h, w_cq).reshape(b, s, X_HEADS, X_HEAD_DIM)
    kv = jnp.einsum("bmd,de->bme", m, w_ckv)
    k = kv[..., :D_MODEL].reshape(b, m.shape[1], X_HEADS, X_HEAD_DIM)
    v = kv[..., D_MODEL:].reshape(b, m.shape[1], X_HEADS, X_HEAD_DIM)
    sc = jnp.einsum("bshd,bmhd->bhsm", q, k).astype(jnp.float32) / math.sqrt(X_HEAD_DIM)
    p = jax.nn.softmax(sc, axis=-1).astype(v.dtype)
    o = jnp.einsum("bhsm,bmhd->bshd", p, v).reshape(b, s, D_MODEL)
    return jnp.einsum("bse,ed->bsd", o, w_co)

def conv_ffn(h, w_up, ffn_dw_w, w_down):
    up = jnp.einsum("bsd,df->bsf", h, w_up)
    up = causal_dwconv(up, ffn_dw_w)
    z = jax.nn.silu(up[..., :D_FF]) * up[..., D_FF:]
    return jnp.einsum("bsf,fd->bsd", z, w_down)

def second_inputs(seed: int = 0) -> dict:
    key = jax.random.key(seed)
    ks = jax.random.split(key, 24)
    f32 = jnp.float32

    def nrm(k, shape, scale):
        return jax.random.normal(k, shape, f32) * scale

    def gain(k, shape):
        return 1.0 + 0.02 * jax.random.normal(k, shape, f32)

    L = DEPTH
    return {
        "x": jax.random.normal(ks[0], (BATCH, SEQ, D_MODEL), f32),
        "mem": jax.random.normal(ks[1], (BATCH, N_MEM, D_MODEL), f32),
        "positions": jnp.broadcast_to(jnp.arange(SEQ, dtype=jnp.int32), (BATCH, SEQ)),
        "norm_mix_g": gain(ks[2], (L, D_MODEL)),
        "w_in": nrm(ks[3], (L, D_MODEL, IN_COLS), D_MODEL ** -0.5),
        "lam_q1": nrm(ks[4], (L, DA_QKDIM), 0.1),
        "lam_k1": nrm(ks[5], (L, DA_QKDIM), 0.1),
        "lam_q2": nrm(ks[6], (L, DA_QKDIM), 0.1),
        "lam_k2": nrm(ks[7], (L, DA_QKDIM), 0.1),
        "subln_g": gain(ks[8], (L, DA_VDIM)),
        "cv_dw_w": nrm(ks[9], (L, CV_KERNEL, CV_WIDTH), CV_KERNEL ** -0.5),
        "cv_dw_b": nrm(ks[10], (L, CV_WIDTH), 0.02),
        "cv_ln_g": gain(ks[11], (L, CV_WIDTH)),
        "cv_ln_b": nrm(ks[12], (L, CV_WIDTH), 0.02),
        "w_out": nrm(ks[13], (L, MIX_WIDTH, D_MODEL), MIX_WIDTH ** -0.5),
        "norm_cross_g": gain(ks[14], (L, D_MODEL)),
        "norm_mem_g": gain(ks[15], (L, D_MODEL)),
        "w_cq": nrm(ks[16], (L, D_MODEL, D_MODEL), D_MODEL ** -0.5),
        "w_ckv": nrm(ks[17], (L, D_MODEL, 2 * D_MODEL), D_MODEL ** -0.5),
        "w_co": nrm(ks[18], (L, D_MODEL, D_MODEL), D_MODEL ** -0.5),
        "norm_ffn_g": gain(ks[19], (L, D_MODEL)),
        "w_up": nrm(ks[20], (L, D_MODEL, 2 * D_FF), D_MODEL ** -0.5),
        "ffn_dw_w": nrm(ks[21], (L, FFN_KERNEL, 2 * D_FF), FFN_KERNEL ** -0.5),
        "w_down": nrm(ks[22], (L, D_FF, D_MODEL), D_FF ** -0.5),
        "norm_final_g": gain(ks[23], (D_MODEL,)),
    }

def second_block(x, mem, positions, norm_mix_g, w_in, lam_q1, lam_k1, lam_q2, lam_k2,
              subln_g, cv_dw_w, cv_dw_b, cv_ln_g, cv_ln_b, w_out,
              norm_cross_g, norm_mem_g, w_cq, w_ckv, w_co,
              norm_ffn_g, w_up, ffn_dw_w, w_down, norm_final_g):
    h = x
    for l in range(DEPTH):
        h = h + hybrid_mixer(rmsnorm(h, norm_mix_g[l]), positions, l, w_in[l],
                             lam_q1[l], lam_k1[l], lam_q2[l], lam_k2[l], subln_g[l],
                             cv_dw_w[l], cv_dw_b[l], cv_ln_g[l], cv_ln_b[l], w_out[l])
        h = h + cross_attention(rmsnorm(h, norm_cross_g[l]), rmsnorm(mem, norm_mem_g[l]),
                                w_cq[l], w_ckv[l], w_co[l])
        h = h + conv_ffn(rmsnorm(h, norm_ffn_g[l]), w_up[l], ffn_dw_w[l], w_down[l])
    return rmsnorm(h, norm_final_g)


def setup_inputs(seed=0):
    out = dict(first_inputs(seed))
    for name, value in second_inputs(seed + 1).items():
        if name != "x":
            out[name + "_2"] = value
    return out


def reference(
    x, c, w_ada, b_ada, norm_g, w_in, b_forget, w_o_sb, w_o_fox, b_gate, w_out, final_g, mem_2,
    positions_2, norm_mix_g_2, w_in_2, lam_q1_2, lam_k1_2, lam_q2_2, lam_k2_2, subln_g_2,
    cv_dw_w_2, cv_dw_b_2, cv_ln_g_2, cv_ln_b_2, w_out_2, norm_cross_g_2, norm_mem_g_2, w_cq_2,
    w_ckv_2, w_co_2, norm_ffn_g_2, w_up_2, ffn_dw_w_2, w_down_2, norm_final_g_2,
):
    x = first_block(
        x, c, w_ada, b_ada, norm_g, w_in, b_forget, w_o_sb, w_o_fox, b_gate, w_out, final_g,
    )
    return second_block(
        x, mem_2, positions_2, norm_mix_g_2, w_in_2, lam_q1_2, lam_k1_2, lam_q2_2, lam_k2_2,
        subln_g_2, cv_dw_w_2, cv_dw_b_2, cv_ln_g_2, cv_ln_b_2, w_out_2, norm_cross_g_2,
        norm_mem_g_2, w_cq_2, w_ckv_2, w_co_2, norm_ffn_g_2, w_up_2, ffn_dw_w_2, w_down_2,
        norm_final_g_2,
    )


_drawn_inputs = setup_inputs


def setup_inputs(seed=0):
    import zlib

    import numpy as np

    out = dict(_drawn_inputs(seed))
    spreads = {}
    factors = {'norm_g': 5.564,
     'b_gate': 8.0,
     'norm_mix_g_2': 3.1,
     'lam_q1_2': 8.0,
     'lam_k1_2': 2.839,
     'subln_g_2': 5.929,
     'cv_dw_b_2': 3.525,
     'cv_ln_g_2': 6.006,
     'cv_ln_b_2': 6.723,
     'norm_cross_g_2': 8.0,
     'norm_mem_g_2': 8.0,
     'norm_ffn_g_2': 3.988,
     'norm_final_g_2': 2.855}
    for name, (base, spread) in spreads.items():
        noise = np.random.default_rng([zlib.crc32(name.encode()), seed]).standard_normal(out[name].shape)
        drawn = base * np.exp(spread * noise) if base else spread * noise
        out[name] = __import__('jax').numpy.asarray(drawn.astype(out[name].dtype))
    for name, factor in factors.items():
        out[name] = (out[name] * factor).astype(out[name].dtype)
    return out
```

```python
from contextlib import ExitStack

import numpy as np

import concourse.bass as bass
from concourse import mybir

F32 = mybir.dt.float32
F32R = mybir.dt.float32r
BF16 = mybir.dt.bfloat16
I32 = mybir.dt.int32
ALU = mybir.AluOpType
ACT = mybir.ActivationFunctionType
AX_X = mybir.AxisListType.X

P = 128
T = 512
D = 1024
KC = 8
M = 256
EPS = 1e-6
NEG = -1e30
LAM_INIT = 0.2
U = 1024

PARAMS = [("norm_g", 8), ("b_ada", 24), ("b_gate", 16), ("norm_mix_g_2", 8), ("norm_cross_g_2", 8),
          ("norm_mem_g_2", 8), ("norm_ffn_g_2", 8), ("norm_final_g_2", 8), ("final_g", 8), ("subln_g_2", 1),
          ("cv_dw_b_2", 4), ("cv_ln_g_2", 4), ("cv_ln_b_2", 4), ("c", 8), ("cv_dw_w_2", 124),
          ("ffn_dw_w_2", 132), ("b_forget", 1)]
POFF = {}
_o = 0
for _n, _w in PARAMS:
    POFF[_n] = _o
    _o += _w
NPAR = _o

CONSTS = ["ident", "tri8", "m8", "o1024", "o128", "o512", "rot", "triu", "one"]
NCON = len(CONSTS) * 128 + 16


def constants():
    i = np.arange(128)
    c = {
        "ident": np.eye(128),
        "tri8": np.where(i[:, None] >= i[None, :], -8.0, 0.0),
        "m8": np.full((128, 128), -8.0),
        "o1024": np.full((128, 128), 2.0 ** -10),
        "o128": np.full((128, 128), 2.0 ** -7),
        "o512": np.full((128, 128), 2.0 ** -9),
        "triu": np.where(i[:, None] <= i[None, :], 1.0, 0.0),
        "one": np.ones((128, 128)),
    }
    rot = np.zeros((128, 128))
    for g in (0, 64):
        for j in range(8):
            rot[g + 8 + j, g + j] = -1.0
            rot[g + j, g + 8 + j] = 1.0
    c["rot"] = rot
    out = np.zeros((128, NCON), np.float32)
    for n, name in enumerate(CONSTS):
        out[:, n * 128:(n + 1) * 128] = c[name]
    o = len(CONSTS) * 128
    for h in range(8):
        out[h, o + h] = 1.0
        out[32 + h, o + h] = 1.0
        out[64 + h, o + h] = 1.0
        out[96 + h, o + h] = 1.0
    inv = np.power(np.float32(500000.0), -(np.arange(0, 16, 2, dtype=np.float32) / np.float32(16)))
    for g in (0, 64):
        out[g:g + 8, o + 8] = inv
        out[g + 8:g + 16, o + 8] = inv
    out[:, o + 9] = EPS
    return out


def masks():
    k = np.arange(128) % 64
    i = np.arange(128)
    out = np.zeros((128, 1024), np.float32)
    for g in range(2):
        row = (k + 64 * g)[:, None]
        out[:, g * 128:g * 128 + 128] = row == i[None, :]
        out[:, 256 + g * 128:384 + g * 128] = np.where(row >= i[None, :], NEG, 0.0)
        out[:, 512 + g * 128:640 + g * 128] = np.where(i[None, :] > row, NEG, 0.0)
    return out


class Queue:

    def __init__(self, name):
        self.name, self.n, self.items, self.seen, self.sem = name, 0, [], {}, None

    def __call__(self, f, *waits, sig=True):
        self.wait(*waits)
        self.items.append((f, self if sig else None, 1))
        if sig:
            self.n += 1
        return (self, self.n)

    def wait(self, *waits):
        for w in waits:
            if w is None:
                continue
            if isinstance(w, list):
                self.wait(*w)
                continue
            src, n = w
            if self.seen.get(src.name, 0) < n:
                self.seen[src.name] = n
                self.items.append((None, src, n))

    def dma(self, line, f, *waits):
        self.wait(*waits)
        line.n += 16
        self.items.append((f, line, 16))
        return (line, line.n)

    def emit(self, eng):
        for f, src, n in self.items:
            if f is None:
                eng.wait_ge(src.sem, n)
            else:
                ins = f(eng)
                if src is not None:
                    ins.then_inc(src.sem, n)


class Line:

    def __init__(self, name):
        self.name, self.n, self.sem = name, 0, None


class Temps:

    def __init__(self, tiles):
        self.tiles, self.i, self.last = tiles, 0, [None] * len(tiles)

    def take(self):
        k = self.i % len(self.tiles)
        self.i += 1
        return k, self.tiles[k], self.last[k]

    def give(self, k, *tokens):
        self.last[k] = list(tokens)


def build(nc, args, order=None):
    names = []
    plan_only = order is None
    raw_n = 4
    spl_n = 4
    if not plan_only:
        units, par, con, msk, xin, memin, posin, lamin, out = args
    st = ExitStack()

    off = [16512]

    def at(name, shape, dt, offset=None):
        if plan_only:
            return None
        nb = int(np.prod(shape[1:])) * (2 if dt == BF16 else 4)
        if offset is None:
            offset = off[0]
            off[0] += (nb + 31) // 32 * 32
        assert offset + nb <= 229344, (name, offset + nb)
        return nc.alloc_sbuf_tensor_at(name, list(shape), dt, offset=offset)

    with st:
        RAW = [at(f"raw{i}", [P, U], F32) for i in range(raw_n)]
        WH = [at(f"wh{i}", [P, U], F32R) for i in range(spl_n)]
        WL = [at(f"wl{i}", [P, U], F32R) for i in range(spl_n)]
        HH = at("hh", [P, KC, T], F32R)
        HL = at("hl", [P, KC, T], F32R)
        n_tmp = 7
        TM = [at(f"tm{i}", [P, T], F32) for i in range(n_tmp)]
        con_raw = at("con_raw", [P, NCON], F32)
        conr = at("conr", [P, NCON], F32R)
        MK = at("mk", [P, 768], BF16)
        par_sb = at("par_sb", [P, NPAR], F32)
        sm = at("sm", [P, 96], F32)
        stat = at("stat", [P, 64], F32)
        SQh = [at(f"sqh{i}", [P, T], F32R) for i in range(2)]
        SQl = [at(f"sql{i}", [P, T], F32R) for i in range(2)]
        base = off[0]
        X = at("x", [P, KC, T], F32)
        a1 = off[0]
        off[0] = base
        SPh = at("sph", [P, 1280], F32R)
        SPl = at("spl", [P, 1280], F32R)
        EWh = at("ewh", [P, 1280], F32R)
        EWl = at("ewl", [P, 1280], F32R)
        PTh = at("pth", [P, 4, T], F32R, base)
        PTl = at("ptl", [P, 4, T], F32R, base + 8192)
        VAh = at("vah", [P, 4, T], F32R)
        VAl = at("val", [P, 4, T], F32R)
        VBh = at("vbh", [P, 4, T], F32R)
        VBl = at("vbl", [P, 4, T], F32R)
        YAh = at("yah", [P, 4, T], F32R)
        YAl = at("yal", [P, 4, T], F32R)
        qk0 = off[0]
        Qh = [at(f"qh{i}", [P, T], F32R) for i in range(2)]
        Ql = [at(f"ql{i}", [P, T], F32R) for i in range(2)]
        Kh = [at(f"kh{i}", [P, T], F32R) for i in range(2)]
        Kl = [at(f"kl{i}", [P, T], F32R) for i in range(2)]
        MG2h = at("mg2h", [P, 4, T], F32R, qk0)
        MG2l = at("mg2l", [P, 4, T], F32R, qk0 + 8192)
        SZ = [at(f"sz{i}", [P, T], F32) for i in range(2)]
        FT = at("ft", [104, T], F32R)
        MA = at("ma", [P, U], F32, base + 5 * 4096 - 4096)
        off[0] = a1
        RB = at("rb", [P, T], F32)
        b2 = off[0]
        CT = at("ct", [P, T], F32)
        STb = at("stb", [P, T], F32)
        CP = at("cp", [P, 4, T + 30], F32)
        AC = at("ac", [P, 4, T], F32)
        v20 = off[0]
        V2h = at("v2h", [P, 4, T], F32R)
        V2l = at("v2l", [P, 4, T], F32R)
        dq0 = off[0]
        DQh = [at(f"dqh{i}", [P, T], F32R) for i in range(2)]
        DQl = [at(f"dql{i}", [P, T], F32R) for i in range(2)]
        DKh = [at(f"dkh{i}", [P, T], F32R) for i in range(2)]
        DKl = [at(f"dkl{i}", [P, T], F32R) for i in range(2)]
        YF = at("yf", [P, 4, T], F32)
        ATh = at("ath", [P, 4, 256], F32R)
        ATl = at("atl", [P, 4, 256], F32R)
        RTh = at("rth", [P, T], F32R)
        RTl = at("rtl", [P, T], F32R)
        YDh = at("ydh", [P, 4, T], F32R, dq0)
        YDl = at("ydl", [P, 4, T], F32R, dq0 + 8192)
        YCh = at("ych", [P, 4, T], F32R, v20)
        YCl = at("ycl", [P, 4, T], F32R, v20 + 8192)
        off[0] = b2
        ymem = off[0] + 24576
        Oh = at("oh", [P, KC, T], F32R)
        Ol = at("ol", [P, KC, T], F32R)
        MTh = at("mth", [P, KC, M], F32R)
        MTl = at("mtl", [P, KC, M], F32R)
        CKh = [at(f"ckh{i}", [P, 2, M], F32R) for i in range(2)]
        CKl = [at(f"ckl{i}", [P, 2, M], F32R) for i in range(2)]
        CVh = [at(f"cvh{i}", [P, 2, M], F32R) for i in range(2)]
        CVl = [at(f"cvl{i}", [P, 2, M], F32R) for i in range(2)]
        MRB = at("mrb", [P, M], F32)
        CPh = at("cph", [P, 2, T], F32R)
        CPl = at("cpl", [P, 2, T], F32R)
        MEMT = at("memt", [P, KC, M], F32, ymem)
        off[0] = b2
        NZ = 10
        ZH = at("zh", [P, NZ, T], F32R)
        ZL = at("zl", [P, NZ, T], F32R)
        CB = [at(f"cb{i}", [P, T + 2], F32) for i in range(4)]

        if not plan_only:
            PS = [nc.alloc_psum_tensor(f"ps{i}", [P, T], F32) for i in range(8)]

        pe, act, dve, pool, sp = (Queue(n) for n in ("pe", "act", "dve", "pool", "sp"))
        l_raw = [Line(f"l_raw{i}") for i in range(raw_n)]
        l_mk0, l_mk1, l_x, l_x2, l_mem, l_con, l_par, l_pos, l_lam, l_out = (
            Line(n) for n in ("l_mk0", "l_mk1", "l_x", "l_x2", "l_mem", "l_con", "l_par", "l_pos", "l_lam", "l_out"))
        l_msk = [l_mk0, l_mk1]
        lines = l_raw + l_msk + [l_x, l_x2, l_mem, l_con, l_par, l_pos, l_lam, l_out]

        def con_f(name, w=128):
            o = CONSTS.index(name) * 128
            return con_raw[:, o:o + w]

        def con_r(name):
            o = CONSTS.index(name) * 128
            return conr[:, o:o + 128]

        CO = len(CONSTS) * 128

        def pcol(name, j=0, rows=P):
            return par_sb[0:rows, POFF[name] + j:POFF[name] + j + 1]

        def a_fn(o, i, func, *w, scale=1.0, bias=None, accum=None):
            def f(e):
                k = {} if accum is None else {"accum_out": accum()}
                k["scale"] = scale() if callable(scale) else scale
                if bias is not None:
                    k["bias"] = bias() if callable(bias) else bias
                return e.activation(o(), i(), func, **k)
            return act(f, *w)

        def tt(q, o, a, b, op, *w):
            return q(lambda e: e.tensor_tensor(o(), a(), b(), op), *w)

        def stt(o, a, s, b, op0, op1, *w):
            return dve(lambda e: e.scalar_tensor_tensor(
                o(), a(), s() if callable(s) else s, b(), op0, op1), *w)

        def ts(q, o, a, s1, s2, op0, op1, *w):
            def f(e):
                x1 = s1() if callable(s1) else s1
                x2 = s2() if callable(s2) else s2
                if op1 is None:
                    return e.tensor_scalar(o(), a(), x1, None, op0)
                return e.tensor_scalar(o(), a(), x1, x2, op0, op1)
            return q(f, *w)

        def cp(q, o, i, *w):
            return q(lambda e: e.tensor_copy(o(), i()), *w)

        def as32(f):
            return lambda: f().bitcast(F32)

        def split_ps(h, l, src, *w, scale=None):
            if scale is None:
                a = a_fn(h, src, ACT.Copy, *w)
                b = tt(dve, l, src, as32(h), ALU.subtract, a, *w)
            else:
                a = a_fn(h, src, ACT.Copy, *w, scale=scale)
                b = stt(l, src, scale, as32(h), ALU.mult, ALU.subtract, a, *w)
            return a, b

        def split_sb(h, l, src, *w, lo=None):
            a = cp(dve, h, src, *w)
            b = tt(lo or dve, l, src, as32(h), ALU.subtract, a, *w)
            return a, b

        state = {"dma": 0, "split": 0, "use": 0}
        raw_free = [None] * raw_n
        wh_ready = {}
        spl_free = {}
        raw_tok = {}

        def send(j):
            s = j % raw_n
            raw_tok[j] = sp.dma(l_raw[s], lambda e, s=s, j=j: e.dma_start(RAW[s][:, :], units[j]),
                                raw_free[s])

        slot_of = {}
        split_users = []

        def ahead():
            while state["split"] < len(order):
                j = state["split"]
                if order[j][0] == "ada":
                    break
                if len(split_users) >= spl_n and split_users[-spl_n] not in spl_free:
                    break
                if j > state["use"] + spl_n - 1:
                    break
                if j >= state["dma"]:
                    break
                s = len(split_users) % spl_n
                w = spl_free[split_users[-spl_n]] if len(split_users) >= spl_n else None
                r = j % raw_n
                a = act(lambda e, s=s, r=r: e.activation(WH[s][:, :], RAW[r][:, :], ACT.Copy), raw_tok[j], w)
                b = pool(lambda e, s=s, r=r: e.tensor_tensor(WL[s][:, :], RAW[r][:, :],
                                                             WH[s][:, :].bitcast(F32), ALU.subtract),
                         raw_tok[j], a, w)
                wh_ready[j] = (s, a, b)
                raw_free[r] = [a, b]
                split_users.append(j)
                state["split"] += 1
                if state["dma"] < len(order) and state["dma"] == j + raw_n:
                    send(state["dma"])
                    state["dma"] += 1

        def use(name):
            if plan_only:
                names.append(name)
                return 0, None, None, len(names) - 1
            j = state["use"]
            assert order[j] == name, (order[j], name)
            ahead()
            assert j in wh_ready, (j, name, state)
            s, a, b = wh_ready[j]
            state["use"] += 1
            return s, a, b, j

        def used(j, tok):
            spl_free[j] = tok
            if not plan_only:
                ahead()

        def use_raw(name):
            if plan_only:
                names.append(name)
                return 0, None, 0
            j = state["use"]
            assert order[j] == name, (order[j], name)
            state["use"] += 1
            return j % raw_n, raw_tok[j], j

        def used_raw(j, tok):
            if plan_only:
                return
            raw_free[j % raw_n] = [tok]
            assert state["dma"] == j + raw_n or state["dma"] == len(order)
            if state["dma"] < len(order):
                send(state["dma"])
                state["dma"] += 1
            assert state["split"] == j
            state["split"] = j + 1
            ahead()

        def mm(o, l, r, start, stop, *w, sig=False, skip=False):
            return pe(lambda e: e.matmul(o(), l(), r(), start=start, stop=stop, skip_group_check=skip),
                      *w, sig=sig)

        def mm3(o, lh, ll, rh, rl, first, last, wh=(), wl=(), sig=False):
            mm(o, lh, rh, first, False, *wh)
            mm(o, lh, rl, False, False, *wl)
            return mm(o, ll, rh, False, last, sig=sig)

        bank = [None] * 8

        class Chunk:

            def __init__(self, name, b, rh, rl, n=T, nk=KC, rtok=None, first=True, last=True):
                self.a = (name, b, rh, rl, n, nk, rtok, first, last)

            def half(self, part):
                name, b, rh, rl, n, nk, rtok, first, last = self.a
                if part == 0:
                    self.u = use(name)
                    s, ta, tb, j = self.u
                    pe.wait(bank[b])
                s, ta, tb, j = self.u
                ks = range(nk // 2) if part == 0 else range(nk // 2, nk)
                tok = None
                for k in ks:
                    lh = lambda k=k, s=s: WH[s][:, k * 128:(k + 1) * 128]
                    ll = lambda k=k, s=s: WL[s][:, k * 128:(k + 1) * 128]
                    rt = rtok(k) if rtok else (None, None)
                    o = lambda b=b, n=n: PS[b][:, 0:n]
                    mm(o, lh, lambda k=k: rh(k), first and k == 0, False, ta, rt[0])
                    mm(o, lh, lambda k=k: rl(k), False, False, rt[1])
                    tok = mm(o, ll, lambda k=k: rh(k), False, last and k == nk - 1, tb, sig=k == nk - 1)
                if part == 1:
                    used(j, tok)
                    self.tok = tok
                return tok

            def both(self):
                self.half(0)
                return self.half(1)

        h_r = (lambda k: HH[:, k, :], lambda k: HL[:, k, :])
        h_tok = [(None, None)] * KC
        h_read = [None]

        def hproj(name, b, **kw):
            return Chunk(name, b, *h_r, rtok=lambda k: h_tok[k], **kw)

        if not plan_only:
            t_con = sp.dma(l_con, lambda e: e.dma_start(con_raw[:, :], con))
            t_par = sp.dma(l_par, lambda e: e.dma_start(par_sb[:, :], par))
            t_x = sp.dma(l_x, lambda e: e.dma_start(X[:, :, :], xin))
            for j in range(raw_n):
                send(j)
            state["dma"] = raw_n
        else:
            t_con = t_par = t_x = None
        t_conr = cp(dve, lambda: conr[:, :], lambda: con_raw[:, :], t_con)
        tmps = Temps(TM)
        t_mk = []
        for g, w in ((0, 512), (1, 256)):
            i, t, _ = tmps.take()
            tm = None
            if not plan_only:
                tm = sp.dma(l_msk[g], lambda e, t=t, g=g: e.dma_start(t[:, :], msk[:, 512 * g:512 * g + 512]))
            t_mk.append(cp(dve, lambda g=g, w=w: MK[:, 512 * g:512 * g + w], lambda t=t, w=w: t[:, 0:w], tm))
            tmps.give(i, t_mk[-1])

        def mask(b, c0, r, which):
            o = lambda: PS[b][:, c0:c0 + 128]
            m0 = 256 if which == "s" else 512
            mm(o, lambda: MK[r:r + 64, 0:128], lambda: MK[r:r + 64, m0:m0 + 128], False, False, *t_mk)
            return mm(o, lambda: MK[r:r + 64, 128:256], lambda: MK[r:r + 64, m0 + 128:m0 + 256], False, True,
                      sig=True)

        def eps():
            return con_raw[:, CO + 9:CO + 10]

        sq_n = [0]
        sq_free = [None, None]

        def square(src, *w, n=T, scale=1.0):
            i, t, lw = tmps.take()
            p = sq_n[0] % 2
            sq_n[0] += 1
            a = a_fn(lambda: t[:, 0:n], src, ACT.Square, lw, *w, scale=scale)
            h = cp(dve, lambda: SQh[p][:, 0:n], lambda: t[:, 0:n], a, sq_free[p])
            l = tt(dve, lambda: SQl[p][:, 0:n], lambda: t[:, 0:n], lambda: SQh[p][:, 0:n].bitcast(F32),
                   ALU.subtract, h, sq_free[p])
            tmps.give(i, l)

            def add(b, ones, first, last, o=0):
                out_ = lambda: PS[b][:, o:o + n]
                mm(out_, lambda: con_r(ones), lambda: SQh[p][:, 0:n], first, False, h, t_conr,
                   bank[b] if first else None)
                tok = mm(out_, lambda: con_r(ones), lambda: SQl[p][:, 0:n], False, last, l, sig=True)
                sq_free[p] = tok
                return tok

            return a, add

        def root(dst, b, *w, n=T):
            i, t, lw = tmps.take()
            a = a_fn(lambda: t[:, 0:n], lambda: PS[b][:, 0:n], ACT.Sqrt, lw, *w, bias=eps)
            r = dve(lambda e: e.reciprocal(dst(), t[:, 0:n]), a, (dve, dve.n))
            tmps.give(i, r)
            return a, r

        def modulation(part, t0):
            tok = None
            for k in range(KC):
                r, tr, j = use_raw(("ada", part, k))
                if k == 0:
                    tok = ts(dve, lambda: MA[:, :], lambda r=r: RAW[r][:, :], lambda k=k: pcol("c", k), None,
                             ALU.mult, None, tr, t_par, t0)
                else:
                    tok = stt(lambda: MA[:, :], lambda r=r: RAW[r][:, :], lambda k=k: pcol("c", k),
                              lambda: MA[:, :], ALU.mult, ALU.add, tr, tok)
                used_raw(j, tok)
            for f in range(8):
                m = mm(lambda f=f: PS[0][:, f:f + 1], lambda f=f: MA[:, f * 128:(f + 1) * 128],
                       lambda: con_f("one", 1), True, True, tok, t_con, bank[0], sig=True)
            a = tt(dve, lambda: sm[:, part * 8:part * 8 + 8], lambda: PS[0][:, 0:8],
                   lambda: par_sb[:, POFF["b_ada"] + part * 8:POFF["b_ada"] + part * 8 + 8], ALU.add, m)
            bank[0] = [a]
            return a, m

        if not plan_only:
            pass
        t_root = None
        pend = None
        for k in range(KC):
            _, add = square(lambda k=k: X[:, k, :], t_x)
            st_tok = add(7, "o1024", k == 0, k == KC - 1)
        RB1 = lambda: SZ[1][:, :]
        a, t_rb = root(RB1, 7, st_tok)
        bank[7] = [a]
        t_sh, m1 = modulation(0, None)
        t_sc, m2 = modulation(1, m1)
        t_g1 = ts(dve, lambda: sm[:, 8:16], lambda: sm[:, 8:16], 1.0, None, ALU.add, None, t_sc)
        t_gs = tt(dve, lambda: sm[:, 8:16], lambda: sm[:, 8:16],
                  lambda: par_sb[:, POFF["norm_g"]:POFF["norm_g"] + 8], ALU.mult, t_g1, t_par)
        for k in range(KC):
            i, t, lw = tmps.take()
            a = stt(lambda t=t: t[:, :], lambda k=k: X[:, k, :], lambda k=k: sm[:, 8 + k:9 + k], RB1,
                    ALU.mult, ALU.mult, lw, t_gs, t_rb)
            b = ts(dve, lambda t=t: t[:, :], lambda t=t: t[:, :], lambda k=k: sm[:, k:k + 1], None,
                   ALU.add, None, a, t_sh)
            hi, lo = split_sb(lambda k=k: HH[:, k, :], lambda k=k: HL[:, k, :], lambda t=t: t[:, :], b)
            tmps.give(i, lo)
            h_tok[k] = (hi, lo)
        x_read = h_tok[KC - 1][1]

        def vproj(name, dh, dl, wfree, scale=None, stok=None):
            toks = []
            for u in range(4):
                s, ta, tb, j = use((name, u))
                for t in range(4):
                    if u == 0:
                        pe.wait(bank[2 + t])
                    for kk in range(2):
                        k = 2 * u + kk
                        o = lambda t=t: PS[2 + t][:, :]
                        wh = lambda s=s, kk=kk: WH[s][:, kk * T:(kk + 1) * T]
                        wl = lambda s=s, kk=kk: WL[s][:, kk * T:(kk + 1) * T]
                        hh = lambda k=k, t=t: HH[:, k, t * 128:(t + 1) * 128]
                        hl = lambda k=k, t=t: HL[:, k, t * 128:(t + 1) * 128]
                        mm(o, hh, wh, k == 0, False, ta, h_tok[k][0])
                        mm(o, hh, wl, False, False, tb)
                        tok = mm(o, hl, wh, False, k == KC - 1, h_tok[k][1], sig=kk == 1)
                    if u == 3:
                        a, b = split_ps(lambda t=t: dh[:, t, :], lambda t=t: dl[:, t, :],
                                        lambda t=t: PS[2 + t][:, :], tok, wfree, stok,
                                        scale=None if scale is None else scale(t))
                        bank[2 + t] = [a, b]
                        toks.append((a, b))
                used(j, tok)
            return toks

        q_tok, k_tok, z_tok = {}, {}, {}
        q_free, z_free = [None, None], [x_read, x_read]
        zf = {}

        def q_steps(br, c):
            p = c % 2
            qc = Chunk((br + "q", c), 0, *h_r, rtok=lambda k: h_tok[k])
            kc = Chunk((br + "k", c), 1, *h_r, rtok=lambda k: h_tok[k])
            zc = Chunk((br + "z", c), 0, *h_r, rtok=lambda k: h_tok[k])

            def fin_q():
                m = qc.half(1)
                q_tok[c] = split_ps(lambda: Qh[p][:, :], lambda: Ql[p][:, :], lambda: PS[0][:, :], m, q_free[p])
                bank[0] = list(q_tok[c])

            def fin_k():
                m = kc.half(1)
                k_tok[c] = split_ps(lambda: Kh[p][:, :], lambda: Kl[p][:, :], lambda: PS[1][:, :], m, q_free[p])
                bank[1] = list(k_tok[c])

            def fin_z():
                m = zc.half(1)
                z_tok[c] = a_fn(lambda: SZ[p][:, :], lambda: PS[0][:, :], ACT.Silu, m, z_free[p])
                bank[0] = [z_tok[c]]

            return [lambda: qc.half(0), fin_q, lambda: kc.half(0), fin_k, lambda: zc.half(0), fin_z]

        OFF = [0, 512, 896, 1152]

        def run(steps, n):
            for _ in range(n):
                if steps:
                    steps.pop(0)()

        y_part = {}

        def gate_y(h, m, dh, dl, wfree):
            c, r = h // 2, 64 * (h % 2)
            z = lambda: SZ[c % 2][r:r + 64, :]
            b = 6 + h % 2
            a = tt(dve, z, lambda: PS[b][r:r + 64, :], z, ALU.mult, m, z_tok[c])
            bank[b] = [a]
            if h % 2 == 0:
                y_part["a"] = a
                return None
            hi, lo = split_sb(lambda: dh[:, c, :], lambda: dl[:, c, :], lambda: SZ[c % 2][:, :], a, y_part["a"],
                              wfree)
            z_free[c % 2] = lo
            return hi, lo

        va = vproj("av", VAh, VAl, None)
        for f in q_steps("a", 0):
            f()
        ew_free = [None]
        sp_free = [x_read]
        sp_tok, ew_tok = {}, {}

        def qk_a(h):
            c, r, p = h // 2, 64 * (h % 2), (h // 2) % 2
            for i in (3, 2, 1, 0):
                b, n = 2 + i, T - 128 * i
                o = lambda b=b, n=n: PS[b][:, 0:n]
                lh = lambda i=i: Kh[p][r:r + 64, i * 128:(i + 1) * 128]
                ll = lambda i=i: Kl[p][r:r + 64, i * 128:(i + 1) * 128]
                rh = lambda i=i: Qh[p][r:r + 64, i * 128:T]
                rl = lambda i=i: Ql[p][r:r + 64, i * 128:T]
                mm3(o, lh, ll, rh, rl, True, False, wh=[k_tok[c], q_tok[c], bank[b]] and
                    [list(k_tok[c]), list(q_tok[c]), bank[b]])
                m = mask(b, 0, r, "s")
                o2 = OFF[i]
                k1, t1, w1 = tmps.take()
                k2, t2, w2 = tmps.take()
                s1 = lambda t1=t1, n=n: t1[:, 0:n]
                s2 = lambda t2=t2, n=n: t2[:, 0:n]
                x4 = ts(dve, s2, o, 0.125, 0.0, ALU.mult, ALU.max, m, w2)
                x1 = stt(s1, s2, -16.0, o, ALU.mult, ALU.add, x4, w1)
                x2 = a_fn(s1, s1, ACT.Exp, x1, scale=0.125)
                x3 = a_fn(s1, s1, ACT.Ln, x2, bias=1.0)
                x5 = tt(dve, s2, s2, s1, ALU.add, x3, x4)
                hi, lo = split_sb(lambda o2=o2, n=n: SPh[:, o2:o2 + n], lambda o2=o2, n=n: SPl[:, o2:o2 + n],
                                  s2, x5, sp_free[0])
                tmps.give(k1, x5)
                tmps.give(k2, lo)
                sp_tok[i] = (hi, lo)
                bank[b] = [x1, x4]
            q_free[p] = m

        def mid_a(h):
            for i in (3, 2, 1, 0):
                b, n = 2 + i, T - 128 * i
                for j in range(3, i - 1, -1):
                    nj = T - 128 * j
                    o = lambda b=b, i=i, j=j, n=n: PS[b][:, 128 * (j - i):n]
                    w = lambda i=i, j=j: con_r("tri8" if i == j else "m8")
                    mm(o, w, lambda j=j, nj=nj: SPh[:, OFF[j]:OFF[j] + nj], False, False, sp_tok[j][0], bank[b],
                       t_conr, skip=True)
                    m = mm(o, w, lambda j=j, nj=nj: SPl[:, OFF[j]:OFF[j] + nj], False, j == i, sp_tok[j][1],
                           skip=True, sig=j == i)
                k1, t1, w1 = tmps.take()
                s1 = lambda t1=t1, n=n: t1[:, 0:n]
                x = a_fn(s1, lambda b=b, n=n: PS[b][:, 0:n], ACT.Exp, m, w1, scale=0.125)
                hi, lo = split_sb(lambda i=i, n=n: EWh[:, OFF[i]:OFF[i] + n],
                                  lambda i=i, n=n: EWl[:, OFF[i]:OFF[i] + n], s1, x, ew_free[0])
                tmps.give(k1, lo)
                ew_tok[i] = (hi, lo)
                bank[b] = [x]
            sp_free[0] = m

        def pv_a(h):
            c = h // 2
            b = 6 + h % 2
            for j in range(4):
                nj = T - 128 * j
                o = lambda j=j: PS[b][:, 128 * j:T]
                lh = lambda j=j: VAh[:, j, c * 128:(c + 1) * 128]
                ll = lambda j=j: VAl[:, j, c * 128:(c + 1) * 128]
                rh = lambda j=j, nj=nj: EWh[:, OFF[j]:OFF[j] + nj]
                rl = lambda j=j, nj=nj: EWl[:, OFF[j]:OFF[j] + nj]
                m = mm3(o, lh, ll, rh, rl, j == 0, j == 3, wh=[ew_tok[j][0], va[j][0], va[j][1], bank[b]],
                        wl=[ew_tok[j][1]], sig=j == 3)
            ew_free[0] = m
            return m

        ya_tok = {}
        qk_a(0)
        steps = []
        f_tok = {}

        def f_steps():
            fc = Chunk(("f", 0), 1, *h_r, rtok=lambda k: h_tok[k])

            def fin():
                m = fc.half(1)
                k1, t1, w1 = tmps.take()
                k2, t2, w2 = tmps.take()
                s1 = lambda: t1[0:8, :]
                s2 = lambda: t2[0:8, :]
                x0 = ts(dve, s2, lambda: PS[1][0:8, :], lambda: pcol("b_forget", 0, 8), None, ALU.add, None,
                        m, w2, t_par)
                bank[1] = [x0]
                x1 = a_fn(s1, s2, ACT.Abs, x0, w1)
                x2 = a_fn(s1, s1, ACT.Exp, x1, scale=-1.0)
                x3 = a_fn(s1, s1, ACT.Ln, x2, bias=1.0)
                x4 = ts(dve, s2, s2, 0.0, None, ALU.min, None, x1)
                x5 = tt(dve, s2, s2, s1, ALU.subtract, x3, x4)
                for n in range(4):
                    m = pe(lambda e, n=n: e.transpose(PS[1][:, 8 * n:8 * n + 8], t2[0:8, 128 * n:128 * n + 128],
                                                      con_raw[0:8, 0:8]), x5, bank[1], t_con)
                x6 = cp(dve, lambda: t1[:, 0:32], lambda: PS[1][:, 0:32], m, x5)
                bank[1] = [x6]
                for n in range(4):
                    for b in range(n + 1):
                        m = mm(lambda n=n: PS[1][0:8, 128 * n:128 * n + 128], lambda b=b: t1[:, 8 * b:8 * b + 8],
                               lambda b=b, n=n: con_f("triu" if b == n else "one"), b == 0, b == n, x6, sig=True)
                x7 = ts(dve, s2, lambda: PS[1][0:8, :], -8.0, None, ALU.mult, None, m)
                x8 = cp(dve, lambda: FT[0:8, :], s2, x7, t_fz)
                x9 = tt(dve, s1, s2, lambda: FT[0:8, :].bitcast(F32), ALU.subtract, x8, m)
                x10 = cp(dve, lambda: FT[32:40, :], s1, x9)
                cp(dve, lambda: FT[64:72, :], lambda: FT[0:8, :].bitcast(F32), x8)
                x10 = cp(dve, lambda: FT[96:104, :], lambda: FT[32:40, :].bitcast(F32), x10)
                tmps.give(k1, x10)
                tmps.give(k2, x9)
                bank[1] = [x7]
                f_tok[0] = x10

            return [lambda: fc.half(0), fin]

        t_fz = pool(lambda e: e.memset(FT[:, :].bitcast(F32), 0.0))
        for h in range(8):
            c = h // 2
            if h % 2 == 0:
                steps += q_steps("a", c + 1) if c < 3 else (q_steps("b", 0)[0:4] + f_steps())
            mid_a(h)
            run(steps, 1)
            if h < 7:
                if h % 2 == 1:
                    run(steps, max(0, len(steps) - 2))
                qk_a(h + 1)
            m = pv_a(h)
            t = gate_y(h, m, YAh, YAl, None)
            if t:
                ya_tok[c] = t
            run(steps, 2 if h % 2 == 0 else 9)

        pv_done = m
        vb = vproj("bv", VBh, VBl, None)
        for f in q_steps("b", 0)[4:]:
            f()
        pt_free = [pv_done]

        def softmax_tile(b, n, scale, t, w, tw):
            k = softmax_tile.n % 8
            softmax_tile.n += 1
            cm, cb, cs, cr = (4 * k + x for x in range(4))
            col = lambda x: (lambda: stat[:, x:x + 1])
            x1 = dve(lambda e: e.tensor_reduce(col(cm)(), PS[b][:, 0:n], AX_X, ALU.max, negate=True), w, tw)
            x2 = ts(dve, col(cb), col(cm), scale, None, ALU.mult, None, x1)
            x3 = a_fn(lambda: t[:, 0:n], lambda: PS[b][:, 0:n], ACT.Exp, x2, tw, scale=scale, bias=col(cb),
                      accum=col(cs))
            x4 = dve(lambda e: e.reciprocal(col(cr)(), col(cs)()), x3)
            return x3, x4, col(cr)
        softmax_tile.n = 0

        pt_tok, pt2 = {}, {}

        def turn(b, nj, t, dh, dl, ready, wfree):
            for j in range(nj):
                m = pe(lambda e, j=j: e.transpose(PS[b][:, 128 * j:128 * j + 128], t[:, 128 * j:128 * j + 128],
                                                  con_f("ident")), ready, t_con)
            src = lambda: PS[b][:, 0:128 * nj].rearrange("p (j t) -> p j t", j=nj)
            a, l = split_ps(dh, dl, src, m, wfree)
            bank[b] = [a, l]
            return m, a, l

        def sel(h):
            r = 64 * (h % 2)
            return conr[r:r + 40, CO + h:CO + h + 1].to_broadcast([40, 128])

        def qk_b(h):
            c, r, p = h // 2, 64 * (h % 2), (h // 2) % 2
            for i in range(4):
                b, n = 2 + i, 128 * (i + 1)
                o = lambda b=b, n=n: PS[b][:, 0:n]
                lh = lambda i=i: Qh[p][r:r + 64, i * 128:(i + 1) * 128]
                ll = lambda i=i: Ql[p][r:r + 64, i * 128:(i + 1) * 128]
                mm3(o, lh, ll, lambda n=n: Kh[p][r:r + 64, 0:n], lambda n=n: Kl[p][r:r + 64, 0:n], True, False,
                    wh=[list(k_tok[c]), list(q_tok[c]), bank[b]])
                mm(o, lambda: sel(h), lambda n=n: FT[r:r + 40, 0:n], False, False, f_tok[0], t_conr)
                m = mask(b, 128 * i, r, "f")
                k1, t1, w1 = tmps.take()
                x3, x4, rc = softmax_tile(b, n, 0.125, t1, m, w1)
                x5 = ts(dve, lambda t1=t1, n=n: t1[:, 0:n], lambda t1=t1, n=n: t1[:, 0:n], rc, None, ALU.mult,
                        None, x4)
                pt_tok[i] = (k1, t1, x3, x5)
            q_free[p] = m

        def mid_b(h):
            for i in range(4):
                k1, t1, x3, x5 = pt_tok[i]
                m, a, l = turn(2 + i, i + 1, t1, lambda i=i: PTh[:, 0:i + 1, 128 * i:128 * i + 128],
                               lambda i=i: PTl[:, 0:i + 1, 128 * i:128 * i + 128], [x5, x3], pt_free[0])
                tmps.give(k1, m)
                pt2[i] = (a, l)

        def pv_b(h):
            c = h // 2
            b = 6 + h % 2
            for j in range(4):
                o = lambda j=j: PS[b][:, 128 * j:T]
                lh = lambda j=j: VBh[:, j, c * 128:(c + 1) * 128]
                ll = lambda j=j: VBl[:, j, c * 128:(c + 1) * 128]
                w = [[list(pt2[i]) for i in range(4)], list(vb[j]), bank[b]]
                m = mm3(o, lh, ll, lambda j=j: PTh[:, j, 128 * j:T], lambda j=j: PTl[:, j, 128 * j:T],
                        j == 0, j == 3, wh=w, sig=j == 3)
            pt_free[0] = m
            return m

        yb_tok = {}
        qk_b(0)
        steps = []
        for h in range(8):
            c = h // 2
            if h % 2 == 0:
                steps += q_steps("b", c + 1) if c < 3 else []
            mid_b(h)
            run(steps, 1)
            if h < 7:
                if h % 2 == 1:
                    run(steps, max(0, len(steps) - 2))
                qk_b(h + 1)
            m = pv_b(h)
            t = gate_y(h, m, VAh, VAl, pv_done)
            if t:
                yb_tok[c] = t
            run(steps, 2 if h % 2 == 0 else 9)
        pv_done = m

        t_xr = None
        if not plan_only:
            t_xr = sp.dma(l_x2, lambda e: e.dma_start(X[:, :, :], xin), pv_done)

        def half_unit(name, b0, rh, rl, rtok, n=T):
            s, ta, tb, j = use(name)
            toks = []
            for g in range(2):
                pe.wait(bank[b0 + g])
                for k in range(4):
                    lh = lambda k=k, g=g, s=s: WH[s][:, k * 256 + g * 128:k * 256 + g * 128 + 128]
                    ll = lambda k=k, g=g, s=s: WL[s][:, k * 256 + g * 128:k * 256 + g * 128 + 128]
                    o = lambda g=g: PS[b0 + g][:, :]
                    tok = mm3(o, lh, ll, lambda k=k: rh(k), lambda k=k: rl(k), k == 0, k == 3,
                              wh=[ta, rtok(k)[0]], wl=[tb, rtok(k)[1]], sig=k == 3)
                toks.append(tok)
            used(j, tok)
            return toks

        mg_tok = {}

        def mgh(k):
            return VBh[:, k, :] if k < 4 else MG2h[:, k - 4, :]

        def mgl(k):
            return VBl[:, k, :] if k < 4 else MG2l[:, k - 4, :]

        for u in range(4):
            ta = half_unit(("oa", u), 0, lambda k: YAh[:, k, :], lambda k: YAl[:, k, :], lambda k: ya_tok[k])
            tb = half_unit(("ob", u), 2, lambda k: VAh[:, k, :], lambda k: VAl[:, k, :], lambda k: yb_tok[k])
            for g in range(2):
                f = 2 * u + g
                ms = []
                for x in range(2):
                    b = 4 + 2 * g + x
                    tok = hproj(("g", 8 * x + f), b).both()
                    h_read[0] = tok
                    k1, t1, w1 = tmps.take()
                    sg = a_fn(lambda t1=t1: t1[:, :], lambda b=b: PS[b][:, :], ACT.Sigmoid, tok, w1, t_par,
                              bias=lambda x=x, f=f: pcol("b_gate", 8 * x + f))
                    bank[b] = [sg]
                    yb_, ty = (g, ta[g]) if x == 0 else (2 + g, tb[g])
                    pr = tt(dve, lambda t1=t1: t1[:, :], lambda t1=t1: t1[:, :], lambda yb_=yb_: PS[yb_][:, :],
                            ALU.mult, sg, ty)
                    bank[yb_] = [pr]
                    ms.append((k1, t1, pr))
                (k1, t1, p1), (k2, t2, p2) = ms
                s_ = tt(dve, lambda t1=t1: t1[:, :], lambda t1=t1: t1[:, :], lambda t2=t2: t2[:, :], ALU.add,
                        p1, p2)
                hi, lo = split_sb(lambda f=f: mgh(f), lambda f=f: mgl(f), lambda t1=t1: t1[:, :], s_, pv_done,
                                  lo=pool)
                tmps.give(k1, hi, lo)
                tmps.give(k2, s_)
                mg_tok[f] = (hi, lo)
        t_gate, _ = modulation(2, pv_done)

        x_rd = [None] * KC
        x_tok = [None] * KC

        def residual(f, b, tok, gname, gate=None, wx=None, both=False):
            if gate is None:
                x = tt(dve, lambda: X[:, f, :], lambda: PS[b][:, :], lambda: X[:, f, :], ALU.add, tok, wx,
                       x_rd[f])
            else:
                x = stt(lambda: X[:, f, :], lambda: PS[b][:, :], gate, lambda: X[:, f, :], ALU.mult, ALU.add,
                        tok, wx)
            bank[b] = [x]
            if gname:
                g = (lambda: sm[:, 40 + f:41 + f]) if both else (lambda: pcol(gname, f))
                hi = a_fn(lambda: HH[:, f, :], lambda: X[:, f, :], ACT.Copy, x, h_read[0], scale=g)
                lo = stt(lambda: HL[:, f, :], lambda: X[:, f, :], g, lambda: HH[:, f, :].bitcast(F32),
                         ALU.mult, ALU.subtract, hi)
                h_tok[f] = (hi, lo)
            sq, add = square(lambda: X[:, f, :], x)
            x_rd[f] = [sq, hi] if gname else [sq]
            x_tok[f] = x
            if both:
                sq2, add2 = square(lambda: X[:, f, :], x, scale=lambda: pcol("final_g", f))
                x_rd[f].append(sq2)

                def adds(b_, ones, first, last):
                    add(b_, ones, first, last)
                    return add2(6, ones, first, last)
                return adds
            return add

        def out_proj(name, rh, rl, rtok, gname, gate=None, wx=None, both=False):
            add = None
            for f in range(KC):
                b = f % 2
                tok = Chunk((name, f), b, rh, rl, rtok=rtok).both()
                if add:
                    add(7, "o1024", f == 1, False)
                add = residual(f, b, tok, gname, gate=(lambda f=f: gate(f)) if gate else None, wx=wx,
                               both=both)
            return add(7, "o1024", False, True)

        mg_read = (pe, pe.n)
        kp, tp, wp = tmps.take()
        ka, tag, wa = tmps.take()
        kk_, tk, wk = tmps.take()
        kl, tl, wl_ = tmps.take()
        if plan_only:
            t_pos = t_lam = None
        else:
            t_pos = sp.dma(l_pos, lambda e: e.dma_start(tp[:, :].bitcast(I32), posin), wp)
            t_lam = sp.dma(l_lam, lambda e: e.dma_start(tl[:, 0:256], lamin), wl_)
        C1 = 6.28125
        C2 = float(np.float32(np.round((2 * np.pi - C1) * 2 ** 20) / 2 ** 20))
        C3 = float(2 * np.pi - C1 - C2)
        MAGIC = 12582912.0
        ang, kr, pv_ = lambda: tag[:, :], lambda: tk[:, :], lambda: tp[:, :]
        x0 = cp(dve, ang, lambda: tp[:, :].bitcast(I32), t_pos, wa)
        x1 = ts(dve, ang, ang, lambda: con_raw[:, CO + 8:CO + 9], None, ALU.mult, None, x0, t_con)
        x2 = ts(dve, kr, ang, float(1 / (2 * np.pi)), MAGIC, ALU.mult, ALU.add, x1, wk)
        x3 = ts(dve, kr, kr, MAGIC, None, ALU.subtract, None, x2)
        x4 = stt(ang, kr, -C1, ang, ALU.mult, ALU.add, x3)
        x5 = stt(ang, kr, -C2, ang, ALU.mult, ALU.add, x4)
        x6 = stt(ang, kr, -C3, ang, ALU.mult, ALU.add, x5)
        x7 = ts(dve, ang, ang, -3.1415925, 3.1415925, ALU.max, ALU.min, x6)
        x8 = a_fn(lambda: STb[:, :], ang, ACT.Sin, x7, mg_read)
        x9 = a_fn(kr, ang, ACT.Abs, x7)
        x10 = ts(dve, kr, kr, -1.0, float(np.pi / 2), ALU.mult, ALU.add, x9)
        x11 = a_fn(lambda: CT[:, :], kr, ACT.Sin, x10, mg_read)
        tmps.give(kp, x0)
        tmps.give(ka, x8, x9)
        tmps.give(kk_, x11)
        x0 = tt(dve, lambda: tl[:, 256:320], lambda: tl[:, 0:64], lambda: tl[:, 64:128], ALU.mult, t_lam)
        x1 = tt(dve, lambda: tl[:, 320:384], lambda: tl[:, 128:192], lambda: tl[:, 192:256], ALU.mult, t_lam)
        x2 = dve(lambda e: e.tensor_reduce(sm[:, 26:28], tl[:, 256:384].rearrange("p (a b) -> p a b", a=2), AX_X,
                                           ALU.add), x0, x1)
        x3 = a_fn(lambda: sm[:, 28:30], lambda: sm[:, 26:28], ACT.Exp, x2)
        x4 = tt(dve, lambda: sm[:, 30:31], lambda: sm[:, 29:30], lambda: sm[:, 28:29], ALU.subtract, x3)
        t_nl = ts(dve, lambda: sm[:, 24:25], lambda: sm[:, 30:31], -LAM_INIT, None, ALU.add, None, x4)
        t_sg = ts(dve, lambda: sm[:, 25:26], lambda: pcol("subln_g_2"), 1.0 - LAM_INIT, None, ALU.mult, None, t_par)
        tmps.give(kl, x2)

        t_fm = tt(dve, lambda: sm[:, 40:48], lambda: par_sb[:, POFF["final_g"]:POFF["final_g"] + 8],
                  lambda: par_sb[:, POFF["norm_mix_g_2"]:POFF["norm_mix_g_2"] + 8], ALU.mult, t_par)
        st_tok = out_proj("wo", mgh, mgl, lambda k: mg_tok[k], "norm_mix_g_2",
                          gate=lambda f: sm[:, 16 + f:17 + f], wx=[t_xr, t_gate, t_fm], both=True)
        rb = lambda: RB[:, :]
        r1 = lambda: YF[:, 0, :]
        a, t_r1 = root(r1, 7, st_tok)
        k1, t1, w1 = tmps.take()
        s1 = lambda t1=t1: t1[:, :]
        x1 = tt(dve, s1, r1, r1, ALU.mult, t_r1, w1)
        x2 = tt(dve, s1, s1, lambda: PS[6][:, :], ALU.mult, x1, st_tok)
        x3 = a_fn(s1, s1, ACT.Sqrt, x2, bias=eps)
        x4 = dve(lambda e, s1=s1: e.reciprocal(s1(), s1()), x3)
        t_rb = tt(dve, rb, s1, r1, ALU.mult, x4, st_tok)
        tmps.give(k1, t_rb)
        bank[6] = [x2]
        for f in range(KC):
            xf = lambda f=f: X[:, f, :]
            x_new = stt(xf, xf, lambda f=f: pcol("final_g", f), r1, ALU.mult, ALU.mult, t_r1, x_rd[f])
        bank[7] = [a]
        free1 = st_tok

        for t in range(4):
            m = mm(lambda t=t: PS[7][:, t:t + 1], lambda t=t: RB[0:1, t * 128:(t + 1) * 128],
                   lambda: con_f("one", 1)[0:1, :], True, True, t_rb, bank[7], sig=True)
        t_rc = cp(dve, lambda: sm[:, 32:36], lambda: PS[7][:, 0:4], m)
        bank[7] = [t_rc]
        t_c2 = tt(dve, lambda: CT[:, :], lambda: CT[:, :], rb, ALU.mult, x11, t_rb)
        t_s2 = tt(dve, lambda: STb[:, :], lambda: STb[:, :], rb, ALU.mult, x8, t_rb)
        t_pad = pool(lambda e: e.memset(CP[:, :, 0:30], 0.0), free1)
        cp_tok = {}
        for j in range(4):
            ua = hproj(("u", j), 0).both()
            k1, t1, w1 = tmps.take()
            xa = tt(dve, lambda t1=t1: t1[:, :], lambda: PS[0][:, :], rb, ALU.mult, ua, w1, t_rb)
            bank[0] = [xa]
            ub = hproj(("u", 4 + j), 1).both()
            k2, t2, w2 = tmps.take()
            xb = tt(dve, lambda t2=t2: t2[:, :], lambda: PS[1][:, :], rb, ALU.mult, ub, w2, t_rb)
            bank[1] = [xb]
            xc = a_fn(lambda t2=t2: t2[:, :], lambda t2=t2: t2[:, :], ACT.Sigmoid, xb)
            xd = tt(dve, lambda j=j: CP[:, j, 30:30 + T], lambda t1=t1: t1[:, :], lambda t2=t2: t2[:, :],
                    ALU.mult, xa, xc, free1)
            tmps.give(k1, xd)
            tmps.give(k2, xd)
            cp_tok[j] = xd
        conv_last = {}
        conv_steps = []

        def tap(j, x):
            w = lambda: pcol("cv_dw_w_2", 4 * x + j)
            o = lambda: AC[:, j, :]
            i = lambda: CP[:, j, x:x + T]
            if x == 0:
                conv_last[j] = ts(dve, o, i, w, lambda: pcol("cv_dw_b_2", j), ALU.mult, ALU.add, cp_tok[j], t_pad,
                                  free1, t_par)
            else:
                conv_last[j] = stt(o, i, w, o, ALU.mult, ALU.add, conv_last[j])

        for j0 in (0, 2):
            for x in range(31):
                for j in (j0, j0 + 1):
                    conv_steps.append(lambda j=j, x=x: tap(j, x))

        v2 = vproj("dv", V2h, V2l, free1, scale=lambda t: (lambda: sm[:, 32 + t:33 + t]), stok=t_rc)
        dq_tok, dk_tok = {}, {}
        dq_free = [free1, free1]
        rt_free = [free1]

        def d_steps(h):
            p = h % 2
            out_ = []
            for b, nm, dh, dl, dt in ((0, "dq", DQh, DQl, dq_tok), (1, "dk", DKh, DKl, dk_tok)):
                ch = Chunk((nm, h), b, *h_r, rtok=lambda k: h_tok[k])

                def second(b=b, ch=ch, dh=dh, dl=dl, dt=dt):
                    m = ch.half(1)
                    ps = lambda: PS[b][:, :]
                    hi, lo = split_ps(lambda: RTh[:, :], lambda: RTl[:, :], ps, m, rt_free[0])
                    k1, t1, w1 = tmps.take()
                    x1 = tt(dve, lambda: t1[:, :], ps, lambda: CT[:, :], ALU.mult, m, w1, t_c2)
                    mm(ps, lambda: con_r("rot"), lambda: RTh[:, :], True, False, hi, lo, x1, t_conr)
                    m2 = mm(ps, lambda: con_r("rot"), lambda: RTl[:, :], False, True, lo, sig=True)
                    rt_free[0] = m2
                    k2, t2, w2 = tmps.take()
                    x2 = tt(dve, lambda: t2[:, :], ps, lambda: STb[:, :], ALU.mult, m2, w2, t_s2)
                    bank[b] = [x2]
                    x3 = tt(dve, lambda: t2[:, :], lambda: t2[:, :], lambda: t1[:, :], ALU.add, x2, x1)
                    dt[h] = split_sb(lambda: dh[p][:, :], lambda: dl[p][:, :], lambda: t2[:, :], x3, dq_free[p])
                    tmps.give(k1, x3)
                    tmps.give(k2, dt[h][1])

                out_ += [lambda ch=ch: ch.half(0), second]
            return out_

        at_tok = {}
        at_free = [free1]
        yf_tok = {}

        def qk_d(s):
            h, half = s // 2, s % 2
            p = h % 2
            for i in (2 * half, 2 * half + 1):
                n = 128 * (i + 1)
                got = []
                for c in range(2):
                    b = 2 + 2 * (i % 2) + c
                    r = 64 * c
                    o = lambda b=b, n=n: PS[b][:, 0:n]
                    mm3(o, lambda i=i, r=r: DQh[p][r:r + 64, 128 * i:128 * i + 128],
                        lambda i=i, r=r: DQl[p][r:r + 64, 128 * i:128 * i + 128],
                        lambda n=n, r=r: DKh[p][r:r + 64, 0:n], lambda n=n, r=r: DKl[p][r:r + 64, 0:n], True, False,
                        wh=[list(dq_tok[h]), list(dk_tok[h]), bank[b]])
                    m = mask(b, 128 * i, r, "f")
                    k1, t1, w1 = tmps.take()
                    x3, x4, rc = softmax_tile(b, n, 0.125, t1, m, w1)
                    got.append((k1, t1, x3, x4, rc))
                    bank[b] = [x3]
                (k1, t1, e1, r1, c1), (k2, t2, e2, r2, c2) = got
                n1 = lambda t1=t1, n=n: t1[:, 0:n]
                n2 = lambda t2=t2, n=n: t2[:, 0:n]
                x5 = ts(dve, n1, n1, c1, None, ALU.mult, None, e1, r1)
                x6 = ts(dve, c2, c2, lambda: sm[:, 24:25], None, ALU.mult, None, r2, t_nl)
                x7 = stt(n2, n2, c2, n1, ALU.mult, ALU.add, x6, x5, e2)
                tmps.give(k1, x7)
                at_tok[i] = (k2, t2, x7)
            if half == 1:
                dq_free[p] = m

        def mid_d(s):
            h, half = s // 2, s % 2
            for i in (2 * half, 2 * half + 1):
                k2, t2, x7 = at_tok[i]
                o = 128 * (i % 2)
                m, a, l = turn(2 + 2 * (i % 2), i + 1, t2, lambda i=i, o=o: ATh[:, 0:i + 1, o:o + 128],
                               lambda i=i, o=o: ATl[:, 0:i + 1, o:o + 128], [x7], at_free[0])
                tmps.give(k2, m)
                at_tok[i] = (a, l)

        def pv_d(s):
            h, half = s // 2, s % 2
            b = 6 + half
            js = 2 * half + 2
            for j in range(js):
                o0 = max(0, 128 * j - 256 * half)
                o = lambda o0=o0: PS[b][:, o0:256]
                w = [list(at_tok[2 * half + 1]), list(at_tok[2 * half]), list(v2[j]), bank[b]]
                m = mm3(o, lambda j=j: V2h[:, j, h * 128:(h + 1) * 128], lambda j=j: V2l[:, j, h * 128:(h + 1) * 128],
                        lambda j=j, o0=o0: ATh[:, j, o0:256], lambda j=j, o0=o0: ATl[:, j, o0:256],
                        j == 0, j == js - 1, wh=w, sig=j == js - 1)
            at_free[0] = m
            x = a_fn(lambda: YF[:, h, 256 * half:256 * half + 256], lambda: PS[b][:, 0:256], ACT.Copy, m, x_new, t_rb)
            bank[b] = [x]
            yf_tok[s] = x
            return m

        for f in d_steps(0):
            f()
            run(conv_steps, 8)
        qk_d(0)
        steps = []
        for s in range(8):
            if s % 2 == 0 and s < 6:
                steps += d_steps(s // 2 + 1)
            run(conv_steps, 8)
            mid_d(s)
            run(steps, 1)
            run(conv_steps, 8)
            if s < 7:
                if s % 2 == 1:
                    run(steps, 9)
                qk_d(s + 1)
            m = pv_d(s)
            run(steps, 1)
            run(conv_steps, 9)
        run(conv_steps, 999)
        att_done = m

        for j in range(4):
            p = sq_n[0] % 2
            sq_n[0] += 1
            hi, lo = split_sb(lambda p=p: SQh[p][:, :], lambda p=p: SQl[p][:, :], lambda j=j: AC[:, j, :],
                              conv_last[j], sq_free[p])
            mm(lambda: PS[6][:, :], lambda: con_r("o512"), lambda p=p: SQh[p][:, :], j == 0, False, hi,
               bank[6] if j == 0 else None)
            m = mm(lambda: PS[6][:, :], lambda: con_r("o512"), lambda p=p: SQl[p][:, :], False, j == 3, lo, sig=True)
            sq_free[p] = m
        dtok = {}
        for j in range(4):
            dtok[j] = tt(dve, lambda j=j: AC[:, j, :], lambda: PS[6][:, :], lambda j=j: AC[:, j, :], ALU.subtract, m)
            _, add = square(lambda j=j: AC[:, j, :], dtok[j])
            stt_ = add(7, "o512", j == 0, j == 3)
        bank[6] = [dtok[3]]
        kr_, tr_, wr_ = tmps.take()
        a, r_ = root(lambda: tr_[:, :], 7, stt_, wr_)
        bank[7] = [a]
        yc_tok = {}
        for j in range(4):
            k1, t1, w1 = tmps.take()
            s1 = lambda t1=t1: t1[:, :]
            x1 = stt(s1, lambda j=j: AC[:, j, :], -1.0, lambda: tr_[:, :], ALU.mult, ALU.mult, r_, dtok[j], w1)
            x2 = a_fn(s1, s1, ACT.Silu, x1, t_par, scale=lambda j=j: pcol("cv_ln_g_2", j),
                      bias=lambda j=j: pcol("cv_ln_b_2", j))
            yc_tok[j] = split_sb(lambda j=j: YCh[:, j, :], lambda j=j: YCl[:, j, :], s1, x2, att_done, lo=pool)
            tmps.give(k1, *yc_tok[j])
        tmps.give(kr_, x1)
        yd_tok = {}
        for h in range(4):
            sq_, add = square(lambda h=h: YF[:, h, :], yf_tok[2 * h], yf_tok[2 * h + 1])
            b = 6 + h % 2
            s_ = add(b, "o128", True, True)
            k1, t1, w1 = tmps.take()
            s1 = lambda t1=t1: t1[:, :]
            a, r_ = root(s1, b, s_, w1)
            bank[b] = [a]
            x1 = stt(s1, lambda h=h: YF[:, h, :], lambda: sm[:, 25:26], s1, ALU.mult, ALU.mult, r_, t_sg)
            yd_tok[h] = split_sb(lambda h=h: YDh[:, h, :], lambda h=h: YDl[:, h, :], s1, x1, att_done, lo=pool)
            tmps.give(k1, *yd_tok[h])

        h_read[0] = att_done
        def y2(k):
            return (lambda: YDh[:, k, :]) if k < 4 else (lambda: YCh[:, k - 4, :])
        st_tok = out_proj("wo2", lambda k: YDh[:, k, :] if k < 4 else YCh[:, k - 4, :],
                          lambda k: YDl[:, k, :] if k < 4 else YCl[:, k - 4, :],
                          lambda k: yd_tok[k] if k < 4 else yc_tok[k - 4], "norm_cross_g_2")
        a, t_rb = root(rb, 7, st_tok)
        bank[7] = [a]
        free2 = st_tok

        mem_tok = {}
        t_mem = None
        if not plan_only:
            t_mem = sp.dma(l_mem, lambda e: e.dma_start(MEMT[:, :, :], memin), free2)
        for k in range(KC):
            _, add = square(lambda k=k: MEMT[:, k, :], t_mem, n=M)
            s_ = add(6, "o1024", k == 0, k == KC - 1)
        a, r_ = root(lambda: MRB[:, :], 6, s_, n=M)
        bank[6] = [a]
        m_tok = [None] * KC
        for k in range(KC):
            k1, t1, w1 = tmps.take()
            s1 = lambda t1=t1: t1[:, 0:M]
            x1 = stt(s1, lambda k=k: MEMT[:, k, :], lambda k=k: pcol("norm_mem_g_2", k), lambda: MRB[:, :],
                     ALU.mult, ALU.mult, r_, w1)
            m_tok[k] = split_sb(lambda k=k: MTh[:, k, :], lambda k=k: MTl[:, k, :], s1, x1, free2)
            tmps.give(k1, m_tok[k][1])
        mem_read = x1

        cq_tok, ck_tok, cv_tok = {}, {}, {}
        ck_free = [free2, free2]
        cv_free = [free2, free2]
        m_r = (lambda k: MTh[:, k, :], lambda k: MTl[:, k, :])

        def c_steps(h):
            p = h % 2
            out_ = []
            for g in range(2):
                f = 2 * h + g
                ch = hproj(("cq", f), g)

                def fin(f=f, g=g, ch=ch):
                    m = ch.half(1)
                    k1, t1, w1 = tmps.take()
                    x = tt(dve, lambda: t1[:, :], lambda: PS[g][:, :], rb, ALU.mult, m, t_rb, w1)
                    bank[g] = [x]
                    cq_tok[f] = split_sb(lambda: Oh[:, f, :], lambda: Ol[:, f, :], lambda: t1[:, :], x, free2,
                                         mem_read)
                    tmps.give(k1, cq_tok[f][1])
                out_ += [lambda ch=ch: ch.half(0), fin]
            for g in range(2):
                f = 2 * h + g
                ch = Chunk(("ck", f), g, *m_r, rtok=lambda k: m_tok[k], n=M)

                def fin(f=f, g=g, ch=ch):
                    m = ch.half(1)
                    ck_tok[f] = split_ps(lambda: CKh[p][:, g, :], lambda: CKl[p][:, g, :],
                                         lambda: PS[g][:, 0:M], m, ck_free[p])
                    bank[g] = list(ck_tok[f])
                out_ += [lambda ch=ch: ch.half(0), fin]

            def vals():
                for u in range(2):
                    s, ta, tb, j = use(("cv", h, u))
                    for mt in range(2):
                        if u == 0:
                            pe.wait(bank[mt])
                        for kk in range(4):
                            k = 4 * u + kk
                            o = lambda mt=mt: PS[mt][:, 0:256]
                            lh = lambda k=k, mt=mt: MTh[:, k, mt * 128:(mt + 1) * 128]
                            ll = lambda k=k, mt=mt: MTl[:, k, mt * 128:(mt + 1) * 128]
                            rh = lambda s=s, kk=kk: WH[s][:, kk * 256:(kk + 1) * 256]
                            rl = lambda s=s, kk=kk: WL[s][:, kk * 256:(kk + 1) * 256]
                            mm(o, lh, rh, k == 0, False, ta, list(m_tok[k]))
                            mm(o, lh, rl, False, False, tb)
                            tok = mm(o, ll, rh, False, k == 7, sig=kk == 3)
                        if u == 1:
                            cv_tok[h, mt] = split_ps(lambda mt=mt: CVh[p][:, mt, :], lambda mt=mt: CVl[p][:, mt, :],
                                                     lambda mt=mt: PS[mt][:, 0:256], tok, cv_free[p])
                            bank[mt] = list(cv_tok[h, mt])
                    used(j, tok)
            out_.append(vals)
            return out_

        cp_free = [free2]
        ct_tok, ct2 = {}, {}

        def qk_c(h):
            p = h % 2
            for i in range(4):
                b = 2 + i
                for g in range(2):
                    f = 2 * h + g
                    m = mm3(lambda b=b: PS[b][:, 0:M], lambda f=f, i=i: Oh[:, f, 128 * i:128 * i + 128],
                            lambda f=f, i=i: Ol[:, f, 128 * i:128 * i + 128],
                            lambda g=g: CKh[p][:, g, :], lambda g=g: CKl[p][:, g, :], g == 0, g == 1,
                            wh=[list(cq_tok[f]), list(ck_tok[f]), bank[b]], sig=g == 1)
                k1, t1, w1 = tmps.take()
                x3, x4, rc = softmax_tile(b, M, 1.0 / 16, t1, m, w1)
                x5 = ts(dve, lambda t1=t1: t1[:, 0:M], lambda t1=t1: t1[:, 0:M], rc, None, ALU.mult, None, x4, x3)
                bank[b] = [x3]
                ct_tok[i] = (k1, t1, x5)
            ck_free[p] = m
            qk_c.last = m

        def mid_c(h):
            for i in range(4):
                k1, t1, x5 = ct_tok[i]
                m, a, l = turn(2 + i, 2, t1, lambda i=i: CPh[:, :, 128 * i:128 * i + 128],
                               lambda i=i: CPl[:, :, 128 * i:128 * i + 128], [x5], cp_free[0])
                tmps.give(k1, m)
                ct2[i] = (a, l)

        o_tok = {}

        def pv_c(h, q_done):
            p = h % 2
            for g in range(2):
                f, b = 2 * h + g, 6 + g
                for mt in range(2):
                    m = mm3(lambda b=b: PS[b][:, :], lambda mt=mt, g=g: CVh[p][:, mt, 128 * g:128 * g + 128],
                            lambda mt=mt, g=g: CVl[p][:, mt, 128 * g:128 * g + 128],
                            lambda mt=mt: CPh[:, mt, :], lambda mt=mt: CPl[:, mt, :], mt == 0, mt == 1,
                            wh=[[list(ct2[i]) for i in range(4)], list(cv_tok[h, mt]), bank[b]], sig=mt == 1)
                o_tok[f] = split_ps(lambda f=f: Oh[:, f, :], lambda f=f: Ol[:, f, :], lambda b=b: PS[b][:, :], m,
                                    q_done)
                bank[b] = list(o_tok[f])
            cp_free[0] = m
            cv_free[p] = m

        for f in c_steps(0):
            f()
        qk_c(0)
        steps = []
        for h in range(4):
            if h < 3:
                steps += c_steps(h + 1)
            run(steps, 3)
            q_done = qk_c.last
            mid_c(h)
            run(steps, 3)
            if h < 3:
                run(steps, 99)
                qk_c(h + 1)
            pv_c(h, q_done)
        h_read[0] = (pe, pe.n)
        st_tok = out_proj("co", lambda k: Oh[:, k, :], lambda k: Ol[:, k, :], lambda k: o_tok[k], "norm_ffn_g_2")
        a, t_rb = root(rb, 7, st_tok)
        bank[7] = [a]
        free3 = st_tok

        cb_tok = [pool(lambda e, i=i: e.memset(CB[i][:, 0:2], 0.0), free3) for i in range(4)]
        cb_n = [0]
        cb_free = [None] * 4
        z_tok, z_free = {}, {}

        def conv3(f, b):
            tok = hproj(("up", f), b).both()
            q = cb_n[0] % 4
            cb_n[0] += 1
            x1 = tt(dve, lambda: CB[q][:, 2:2 + T], lambda: PS[b][:, :], rb, ALU.mult, tok, t_rb, cb_free[q], free3)
            bank[b] = [x1]
            k1, t1, w1 = tmps.take()
            s1 = lambda: t1[:, :]
            x2 = a_fn(s1, lambda: CB[q][:, 2:2 + T], ACT.Copy, x1, w1, scale=lambda: pcol("ffn_dw_w_2", 88 + f))
            x3 = stt(s1, lambda: CB[q][:, 1:1 + T], lambda: pcol("ffn_dw_w_2", 44 + f), s1, ALU.mult, ALU.add, x2,
                     cb_tok[q])
            x4 = stt(s1, lambda: CB[q][:, 0:T], lambda: pcol("ffn_dw_w_2", f), s1, ALU.mult, ALU.add, x3)
            cb_free[q] = x4
            return k1, t1, x4

        def up(n):
            s = n % NZ
            k1, t1, x1 = conv3(n, 2 * (n % 2))
            g = a_fn(lambda: t1[:, :], lambda: t1[:, :], ACT.Silu, x1)
            k2, t2, x2 = conv3(22 + n, 2 * (n % 2) + 1)
            z = tt(dve, lambda: t2[:, :], lambda: t2[:, :], lambda: t1[:, :], ALU.mult, g, x2)
            z_tok[n] = split_sb(lambda: ZH[:, s, :], lambda: ZL[:, s, :], lambda: t2[:, :], z, z_free.get(s), free3,
                                lo=pool)
            tmps.give(k1, z)
            tmps.give(k2, *z_tok[n])

        def down(g, last):
            add = None
            nk = min(8, 22 - 8 * g)
            for f in range(KC):
                b = 4 + f % 2
                zz = [(8 * g + k) % NZ for k in range(nk)]
                tok = Chunk(("down", g, f), b, lambda k: ZH[:, zz[k], :], lambda k: ZL[:, zz[k], :], nk=nk,
                            rtok=lambda k: z_tok[8 * g + k]).both()
                if last:
                    if add:
                        add(7, "o1024", f == 1, False)
                    add = residual(f, b, tok, None)
                else:
                    xf = lambda f=f: X[:, f, :]
                    x = tt(dve, xf, lambda b=b: PS[b][:, :], xf, ALU.add, tok, x_rd[f])
                    bank[b] = [x]
                    x_rd[f] = [x]
            for s in zz:
                z_free[s] = tok
            return add(7, "o1024", False, True) if last else None

        for n in range(9):
            up(n)
        down(0, False)
        for n in range(9, 17):
            up(n)
        down(1, False)
        for n in range(17, 22):
            up(n)
        st_tok = down(2, True)
        a, t_rb = root(rb, 7, st_tok)
        for f in range(KC):
            x = stt(lambda f=f: X[:, f, :], lambda f=f: X[:, f, :], lambda f=f: pcol("norm_final_g_2", f), rb,
                    ALU.mult, ALU.mult, t_rb, x_rd[f])
            if not plan_only:
                t_out = sp.dma(l_out, lambda e, f=f: e.dma_start(out[f * 128:(f + 1) * 128, :], X[:, f, :]), x)
        if plan_only:
            return names
        sp.wait(t_out)
        assert state["use"] == len(order) and state["dma"] == len(order), state

        for q in (pe, act, dve, pool, sp):
            q.sem = st.enter_context(nc.semaphore("s_" + q.name))
        for l in lines:
            l.sem = st.enter_context(nc.semaphore(l.name))
        with nc.Block() as block:
            block.tensor(lambda e: pe.emit(e))
            block.scalar(lambda e: act.emit(e))
            block.vector(lambda e: dve.emit(e))
            block.gpsimd(lambda e: pool.emit(e))
            block.sync(lambda e: sp.emit(e))
    return names


def pack_units(order, w):
    def cols(a, c0, n=128, k0=0, nk=8):
        blk = a[128 * k0:128 * (k0 + nk), c0:c0 + n]
        if blk.shape[1] < n:
            blk = np.concatenate([blk, np.zeros((blk.shape[0], n - blk.shape[1]), blk.dtype)], axis=1)
        return blk.reshape(nk, 128, n).transpose(1, 0, 2).reshape(128, nk * n)

    win, wada, wsb, wfox, wout = w["w_in"][0], w["w_ada"][0], w["w_o_sb"][0], w["w_o_fox"][0], w["w_out"][0]
    win2, wout2, wcq, wckv, wco = w["w_in_2"][0], w["w_out_2"][0], w["w_cq_2"][0], w["w_ckv_2"][0], w["w_co_2"][0]
    wup, wdown = w["w_up_2"][0], w["w_down_2"][0]
    res = np.zeros((len(order), 128, U), np.float32)
    for n, u in enumerate(order):
        k = u[0]
        if k == "ada":
            b = wada[128 * u[2]:128 * u[2] + 128, 1024 * u[1]:1024 * u[1] + 1024]
        elif k in ("aq", "ak", "az", "bq", "bk", "bz"):
            o = {"aq": 0, "ak": 512, "az": 1536, "bq": 2048, "bk": 2560, "bz": 3584}[k]
            b = cols(win, o + 128 * u[1])
        elif k in ("av", "bv"):
            b = cols(win, 1024 if k == "av" else 3072, 512, 2 * u[1], 2)
        elif k == "f":
            b = cols(win[:, 4096:4104], 0)
        elif k == "g":
            b = cols(win, 4104 + 128 * u[1])
        elif k in ("oa", "ob"):
            b = cols(wsb if k == "oa" else wfox, 256 * u[1], 256, 0, 4)
        elif k == "wo":
            b = cols(wout, 128 * u[1])
        elif k == "u":
            b = cols(win2, 1536 + 128 * u[1])
        elif k == "dq":
            b = cols(win2, 128 * u[1])
        elif k == "dk":
            b = cols(win2, 512 + 128 * u[1])
        elif k == "dv":
            b = cols(win2, 1024, 512, 2 * u[1], 2)
        elif k == "wo2":
            b = cols(wout2, 128 * u[1])
        elif k == "cq":
            b = cols(wcq, 128 * u[1])
        elif k == "ck":
            b = cols(wckv, 128 * u[1])
        elif k == "cv":
            b = cols(wckv, 1024 + 256 * u[1], 256, 4 * u[2], 4)
        elif k == "co":
            b = cols(wco, 128 * u[1])
        elif k == "up":
            b = cols(wup, 128 * u[1])
        elif k == "down":
            b = cols(wdown, 128 * u[2], 128, 8 * u[1], min(8, 22 - 8 * u[1]))
        res[n, :, 0:b.shape[1]] = b
    return res


def pack_params(w):
    res = np.zeros((128, NPAR), np.float32)
    for name, n in PARAMS:
        a = np.asarray(w[name])
        o = POFF[name]
        if name == "b_forget":
            res[0:8, o] = a.reshape(8)
        elif name == "cv_dw_w_2":
            res[:, o:o + n] = a.reshape(31, 4, 128).transpose(2, 0, 1).reshape(128, n)
        elif name == "ffn_dw_w_2":
            res[:, o:o + n] = a.reshape(3, 44, 128).transpose(2, 0, 1).reshape(128, n)
        else:
            res[:, o:o + n] = a.reshape(n, 128).T
    return res


def kernel(**inputs):
    import concourse.bacc as bacc
    from concourse.bass_utils import run_bass_kernel_spmd

    w = {k: np.asarray(v) for k, v in inputs.items()}
    order = build(None, None)
    arrays = {
        "units": pack_units(order, w),
        "par": pack_params(w),
        "con": constants(),
        "msk": masks(),
        "xin": np.ascontiguousarray(w["x"][0].T.reshape(KC, 128, T).transpose(1, 0, 2)),
        "memin": np.ascontiguousarray(w["mem_2"][0].T.reshape(KC, 128, M).transpose(1, 0, 2)),
        "posin": np.ascontiguousarray(np.broadcast_to(w["positions_2"][0], (128, T))),
        "lamin": np.ascontiguousarray(np.broadcast_to(np.concatenate(
            [w[n][0] for n in ("lam_q1_2", "lam_k1_2", "lam_q2_2", "lam_k2_2")]), (128, 256))),
    }
    nc = bacc.Bacc("TRN2", target_bir_lowering=False, num_devices=1)
    args = [nc.dram_tensor(n, a.shape, mybir.dt.from_np(a.dtype), kind="ExternalInput").ap()
            for n, a in arrays.items()]
    args.append(nc.dram_tensor("out", (D, T), F32, kind="ExternalOutput").ap())
    build(nc, args, order)
    r = run_bass_kernel_spmd(nc, [arrays], core_ids=[0])
    return np.ascontiguousarray(r.results[0]["out"].T).reshape(1, T, D)
```

```python
from contextlib import ExitStack

import numpy as np

import concourse.bass as bass
from concourse import mybir

F32 = mybir.dt.float32
F32R = mybir.dt.float32r
BF16 = mybir.dt.bfloat16
I32 = mybir.dt.int32
ALU = mybir.AluOpType
ACT = mybir.ActivationFunctionType
AX_X = mybir.AxisListType.X

P = 128
T = 512
D = 1024
KC = 8
M = 256
EPS = 1e-6
NEG = -1e30
LAM_INIT = 0.2
U = 1024

PARAMS = [("norm_g", 8), ("b_ada", 24), ("b_gate", 16), ("norm_mix_g_2", 8), ("norm_cross_g_2", 8),
          ("norm_mem_g_2", 8), ("norm_ffn_g_2", 8), ("norm_final_g_2", 8), ("final_g", 8), ("subln_g_2", 1),
          ("cv_dw_b_2", 4), ("cv_ln_g_2", 4), ("cv_ln_b_2", 4), ("c", 8), ("cv_dw_w_2", 124),
          ("ffn_dw_w_2", 132), ("b_forget", 1)]
POFF = {}
_o = 0
for _n, _w in PARAMS:
    POFF[_n] = _o
    _o += _w
NPAR = _o

CONSTS = ["ident", "tri8", "m8", "o1024", "o128", "o512", "rot", "triu", "one"]
NCON = len(CONSTS) * 128 + 16


def constants():
    i = np.arange(128)
    c = {
        "ident": np.eye(128),
        "tri8": np.where(i[:, None] >= i[None, :], -8.0, 0.0),
        "m8": np.full((128, 128), -8.0),
        "o1024": np.full((128, 128), 2.0 ** -10),
        "o128": np.full((128, 128), 2.0 ** -7),
        "o512": np.full((128, 128), 2.0 ** -9),
        "triu": np.where(i[:, None] <= i[None, :], 1.0, 0.0),
        "one": np.ones((128, 128)),
    }
    rot = np.zeros((128, 128))
    for g in (0, 64):
        for j in range(8):
            rot[g + 8 + j, g + j] = -1.0
            rot[g + j, g + 8 + j] = 1.0
    c["rot"] = rot
    out = np.zeros((128, NCON), np.float32)
    for n, name in enumerate(CONSTS):
        out[:, n * 128:(n + 1) * 128] = c[name]
    o = len(CONSTS) * 128
    for h in range(8):
        out[h, o + h] = 1.0
        out[32 + h, o + h] = 1.0
        out[64 + h, o + h] = 1.0
        out[96 + h, o + h] = 1.0
    inv = np.power(np.float32(500000.0), -(np.arange(0, 16, 2, dtype=np.float32) / np.float32(16)))
    for g in (0, 64):
        out[g:g + 8, o + 8] = inv
        out[g + 8:g + 16, o + 8] = inv
    out[:, o + 9] = EPS
    return out


def masks():
    k = np.arange(128) % 64
    i = np.arange(128)
    out = np.zeros((128, 1024), np.float32)
    for g in range(2):
        row = (k + 64 * g)[:, None]
        out[:, g * 128:g * 128 + 128] = row == i[None, :]
        out[:, 256 + g * 128:384 + g * 128] = np.where(row >= i[None, :], NEG, 0.0)
        out[:, 512 + g * 128:640 + g * 128] = np.where(i[None, :] > row, NEG, 0.0)
    return out


class Queue:

    def __init__(self, name):
        self.name, self.n, self.items, self.seen, self.sem = name, 0, [], {}, None

    def __call__(self, f, *waits, sig=True):
        self.wait(*waits)
        self.items.append((f, self if sig else None, 1))
        if sig:
            self.n += 1
        return (self, self.n)

    def wait(self, *waits):
        for w in waits:
            if w is None:
                continue
            if isinstance(w, list):
                self.wait(*w)
                continue
            src, n = w
            if self.seen.get(src.name, 0) < n:
                self.seen[src.name] = n
                self.items.append((None, src, n))

    def dma(self, line, f, *waits):
        self.wait(*waits)
        line.n += 16
        self.items.append((f, line, 16))
        return (line, line.n)

    def emit(self, eng):
        for f, src, n in self.items:
            if f is None:
                eng.wait_ge(src.sem, n)
            else:
                ins = f(eng)
                if src is not None:
                    ins.then_inc(src.sem, n)


class Line:

    def __init__(self, name):
        self.name, self.n, self.sem = name, 0, None


class Temps:

    def __init__(self, tiles):
        self.tiles, self.i, self.last, self.held = tiles, 0, [None] * len(tiles), set()

    def take(self):
        k = self.i % len(self.tiles)
        self.i += 1
        assert k not in self.held
        self.held.add(k)
        return k, self.tiles[k], self.last[k]

    def give(self, k, *tokens):
        self.last[k] = list(tokens)
        self.held.discard(k)


def build(nc, args, order=None):
    names = []
    plan_only = order is None
    raw_n = 4
    spl_n = 4
    if not plan_only:
        units, par, con, msk, xin, memin, posin, lamin, out = args
    st = ExitStack()

    off = [16512]

    def at(name, shape, dt, offset=None):
        if plan_only:
            return None
        nb = int(np.prod(shape[1:])) * (2 if dt == BF16 else 4)
        if offset is None:
            offset = off[0]
            off[0] += (nb + 31) // 32 * 32
        assert offset + nb <= 229344, (name, offset + nb)
        return nc.alloc_sbuf_tensor_at(name, list(shape), dt, offset=offset)

    with st:
        RAW = [at(f"raw{i}", [P, U], F32) for i in range(raw_n)]
        WH = [at(f"wh{i}", [P, U], F32R) for i in range(spl_n)]
        WL = [at(f"wl{i}", [P, U], F32R) for i in range(spl_n)]
        HH = at("hh", [P, KC, T], F32R)
        HL = at("hl", [P, KC, T], F32R)
        n_tmp = 7
        TM = [at(f"tm{i}", [P, T], F32) for i in range(n_tmp)]
        con_raw = at("con_raw", [P, NCON], F32)
        conr = at("conr", [P, NCON], F32R)
        MK = at("mk", [P, 768], BF16)
        par_sb = at("par_sb", [P, NPAR], F32)
        sm = at("sm", [P, 96], F32)
        stat = at("stat", [P, 64], F32)
        nrm = at("nrm", [P, 96], F32)
        sq0 = off[0]
        CV = [at(f"cvt{i}", [P, T], F32, sq0 + 2048 + 4096 * i) for i in range(2)]
        SQh = [at(f"sqh{i}", [P, T], F32R) for i in range(2)]
        SQl = [at(f"sql{i}", [P, T], F32R) for i in range(2)]
        base = off[0]
        X = at("x", [P, KC, T], F32)
        a1 = off[0]
        off[0] = base
        SPh = at("sph", [P, 1280], F32R)
        SPl = at("spl", [P, 1280], F32R)
        EWh = at("ewh", [P, 1280], F32R)
        EWl = at("ewl", [P, 1280], F32R)
        PTh = at("pth", [P, 4, T], F32R, base)
        PTl = at("ptl", [P, 4, T], F32R, base + 8192)
        VAh = at("vah", [P, 4, T], F32R)
        VAl = at("val", [P, 4, T], F32R)
        VBh = at("vbh", [P, 4, T], F32R)
        VBl = at("vbl", [P, 4, T], F32R)
        YAh = at("yah", [P, 4, T], F32R)
        YAl = at("yal", [P, 4, T], F32R)
        qk0 = off[0]
        Qh = [at(f"qh{i}", [P, T], F32R) for i in range(2)]
        Ql = [at(f"ql{i}", [P, T], F32R) for i in range(2)]
        Kh = [at(f"kh{i}", [P, T], F32R) for i in range(2)]
        Kl = [at(f"kl{i}", [P, T], F32R) for i in range(2)]
        MG2h = at("mg2h", [P, 4, T], F32R, qk0)
        MG2l = at("mg2l", [P, 4, T], F32R, qk0 + 8192)
        SZ = [at(f"sz{i}", [P, T], F32) for i in range(2)]
        FT = at("ft", [104, T], F32R)
        MA = at("ma", [P, U], F32, a1)
        off[0] = a1
        RB = at("rb", [P, T], F32)
        b2 = off[0]
        CT = at("ct", [P, T], F32)
        STb = at("stb", [P, T], F32)
        cp0 = off[0]
        CP = at("cp", [P, 4, T + 30], F32)
        ac0 = off[0]
        AC = at("ac", [P, 4, T], F32)
        V2h = at("v2h", [P, 4, T], F32R)
        V2l = at("v2l", [P, 4, T], F32R)
        dq0 = off[0]
        DQh, DQl, DKh, DKl = ([None] * 2 for _ in range(4))
        for i in range(2):
            DQh[i], DQl[i] = at(f"dqh{i}", [P, T], F32R), at(f"dql{i}", [P, T], F32R)
            DKh[i], DKl[i] = at(f"dkh{i}", [P, T], F32R), at(f"dkl{i}", [P, T], F32R)
        yf0 = off[0]
        YF = at("yf", [P, 4, T], F32)
        ATh = at("ath", [P, 4, 256], F32R)
        ATl = at("atl", [P, 4, 256], F32R)
        RT = [at(f"rt{i}", [P, T], F32, off[0] + 2048 * i) for i in range(2)]
        RTh = at("rth", [P, T], F32R)
        RTl = at("rtl", [P, T], F32R)
        YDh = at("ydh", [P, 4, T], F32R, dq0)
        YDl = at("ydl", [P, 4, T], F32R, yf0)
        YCh = at("ych", [P, 4, T], F32R, cp0)
        YCl = at("ycl", [P, 4, T], F32R, ac0)
        off[0] = b2
        ymem = off[0] + 24576
        Oh = at("oh", [P, KC, T], F32R)
        Ol = at("ol", [P, KC, T], F32R)
        MTh = at("mth", [P, KC, M], F32R)
        MTl = at("mtl", [P, KC, M], F32R)
        CKh = [at(f"ckh{i}", [P, 2, M], F32R) for i in range(2)]
        CKl = [at(f"ckl{i}", [P, 2, M], F32R) for i in range(2)]
        CVh = [at(f"cvh{i}", [P, 2, M], F32R) for i in range(2)]
        CVl = [at(f"cvl{i}", [P, 2, M], F32R) for i in range(2)]
        MRB = at("mrb", [P, M], F32)
        CPh = at("cph", [P, 2, T], F32R)
        CPl = at("cpl", [P, 2, T], F32R)
        MEMT = at("memt", [P, KC, M], F32, ymem)
        off[0] = b2
        NZ = 10
        ZH = at("zh", [P, NZ, T], F32R)
        ZL = at("zl", [P, NZ, T], F32R)
        CB = [at(f"cb{i}", [P, T + 2], F32) for i in range(4)]

        if not plan_only:
            PS = [nc.alloc_psum_tensor(f"ps{i}", [P, T], F32) for i in range(8)]

        pe, act, dve, pool, sp = (Queue(n) for n in ("pe", "act", "dve", "pool", "sp"))
        l_raw = [Line(f"l_raw{i}") for i in range(raw_n)]
        l_mk0, l_mk1, l_x, l_xb, l_x2, l_mem, l_con, l_par, l_pos, l_lam, l_out = (
            Line(n) for n in ("l_mk0", "l_mk1", "l_x", "l_xb", "l_x2", "l_mem", "l_con", "l_par", "l_pos", "l_lam", "l_out"))
        l_msk = [l_mk0, l_mk1]
        lines = l_raw + l_msk + [l_x, l_xb, l_x2, l_mem, l_con, l_par, l_pos, l_lam, l_out]

        def con_f(name, w=128):
            o = CONSTS.index(name) * 128
            return con_raw[:, o:o + w]

        def con_r(name):
            o = CONSTS.index(name) * 128
            return conr[:, o:o + 128]

        CO = len(CONSTS) * 128

        def pcol(name, j=0, rows=P):
            return par_sb[0:rows, POFF[name] + j:POFF[name] + j + 1]

        def a_fn(o, i, func, *w, scale=1.0, bias=None, accum=None):
            def f(e):
                k = {} if accum is None else {"accum_out": accum()}
                k["scale"] = scale() if callable(scale) else scale
                if bias is not None:
                    k["bias"] = bias() if callable(bias) else bias
                return e.activation(o(), i(), func, **k)
            return act(f, *w)

        def tt(q, o, a, b, op, *w):
            return q(lambda e: e.tensor_tensor(o(), a(), b(), op), *w)

        def stt(o, a, s, b, op0, op1, *w):
            return dve(lambda e: e.scalar_tensor_tensor(
                o(), a(), s() if callable(s) else s, b(), op0, op1), *w)

        def ts(q, o, a, s1, s2, op0, op1, *w):
            def f(e):
                x1 = s1() if callable(s1) else s1
                x2 = s2() if callable(s2) else s2
                if op1 is None:
                    return e.tensor_scalar(o(), a(), x1, None, op0)
                return e.tensor_scalar(o(), a(), x1, x2, op0, op1)
            return q(f, *w)

        def cp(q, o, i, *w):
            return q(lambda e: e.tensor_copy(o(), i()), *w)

        def as32(f):
            return lambda: f().bitcast(F32)

        def split_ps(h, l, src, *w, scale=None):
            if scale is None:
                a = a_fn(h, src, ACT.Copy, *w)
                b = tt(dve, l, src, as32(h), ALU.subtract, a, *w)
            else:
                a = a_fn(h, src, ACT.Copy, *w, scale=scale)
                b = stt(l, src, scale, as32(h), ALU.mult, ALU.subtract, a, *w)
            return a, b

        def split_sb(h, l, src, *w, lo=None):
            a = cp(dve, h, src, *w)
            b = tt(lo or dve, l, src, as32(h), ALU.subtract, a, *w)
            return a, b

        state = {"dma": 0, "split": 0, "use": 0}
        raw_free = [None] * raw_n
        wh_ready = {}
        spl_free = {}
        raw_tok = {}

        def send(j):
            s = j % raw_n
            raw_tok[j] = sp.dma(l_raw[s], lambda e, s=s, j=j: e.dma_start(RAW[s][:, :], units[j]),
                                raw_free[s])

        slot_of = {}
        split_users = []

        read = set()

        def pump(j):
            read.add(j)
            while state["dma"] < len(order) and state["dma"] - raw_n in read:
                send(state["dma"])
                state["dma"] += 1

        def ahead():
            while state["split"] < len(order):
                j = state["split"]
                if order[j][0] == "ada":
                    state["split"] += 1
                    continue
                if len(split_users) >= spl_n and split_users[-spl_n] not in spl_free:
                    break
                if j > state["use"] + spl_n - 1:
                    break
                if j >= state["dma"]:
                    break
                s = len(split_users) % spl_n
                w = spl_free[split_users[-spl_n]] if len(split_users) >= spl_n else None
                r = j % raw_n
                a = act(lambda e, s=s, r=r: e.activation(WH[s][:, :], RAW[r][:, :], ACT.Copy), raw_tok[j], w)
                b = pool(lambda e, s=s, r=r: e.tensor_tensor(WL[s][:, :], RAW[r][:, :],
                                                             WH[s][:, :].bitcast(F32), ALU.subtract),
                         raw_tok[j], a, w)
                wh_ready[j] = (s, a, b)
                raw_free[r] = [a, b]
                split_users.append(j)
                state["split"] += 1
                pump(j)

        def use(name):
            if plan_only:
                names.append(name)
                return 0, None, None, len(names) - 1
            j = state["use"]
            assert order[j] == name, (order[j], name)
            ahead()
            assert j in wh_ready, (j, name, state)
            s, a, b = wh_ready[j]
            state["use"] += 1
            return s, a, b, j

        def used(j, tok):
            spl_free[j] = tok
            if not plan_only:
                ahead()

        def use_raw(name):
            if plan_only:
                names.append(name)
                return 0, None, 0
            j = state["use"]
            assert order[j] == name, (order[j], name)
            state["use"] += 1
            return j % raw_n, raw_tok[j], j

        def used_raw(j, tok):
            if plan_only:
                return
            raw_free[j % raw_n] = [tok]
            pump(j)
            ahead()

        def mm(o, l, r, start, stop, *w, sig=False, skip=False):
            return pe(lambda e: e.matmul(o(), l(), r(), start=start, stop=stop, skip_group_check=skip),
                      *w, sig=sig)

        def mm3(o, lh, ll, rh, rl, first, last, wh=(), wl=(), sig=False):
            mm(o, lh, rh, first, False, *wh)
            mm(o, lh, rl, False, False, *wl)
            return mm(o, ll, rh, False, last, sig=sig)

        bank = [None] * 8

        class Chunk:

            def __init__(self, name, b, rh, rl, n=T, nk=KC, rtok=None, ks=None):
                self.a = (name, b, rh, rl, n, nk, rtok, ks or tuple(range(nk)))

            def half(self, part):
                name, b, rh, rl, n, nk, rtok, order_k = self.a
                if part == 0:
                    self.u = use(name)
                    s, ta, tb, j = self.u
                    pe.wait(bank[b])
                s, ta, tb, j = self.u
                ks = order_k[:nk // 2] if part == 0 else order_k[nk // 2:]
                tok = None
                for k in ks:
                    lh = lambda k=k, s=s: WH[s][:, k * 128:(k + 1) * 128]
                    ll = lambda k=k, s=s: WL[s][:, k * 128:(k + 1) * 128]
                    rt = rtok(k) if rtok else (None, None)
                    o = lambda b=b, n=n: PS[b][:, 0:n]
                    mm(o, lh, lambda k=k: rh(k), k == order_k[0], False, ta, rt[0])
                    mm(o, lh, lambda k=k: rl(k), False, False, rt[1])
                    tok = mm(o, ll, lambda k=k: rh(k), False, k == order_k[-1], tb, sig=k == order_k[-1])
                if part == 1:
                    used(j, tok)
                    self.tok = tok
                return tok

            def both(self):
                self.half(0)
                return self.half(1)

        h_r = (lambda k: HH[:, k, :], lambda k: HL[:, k, :])
        h_tok = [(None, None)] * KC
        h_read = [None]

        def hproj(name, b, **kw):
            return Chunk(name, b, *h_r, rtok=lambda k: h_tok[k], **kw)

        if not plan_only:
            t_par = sp.dma(l_par, lambda e: e.dma_start(par_sb[:, :], par))
            t_x = [sp.dma(l_x, lambda e: e.dma_start(X[:, 0:4, :], xin[:, 0:4, :])), None]
            send(0)
            t_x[1] = sp.dma(l_xb, lambda e: e.dma_start(X[:, 4:8, :], xin[:, 4:8, :]))
            t_con = sp.dma(l_con, lambda e: e.dma_start(con_raw[:, :], con))
            for j in range(1, raw_n):
                send(j)
            state["dma"] = raw_n
        else:
            t_con = t_par = None
            t_x = [None, None]
        t_conr = cp(dve, lambda: conr[:, :], lambda: con_raw[:, :], t_con)
        tmps = Temps(TM)
        late_t = Temps(RT if not plan_only else [None] * 2)
        scr = [tmps]
        t_mk = []
        for g, w in ((0, 512), (1, 256)):
            i, t, _ = tmps.take()
            tm = None
            if not plan_only:
                tm = sp.dma(l_msk[g], lambda e, t=t, g=g: e.dma_start(t[:, :], msk[:, 512 * g:512 * g + 512]))
            t_mk.append(cp(dve, lambda g=g, w=w: MK[:, 512 * g:512 * g + w], lambda t=t, w=w: t[:, 0:w], tm))
            tmps.give(i, t_mk[-1])

        def mask(b, c0, r, which):
            o = lambda: PS[b][:, c0:c0 + 128]
            m0 = 256 if which == "s" else 512
            mm(o, lambda: MK[r:r + 64, 0:128], lambda: MK[r:r + 64, m0:m0 + 128], False, False, *t_mk)
            return mm(o, lambda: MK[r:r + 64, 128:256], lambda: MK[r:r + 64, m0 + 128:m0 + 256], False, True,
                      sig=True)

        def eps():
            return con_raw[:, CO + 9:CO + 10]

        sq_n = [0]
        sq_free = [None, None]

        def square(src, *w, n=T, scale=1.0, q=None):
            ring = scr[0]
            i, t, lw = ring.take()
            p = sq_n[0] % 2
            sq_n[0] += 1
            a = a_fn(lambda: t[:, 0:n], src, ACT.Square, lw, *w, scale=scale)
            if q is None:
                h = cp(dve, lambda: SQh[p][:, 0:n], lambda: t[:, 0:n], a, sq_free[p])
            else:
                h = a_fn(lambda: SQh[p][:, 0:n], lambda: t[:, 0:n], ACT.Copy, a, sq_free[p])
            l = tt(q or dve, lambda: SQl[p][:, 0:n], lambda: t[:, 0:n], lambda: SQh[p][:, 0:n].bitcast(F32),
                   ALU.subtract, h, sq_free[p])
            ring.give(i, l)

            def add(b, ones, first, last):
                out_ = lambda: PS[b][:, 0:n]
                mm(out_, lambda: con_r(ones), lambda: SQh[p][:, 0:n], first, False, h, t_conr,
                   bank[b] if first else None)
                tok = mm(out_, lambda: con_r(ones), lambda: SQl[p][:, 0:n], False, last, l, sig=True)
                sq_free[p] = tok
                return tok

            return a, add

        nrm_n = [0]

        def warm(func):
            a_fn(lambda: sm[:, 60:61], lambda: con_raw[:, 0:1], func, t_con, (act, act.n))

        def root_cols(b, *w, n=T, raw=False):
            k = 8 * (nrm_n[0] % 8)
            nrm_n[0] += 1
            m = n // 128
            ring = scr[0]
            i, t, lw = ring.take()
            v = lambda: t[:, 0:n].rearrange("p (m j) -> p m j", m=m)
            c = lambda: nrm[:, k:k + m]
            d = dve(lambda e: e.tensor_tensor(
                v(), PS[b][:, 0:n].rearrange("p (m j) -> p m j", m=m),
                con_f("ident").unsqueeze(1).to_broadcast([P, m, 128]), ALU.mult), lw, t_con, *w)
            bank[b] = [d]
            d = dve(lambda e: e.tensor_reduce(c(), v(), AX_X, ALU.add), d)
            ring.give(i, d)
            if raw:
                return d, c
            a = a_fn(c, c, ACT.Sqrt, d, bias=eps)
            return dve(lambda e: e.reciprocal(c(), c()), a), c

        def spread(b, cols, *w, n=T):
            ring = scr[0]
            i, t, lw = ring.take()
            m = n // 128
            d = dve(lambda e: e.tensor_tensor(
                t[:, 0:n].rearrange("p (m j) -> p m j", m=m),
                con_f("ident").unsqueeze(1).to_broadcast([P, m, 128]),
                cols()[:, 0:m].unsqueeze(2).to_broadcast([P, m, 128]), ALU.mult), lw, *w, t_con)
            tok = mm(lambda: PS[b][:, 0:n], lambda: con_f("one"), lambda: t[:, 0:n], True, True, d, bank[b], sig=True)
            ring.give(i, tok)
            return tok

        def root(dst, b, *w, n=T):
            r, c = root_cols(b, *w, n=n)
            m = spread(b, c, r, n=n)
            x = cp(dve, dst, lambda: PS[b][:, 0:n], m, *w)
            bank[b] = [x]
            return x, x

        def mod_step(part, k, tok):
            r, tr, j = use_raw(("ada", part, k))
            if k == 0:
                tok = ts(dve, lambda: MA[:, :], lambda: RAW[r][:, :], lambda: pcol("c", k), None,
                         ALU.mult, None, tr, t_par, tok)
            else:
                tok = stt(lambda: MA[:, :], lambda: RAW[r][:, :], lambda: pcol("c", k),
                          lambda: MA[:, :], ALU.mult, ALU.add, tr, tok)
            used_raw(j, tok)
            return tok

        def mod_end(part, tok, b):
            for f in range(8):
                m = mm(lambda f=f: PS[b][:, f:f + 1], lambda f=f: MA[:, f * 128:(f + 1) * 128],
                       lambda: con_f("one", 1), True, True, tok, t_con, bank[b], sig=True)
            a = tt(dve, lambda: sm[:, part * 8:part * 8 + 8], lambda: PS[b][:, 0:8],
                   lambda: par_sb[:, POFF["b_ada"] + part * 8:POFF["b_ada"] + part * 8 + 8], ALU.add, m, t_par)
            bank[b] = [a]
            return a, m

        for k in range(KC):
            _, add = square(lambda k=k: X[:, k, :], t_x[k // 4], q=pool)
            st_tok = add(7, "o1024", k == 0, k == KC - 1)
        RB1 = lambda: SZ[1][:, :]
        tok = None
        for k in range(KC):
            tok = mod_step(1, k, tok)
        t_sc, m = mod_end(1, tok, 0)
        tok = m
        for k in range(KC):
            tok = mod_step(0, k, tok)
        a, t_rb = root(RB1, 7, st_tok)
        t_g1 = ts(dve, lambda: sm[:, 8:16], lambda: sm[:, 8:16], 1.0, None, ALU.add, None, t_sc)
        t_gs = tt(dve, lambda: sm[:, 8:16], lambda: sm[:, 8:16],
                  lambda: par_sb[:, POFF["norm_g"]:POFF["norm_g"] + 8], ALU.mult, t_g1, t_par)
        t_sh, _ = mod_end(0, tok, 1)
        for k in range(KC):
            i, t, lw = tmps.take()
            a = stt(lambda t=t: t[:, :], lambda k=k: X[:, k, :], lambda k=k: sm[:, 8 + k:9 + k], RB1,
                    ALU.mult, ALU.mult, lw, t_gs, t_rb)
            hi = a_fn(lambda k=k: HH[:, k, :], lambda t=t: t[:, :], ACT.Identity, a, t_sh,
                      bias=lambda k=k: sm[:, k:k + 1])
            lo = stt(lambda k=k: HL[:, k, :], lambda t=t: t[:, :], lambda k=k: sm[:, k:k + 1],
                     lambda k=k: HH[:, k, :].bitcast(F32), ALU.add, ALU.subtract, hi)
            tmps.give(i, lo)
            h_tok[k] = (hi, lo)
        x_read = h_tok[KC - 1][1]

        def vproj(name, dh, dl, wfree, scale=None, stok=None):
            toks = []
            for u in range(4):
                s, ta, tb, j = use((name, u))
                for t in range(4):
                    if u == 0:
                        pe.wait(bank[2 + t])
                    for kk in range(2):
                        k = 2 * u + kk
                        o = lambda t=t: PS[2 + t][:, :]
                        wh = lambda s=s, kk=kk: WH[s][:, kk * T:(kk + 1) * T]
                        wl = lambda s=s, kk=kk: WL[s][:, kk * T:(kk + 1) * T]
                        hh = lambda k=k, t=t: HH[:, k, t * 128:(t + 1) * 128]
                        hl = lambda k=k, t=t: HL[:, k, t * 128:(t + 1) * 128]
                        mm(o, hh, wh, k == 0, False, ta, h_tok[k][0])
                        mm(o, hh, wl, False, False, tb)
                        tok = mm(o, hl, wh, False, k == KC - 1, h_tok[k][1], sig=kk == 1)
                    if u == 3:
                        a, b = split_ps(lambda t=t: dh[:, t, :], lambda t=t: dl[:, t, :],
                                        lambda t=t: PS[2 + t][:, :], tok, wfree, stok,
                                        scale=None if scale is None else scale(t))
                        bank[2 + t] = [a, b]
                        toks.append((a, b))
                used(j, tok)
            return toks

        q_tok, k_tok, z_tok = {}, {}, {}
        q_free, z_free = [None, None], [x_read, x_read]
        zf = {}

        def q_steps(br, c):
            p = c % 2
            qc = Chunk((br + "q", c), 0, *h_r, rtok=lambda k: h_tok[k])
            kc = Chunk((br + "k", c), 1, *h_r, rtok=lambda k: h_tok[k])
            zc = Chunk((br + "z", c), 0, *h_r, rtok=lambda k: h_tok[k])

            def fin_q():
                m = qc.half(1)
                q_tok[c] = split_ps(lambda: Qh[p][:, :], lambda: Ql[p][:, :], lambda: PS[0][:, :], m, q_free[p])
                bank[0] = list(q_tok[c])

            def fin_k():
                m = kc.half(1)
                k_tok[c] = split_ps(lambda: Kh[p][:, :], lambda: Kl[p][:, :], lambda: PS[1][:, :], m, q_free[p])
                bank[1] = list(k_tok[c])

            def fin_z():
                m = zc.half(1)
                z_tok[c] = a_fn(lambda: SZ[p][:, :], lambda: PS[0][:, :], ACT.Silu, m, z_free[p])
                bank[0] = [z_tok[c]]

            return [lambda: qc.half(0), fin_q, lambda: kc.half(0), fin_k, lambda: zc.half(0), fin_z]

        OFF = [0, 512, 896, 1152]

        def run(steps, n):
            for _ in range(n):
                if steps:
                    steps.pop(0)()

        y_part = {}

        def gate_y(h, m, dh, dl, wfree):
            c, r = h // 2, 64 * (h % 2)
            z = lambda: SZ[c % 2][r:r + 64, :]
            b = 6 + h % 2
            a = tt(dve, z, lambda: PS[b][r:r + 64, :], z, ALU.mult, m, z_tok[c])
            bank[b] = [a]
            if h % 2 == 0:
                y_part["a"] = a
                return None
            hi, lo = split_sb(lambda: dh[:, c, :], lambda: dl[:, c, :], lambda: SZ[c % 2][:, :], a, y_part["a"],
                              wfree)
            z_free[c % 2] = lo
            return hi, lo

        va = vproj("av", VAh, VAl, None)
        for f in q_steps("a", 0):
            f()
        ew_free = [None]
        sp_free = [x_read]
        sp_tok, ew_tok = {}, {}

        def qk_a(h):
            c, r, p = h // 2, 64 * (h % 2), (h // 2) % 2
            later = []
            for i in (3, 2, 1, 0):
                b, n = 2 + i, T - 128 * i
                o = lambda b=b, n=n: PS[b][:, 0:n]
                lh = lambda i=i: Kh[p][r:r + 64, i * 128:(i + 1) * 128]
                ll = lambda i=i: Kl[p][r:r + 64, i * 128:(i + 1) * 128]
                rh = lambda i=i: Qh[p][r:r + 64, i * 128:T]
                rl = lambda i=i: Ql[p][r:r + 64, i * 128:T]
                mm3(o, lh, ll, rh, rl, True, False, wh=[k_tok[c], q_tok[c], bank[b]] and
                    [list(k_tok[c]), list(q_tok[c]), bank[b]])
                m = mask(b, 0, r, "s")
                o2 = OFF[i]
                if i != 1:
                    pair = (tmps.take(), tmps.take())
                    if i == 3:
                        pair3 = pair
                (k1, t1, w1), (k2, t2, w2) = pair3 if i == 1 else pair
                c0 = 128 if i == 1 else 0
                s1 = lambda t1=t1, n=n, c0=c0: t1[:, c0:c0 + n]
                s2 = lambda t2=t2, n=n, c0=c0: t2[:, c0:c0 + n]
                x4 = ts(dve, s2, o, 0.125, 0.0, ALU.mult, ALU.max, m, w2)
                x1 = stt(s1, s2, -16.0, o, ALU.mult, ALU.add, x4, w1)
                x2 = a_fn(s1, s1, ACT.Exp, x1, scale=0.125)
                bank[b] = [x1, x4]
                later.append((i, n, o2, s1, s2, x2, x4, k1, k2))
            for i, n, o2, s1, s2, x2, x4, k1, k2 in later:
                x3 = a_fn(s1, s1, ACT.Ln, x2, bias=1.0)
                x5 = tt(dve, s2, s2, s1, ALU.add, x3, x4)
                hi, lo = split_sb(lambda o2=o2, n=n: SPh[:, o2:o2 + n], lambda o2=o2, n=n: SPl[:, o2:o2 + n],
                                  s2, x5, sp_free[0])
                tmps.give(k1, x5)
                tmps.give(k2, lo)
                sp_tok[i] = (hi, lo)
            q_free[p] = m

        def mid_a(h):
            for i in (3, 2, 1, 0):
                b, n = 2 + i, T - 128 * i
                for j in range(3, i - 1, -1):
                    nj = T - 128 * j
                    o = lambda b=b, i=i, j=j, n=n: PS[b][:, 128 * (j - i):n]
                    w = lambda i=i, j=j: con_r("tri8" if i == j else "m8")
                    mm(o, w, lambda j=j, nj=nj: SPh[:, OFF[j]:OFF[j] + nj], False, False, sp_tok[j][0], bank[b],
                       t_conr, skip=True)
                    m = mm(o, w, lambda j=j, nj=nj: SPl[:, OFF[j]:OFF[j] + nj], False, j == i, sp_tok[j][1],
                           skip=True, sig=j == i)
                k1, t1, w1 = tmps.take()
                s1 = lambda t1=t1, n=n: t1[:, 0:n]
                x = a_fn(s1, lambda b=b, n=n: PS[b][:, 0:n], ACT.Exp, m, w1, scale=0.125)
                hi, lo = split_sb(lambda i=i, n=n: EWh[:, OFF[i]:OFF[i] + n],
                                  lambda i=i, n=n: EWl[:, OFF[i]:OFF[i] + n], s1, x, ew_free[0])
                tmps.give(k1, lo)
                ew_tok[i] = (hi, lo)
                bank[b] = [x]
            sp_free[0] = m

        def pv_a(h):
            c = h // 2
            b = 6 + h % 2
            for j in range(4):
                nj = T - 128 * j
                o = lambda j=j: PS[b][:, 128 * j:T]
                lh = lambda j=j: VAh[:, j, c * 128:(c + 1) * 128]
                ll = lambda j=j: VAl[:, j, c * 128:(c + 1) * 128]
                rh = lambda j=j, nj=nj: EWh[:, OFF[j]:OFF[j] + nj]
                rl = lambda j=j, nj=nj: EWl[:, OFF[j]:OFF[j] + nj]
                m = mm3(o, lh, ll, rh, rl, j == 0, j == 3, wh=[ew_tok[j][0], va[j][0], va[j][1], bank[b]],
                        wl=[ew_tok[j][1]], sig=j == 3)
            ew_free[0] = m
            return m

        ya_tok = {}
        qk_a(0)
        steps = []
        f_tok = {}

        def f_steps():
            fc = Chunk(("f", 0), 1, *h_r, rtok=lambda k: h_tok[k])

            def fin():
                m = fc.half(1)
                k1, t1, w1 = tmps.take()
                k2, t2, w2 = tmps.take()
                s1 = lambda: t1[0:8, :]
                s2 = lambda: t2[0:8, :]
                x0 = ts(dve, s2, lambda: PS[1][0:8, :], lambda: pcol("b_forget", 0, 8), None, ALU.add, None,
                        m, w2, t_par)
                bank[1] = [x0]
                x1 = a_fn(s1, s2, ACT.Abs, x0, w1)
                x2 = a_fn(s1, s1, ACT.Exp, x1, scale=-1.0)
                x3 = a_fn(s1, s1, ACT.Ln, x2, bias=1.0)
                x4 = ts(dve, s2, s2, 0.0, None, ALU.min, None, x1)
                x5 = tt(dve, s2, s2, s1, ALU.subtract, x3, x4)
                for n in range(4):
                    m = pe(lambda e, n=n: e.transpose(PS[1][:, 8 * n:8 * n + 8], t2[0:8, 128 * n:128 * n + 128],
                                                      con_raw[0:8, 0:8]), x5, bank[1], t_con)
                x6 = cp(dve, lambda: t1[:, 0:32], lambda: PS[1][:, 0:32], m, x5)
                bank[1] = [x6]
                for n in range(4):
                    for b in range(n + 1):
                        m = mm(lambda n=n: PS[1][0:8, 128 * n:128 * n + 128], lambda b=b: t1[:, 8 * b:8 * b + 8],
                               lambda b=b, n=n: con_f("triu" if b == n else "one"), b == 0, b == n, x6, sig=True)
                x7 = ts(dve, s2, lambda: PS[1][0:8, :], -8.0, None, ALU.mult, None, m)
                x8 = cp(dve, lambda: FT[0:8, :], s2, x7, t_fz)
                x9 = tt(dve, s1, s2, lambda: FT[0:8, :].bitcast(F32), ALU.subtract, x8, m)
                x10 = cp(dve, lambda: FT[32:40, :], s1, x9)
                cp(dve, lambda: FT[64:72, :], lambda: FT[0:8, :].bitcast(F32), x8)
                x10 = cp(dve, lambda: FT[96:104, :], lambda: FT[32:40, :].bitcast(F32), x10)
                tmps.give(k1, x10)
                tmps.give(k2, x9)
                bank[1] = [x7]
                f_tok[0] = x10

            return [lambda: fc.half(0), fin]

        t_fz = pool(lambda e: e.memset(FT[:, :].bitcast(F32), 0.0))
        for h in range(8):
            c = h // 2
            if h % 2 == 0:
                steps += q_steps("a", c + 1) if c < 3 else (q_steps("b", 0)[0:4] + f_steps())
            mid_a(h)
            run(steps, 1)
            if h < 7:
                if h % 2 == 1:
                    run(steps, max(0, len(steps) - 2))
                qk_a(h + 1)
            m = pv_a(h)
            t = gate_y(h, m, YAh, YAl, None)
            if t:
                ya_tok[c] = t
            run(steps, 2 if h % 2 == 0 else 9)

        pv_done = m
        vb = vproj("bv", VBh, VBl, None)
        for f in q_steps("b", 0)[4:]:
            f()
        pt_free = [pv_done]

        def softmax_tile(b, n, scale, t, w, tw):
            k = softmax_tile.n % 8
            softmax_tile.n += 1
            cm, cb, cs, cr = (4 * k + x for x in range(4))
            col = lambda x: (lambda: stat[:, x:x + 1])
            x1 = dve(lambda e: e.tensor_reduce(col(cm)(), PS[b][:, 0:n], AX_X, ALU.max, negate=True), w, tw)
            x2 = ts(dve, col(cb), col(cm), scale, None, ALU.mult, None, x1)
            x3 = a_fn(lambda: t[:, 0:n], lambda: PS[b][:, 0:n], ACT.Exp, x2, tw, scale=scale, bias=col(cb),
                      accum=col(cs))
            return x3, (col(cs), col(cr))
        softmax_tile.n = 0

        def softmax_sum(x3, cols):
            cs, cr = cols
            return dve(lambda e: e.reciprocal(cr(), cs()), x3), cr

        pt_tok, pt2 = {}, {}

        def turn(b, nj, t, dh, dl, ready, wfree):
            for j in range(nj):
                m = pe(lambda e, j=j: e.transpose(PS[b][:, 128 * j:128 * j + 128], t[:, 128 * j:128 * j + 128],
                                                  con_f("ident")), ready, t_con, bank[b])
            src = lambda: PS[b][:, 0:128 * nj].rearrange("p (j t) -> p j t", j=nj)
            a, l = split_ps(dh, dl, src, m, wfree)
            bank[b] = [a, l]
            return m, a, l

        def sel(h):
            r = 64 * (h % 2)
            return conr[r:r + 40, CO + h:CO + h + 1].to_broadcast([40, 128])

        def qk_b(h):
            c, r, p = h // 2, 64 * (h % 2), (h // 2) % 2
            later = []
            for i in range(4):
                b, n = 2 + i, 128 * (i + 1)
                o = lambda b=b, n=n: PS[b][:, 0:n]
                lh = lambda i=i: Qh[p][r:r + 64, i * 128:(i + 1) * 128]
                ll = lambda i=i: Ql[p][r:r + 64, i * 128:(i + 1) * 128]
                mm3(o, lh, ll, lambda n=n: Kh[p][r:r + 64, 0:n], lambda n=n: Kl[p][r:r + 64, 0:n], True, False,
                    wh=[list(k_tok[c]), list(q_tok[c]), bank[b]])
                mm(o, lambda: sel(h), lambda n=n: FT[r:r + 40, 0:n], False, False, f_tok[0], t_conr)
                m = mask(b, 128 * i, r, "f")
                k1, t1, w1 = tmps.take()
                x3, cols = softmax_tile(b, n, 0.125, t1, m, w1)
                later.append((i, n, k1, t1, x3, cols))
            for i, n, k1, t1, x3, cols in later:
                x4, rc = softmax_sum(x3, cols)
                x5 = ts(dve, lambda t1=t1, n=n: t1[:, 0:n], lambda t1=t1, n=n: t1[:, 0:n], rc, None, ALU.mult,
                        None, x4)
                pt_tok[i] = (k1, t1, x3, x5)
            q_free[p] = m

        def mid_b(h):
            for i in range(4):
                k1, t1, x3, x5 = pt_tok[i]
                m, a, l = turn(2 + i, i + 1, t1, lambda i=i: PTh[:, 0:i + 1, 128 * i:128 * i + 128],
                               lambda i=i: PTl[:, 0:i + 1, 128 * i:128 * i + 128], [x5, x3], pt_free[0])
                tmps.give(k1, m)
                pt2[i] = (a, l)

        def pv_b(h):
            c = h // 2
            b = 6 + h % 2
            for j in range(4):
                o = lambda j=j: PS[b][:, 128 * j:T]
                lh = lambda j=j: VBh[:, j, c * 128:(c + 1) * 128]
                ll = lambda j=j: VBl[:, j, c * 128:(c + 1) * 128]
                w = [[list(pt2[i]) for i in range(4)], list(vb[j]), bank[b]]
                m = mm3(o, lh, ll, lambda j=j: PTh[:, j, 128 * j:T], lambda j=j: PTl[:, j, 128 * j:T],
                        j == 0, j == 3, wh=w, sig=j == 3)
            pt_free[0] = m
            return m

        yb_tok = {}
        gate_tok = pv_done
        qk_b(0)
        steps = []
        for h in range(8):
            c = h // 2
            if h % 2 == 0:
                steps += q_steps("b", c + 1) if c < 3 else []
            mid_b(h)
            run(steps, 1)
            if h < 7:
                if h % 2 == 1:
                    run(steps, max(0, len(steps) - 2))
                qk_b(h + 1)
            m = pv_b(h)
            t = gate_y(h, m, VAh, VAl, pv_done)
            if t:
                yb_tok[c] = t
            run(steps, 2 if h % 2 == 0 else 9)
            gate_tok = mod_step(2, h, gate_tok)
        pv_done = m
        t_gate, _ = mod_end(2, gate_tok, 0)

        t_xr = None
        if not plan_only:
            t_xr = sp.dma(l_x2, lambda e: e.dma_start(X[:, :, :], xin), pv_done)

        def half_unit(name, b0, rh, rl, rtok, n=T):
            s, ta, tb, j = use(name)
            toks = []
            for g in range(2):
                pe.wait(bank[b0 + g])
                for k in range(4):
                    lh = lambda k=k, g=g, s=s: WH[s][:, k * 256 + g * 128:k * 256 + g * 128 + 128]
                    ll = lambda k=k, g=g, s=s: WL[s][:, k * 256 + g * 128:k * 256 + g * 128 + 128]
                    o = lambda g=g: PS[b0 + g][:, :]
                    tok = mm3(o, lh, ll, lambda k=k: rh(k), lambda k=k: rl(k), k == 0, k == 3,
                              wh=[ta, rtok(k)[0]], wl=[tb, rtok(k)[1]], sig=k == 3)
                toks.append(tok)
            used(j, tok)
            return toks

        mg_tok = {}

        def mgh(k):
            return VBh[:, k, :] if k < 4 else MG2h[:, k - 4, :]

        def mgl(k):
            return VBl[:, k, :] if k < 4 else MG2l[:, k - 4, :]

        for u in range(4):
            ta = half_unit(("oa", u), 0, lambda k: YAh[:, k, :], lambda k: YAl[:, k, :], lambda k: ya_tok[k])
            tb = half_unit(("ob", u), 2, lambda k: VAh[:, k, :], lambda k: VAl[:, k, :], lambda k: yb_tok[k])
            for g in range(2):
                f = 2 * u + g
                ms = []
                for x in range(2):
                    b = 4 + 2 * g + x
                    tok = hproj(("g", 8 * x + f), b).both()
                    h_read[0] = tok
                    k1, t1, w1 = tmps.take()
                    sg = a_fn(lambda t1=t1: t1[:, :], lambda b=b: PS[b][:, :], ACT.Sigmoid, tok, w1, t_par,
                              bias=lambda x=x, f=f: pcol("b_gate", 8 * x + f))
                    bank[b] = [sg]
                    yb_, ty = (g, ta[g]) if x == 0 else (2 + g, tb[g])
                    pr = tt(dve, lambda t1=t1: t1[:, :], lambda t1=t1: t1[:, :], lambda yb_=yb_: PS[yb_][:, :],
                            ALU.mult, sg, ty)
                    bank[yb_] = [pr]
                    ms.append((k1, t1, pr))
                (k1, t1, p1), (k2, t2, p2) = ms
                s_ = tt(dve, lambda t1=t1: t1[:, :], lambda t1=t1: t1[:, :], lambda t2=t2: t2[:, :], ALU.add,
                        p1, p2)
                hi, lo = split_sb(lambda f=f: mgh(f), lambda f=f: mgl(f), lambda t1=t1: t1[:, :], s_, pv_done,
                                  lo=pool)
                tmps.give(k1, hi, lo)
                tmps.give(k2, s_)
                mg_tok[f] = (hi, lo)

        x_rd = [None] * KC
        x_tok = [None] * KC

        def residual(f, b, tok, gname, gate=None, wx=None, both=False):
            if gate is None:
                x = tt(dve, lambda: X[:, f, :], lambda: PS[b][:, :], lambda: X[:, f, :], ALU.add, tok, wx,
                       x_rd[f])
            else:
                x = stt(lambda: X[:, f, :], lambda: PS[b][:, :], gate, lambda: X[:, f, :], ALU.mult, ALU.add,
                        tok, wx)
            bank[b] = [x]
            if gname:
                g = (lambda: sm[:, 40 + f:41 + f]) if both else (lambda: pcol(gname, f))
                hi = a_fn(lambda: HH[:, f, :], lambda: X[:, f, :], ACT.Copy, x, h_read[0], scale=g)
                lo = stt(lambda: HL[:, f, :], lambda: X[:, f, :], g, lambda: HH[:, f, :].bitcast(F32),
                         ALU.mult, ALU.subtract, hi)
                h_tok[f] = (hi, lo)
            sq, add = square(lambda: X[:, f, :], x)
            x_rd[f] = [sq, hi] if gname else [sq]
            x_tok[f] = x
            if both:
                sq2, add2 = square(lambda: X[:, f, :], x, scale=lambda: pcol("final_g", f))
                x_rd[f].append(sq2)

                def adds(b_, ones, first, last):
                    add(b_, ones, first, last)
                    return add2(6, ones, first, last)
                return adds
            return add

        def out_proj(name, rh, rl, rtok, gname, gate=None, wx=None, both=False, ks=None, lead=0):
            add = None
            chunks = [Chunk((name, f), f % (4 if lead else 2), rh, rl, rtok=rtok, ks=ks) for f in range(KC)]
            for f in range(lead):
                chunks[f].half(0)
            for f in range(KC):
                b = f % (4 if lead else 2)
                tok = chunks[f].half(1) if f < lead else chunks[f].both()
                if add:
                    add(7, "o1024", f == 1, False)
                add = residual(f, b, tok, gname, gate=(lambda f=f: gate(f)) if gate else None, wx=wx,
                               both=both)
            warm(ACT.Sqrt)
            return add(7, "o1024", False, True)

        mg_read = (pe, pe.n)
        kp, tp, wp = tmps.take()
        ka, tag, wa = tmps.take()
        kk_, tk, wk = tmps.take()
        kl, tl, wl_ = tmps.take()
        if plan_only:
            t_pos = t_lam = None
        else:
            t_pos = sp.dma(l_pos, lambda e: e.dma_start(tp[:, :].bitcast(I32), posin), wp)
            t_lam = sp.dma(l_lam, lambda e: e.dma_start(tl[:, 0:256], lamin), wl_)
        C1 = 6.28125
        C2 = float(np.float32(np.round((2 * np.pi - C1) * 2 ** 20) / 2 ** 20))
        C3 = float(2 * np.pi - C1 - C2)
        MAGIC = 12582912.0
        ang, kr, pv_ = lambda: tag[:, :], lambda: tk[:, :], lambda: tp[:, :]
        x0 = cp(dve, ang, lambda: tp[:, :].bitcast(I32), t_pos, wa)
        x1 = ts(dve, ang, ang, lambda: con_raw[:, CO + 8:CO + 9], None, ALU.mult, None, x0, t_con)
        x2 = ts(dve, kr, ang, float(1 / (2 * np.pi)), MAGIC, ALU.mult, ALU.add, x1, wk)
        x3 = ts(dve, kr, kr, MAGIC, None, ALU.subtract, None, x2)
        x4 = stt(ang, kr, -C1, ang, ALU.mult, ALU.add, x3)
        x5 = stt(ang, kr, -C2, ang, ALU.mult, ALU.add, x4)
        x6 = stt(ang, kr, -C3, ang, ALU.mult, ALU.add, x5)
        x7 = ts(dve, ang, ang, -3.1415925, 3.1415925, ALU.max, ALU.min, x6)
        x8 = a_fn(lambda: STb[:, :], ang, ACT.Sin, x7, mg_read)
        x9 = a_fn(kr, ang, ACT.Abs, x7)
        x10 = ts(dve, kr, kr, -1.0, float(np.pi / 2), ALU.mult, ALU.add, x9)
        x11 = a_fn(lambda: CT[:, :], kr, ACT.Sin, x10, mg_read)
        tmps.give(kp, x0)
        tmps.give(ka, x8, x9)
        tmps.give(kk_, x11)
        x0 = tt(dve, lambda: tl[:, 256:320], lambda: tl[:, 0:64], lambda: tl[:, 64:128], ALU.mult, t_lam)
        x1 = tt(dve, lambda: tl[:, 320:384], lambda: tl[:, 128:192], lambda: tl[:, 192:256], ALU.mult, t_lam)
        x2 = dve(lambda e: e.tensor_reduce(sm[:, 26:28], tl[:, 256:384].rearrange("p (a b) -> p a b", a=2), AX_X,
                                           ALU.add), x0, x1)
        x3 = a_fn(lambda: sm[:, 28:30], lambda: sm[:, 26:28], ACT.Exp, x2)
        x4 = tt(dve, lambda: sm[:, 30:31], lambda: sm[:, 29:30], lambda: sm[:, 28:29], ALU.subtract, x3)
        t_nl = ts(dve, lambda: sm[:, 24:25], lambda: sm[:, 30:31], -LAM_INIT, None, ALU.add, None, x4)
        t_sg = ts(dve, lambda: sm[:, 25:26], lambda: pcol("subln_g_2"), 1.0 - LAM_INIT, None, ALU.mult, None, t_par)
        tmps.give(kl, x2)

        t_fm = tt(dve, lambda: sm[:, 40:48], lambda: par_sb[:, POFF["final_g"]:POFF["final_g"] + 8],
                  lambda: par_sb[:, POFF["norm_mix_g_2"]:POFF["norm_mix_g_2"] + 8], ALU.mult, t_par)
        st_tok = out_proj("wo", mgh, mgl, lambda k: mg_tok[k], "norm_mix_g_2",
                          gate=lambda f: sm[:, 16 + f:17 + f], wx=[t_xr, t_gate, t_fm], both=True)
        rb = lambda: RB[:, :]
        r1 = lambda: YF[:, 0, :]
        x1, c1_ = root_cols(7, st_tok)
        x2_, c2_ = root_cols(6, st_tok, raw=True)
        rc2 = lambda: sm[:, 64:68]
        x2 = tt(dve, rc2, c1_, c1_, ALU.mult, x1)
        x2 = tt(dve, rc2, rc2, c2_, ALU.mult, x2, x2_)
        x3 = a_fn(rc2, rc2, ACT.Sqrt, x2, bias=eps)
        x3 = dve(lambda e: e.reciprocal(rc2(), rc2()), x3)
        t_rc = tt(dve, rc2, rc2, c1_, ALU.mult, x3)
        m = spread(7, rc2, t_rc)
        t_rb = cp(dve, rb, lambda: PS[7][:, :], m)
        bank[7] = [t_rb]
        m = spread(6, c1_, x1)
        t_r1 = cp(dve, r1, lambda: PS[6][:, :], m)
        bank[6] = [t_r1]
        for f in range(KC):
            xf = lambda f=f: X[:, f, :]
            x_new = stt(xf, xf, lambda f=f: pcol("final_g", f), r1, ALU.mult, ALU.mult, t_r1, x_rd[f])
        free1 = st_tok

        t_c2 = tt(dve, lambda: CT[:, :], lambda: CT[:, :], rb, ALU.mult, x11, t_rb)
        t_s2 = tt(dve, lambda: STb[:, :], lambda: STb[:, :], rb, ALU.mult, x8, t_rb)
        t_pad = pool(lambda e: e.memset(CP[:, :, 0:30], 0.0), free1)
        cp_tok = {}
        for j in range(4):
            b0, b1 = ((0, 1), (2, 3), (4, 5), (0, 1))[j]
            ua = hproj(("u", j), b0).both()
            k1, t1, w1 = tmps.take()
            xa = tt(dve, lambda t1=t1: t1[:, :], lambda b0=b0: PS[b0][:, :], rb, ALU.mult, ua, w1, t_rb)
            bank[b0] = [xa]
            ub = hproj(("u", 4 + j), b1).both()
            k2, t2, w2 = tmps.take()
            xb = tt(dve, lambda t2=t2: t2[:, :], lambda b1=b1: PS[b1][:, :], rb, ALU.mult, ub, w2, t_rb)
            bank[b1] = [xb]
            xc = a_fn(lambda t2=t2: t2[:, :], lambda t2=t2: t2[:, :], ACT.Sigmoid, xb)
            xd = tt(dve, lambda j=j: CP[:, j, 30:30 + T], lambda t1=t1: t1[:, :], lambda t2=t2: t2[:, :],
                    ALU.mult, xa, xc, free1)
            tmps.give(k1, xd)
            tmps.give(k2, xd)
            cp_tok[j] = xd
        conv_last = {}
        cv_free_ = [sq_free[1], sq_free[1]]
        conv_steps = []

        def tap(j, x):
            w = lambda: pcol("cv_dw_w_2", 4 * x + j)
            o = lambda: AC[:, j, :]
            i = lambda: CP[:, j, x:x + T]
            if x == 0:
                conv_last[j] = ts(dve, o, i, w, lambda: pcol("cv_dw_b_2", j), ALU.mult, ALU.add, cp_tok[j], t_pad,
                                  free1, t_par)
            else:
                if j < 2:
                    conv_last[j] = stt(o, i, w, o, ALU.mult, ALU.add, conv_last[j])
                else:
                    v = j - 2
                    a = a_fn(lambda: CV[v][:, :], i, ACT.Copy, cv_free_[v], cp_tok[j], t_pad, scale=w)
                    conv_last[j] = tt(pool, o, o, lambda: CV[v][:, :], ALU.add, a, conv_last[j])
                    cv_free_[v] = conv_last[j]

        for j0 in (0, 1):
            for x in range(31):
                for j in (j0, j0 + 2):
                    conv_steps.append(lambda j=j, x=x: tap(j, x))

        v2 = vproj("dv", V2h, V2l, free1, scale=lambda t: (lambda: sm[:, 64 + t:65 + t]), stok=t_rc)
        dq_tok, dk_tok = {}, {}
        dq_free = [free1, free1]
        rt_free = [free1]

        def d_steps(h):
            p = h % 2
            out_ = []
            for b, nm, dh, dl, dt in ((0, "dq", DQh, DQl, dq_tok), (1, "dk", DKh, DKl, dk_tok)):
                ch = Chunk((nm, h), b, *h_r, rtok=lambda k: h_tok[k])

                def second(b=b, ch=ch, dh=dh, dl=dl, dt=dt):
                    m = ch.half(1)
                    ps = lambda: PS[b][:, :]
                    hi, lo = split_ps(lambda: RTh[:, :], lambda: RTl[:, :], ps, m, rt_free[0])
                    k1, t1, w1 = tmps.take()
                    x1 = tt(dve, lambda: t1[:, :], ps, lambda: CT[:, :], ALU.mult, m, w1, t_c2)
                    mm(ps, lambda: con_r("rot"), lambda: RTh[:, :], True, False, hi, lo, x1, t_conr)
                    m2 = mm(ps, lambda: con_r("rot"), lambda: RTl[:, :], False, True, lo, sig=True)
                    rt_free[0] = m2
                    k2, t2, w2 = tmps.take()
                    x2 = tt(dve, lambda: t2[:, :], ps, lambda: STb[:, :], ALU.mult, m2, w2, t_s2)
                    bank[b] = [x2]
                    x3 = tt(dve, lambda: t2[:, :], lambda: t2[:, :], lambda: t1[:, :], ALU.add, x2, x1)
                    dt[h] = split_sb(lambda: dh[p][:, :], lambda: dl[p][:, :], lambda: t2[:, :], x3, dq_free[p])
                    tmps.give(k1, x3)
                    tmps.give(k2, dt[h][1])

                out_ += [lambda ch=ch: ch.half(0), second]
            return out_

        at_tok = {}
        at_free = [free1]
        yf_tok = {}

        def qk_d(n_):
            h, i = n_ // 4, n_ % 4
            p, n = h % 2, 128 * (i + 1)
            got = []
            for c in range(2):
                b = 2 + 2 * (n_ % 2) + c
                r = 64 * c
                o = lambda b=b: PS[b][:, 0:n]
                mm3(o, lambda r=r: DQh[p][r:r + 64, 128 * i:128 * i + 128],
                    lambda r=r: DQl[p][r:r + 64, 128 * i:128 * i + 128],
                    lambda r=r: DKh[p][r:r + 64, 0:n], lambda r=r: DKl[p][r:r + 64, 0:n], True, False,
                    wh=[list(dq_tok[h]), list(dk_tok[h]), bank[b]])
                m = mask(b, 128 * i, r, "f")
                k1, t1, w1 = tmps.take()
                x3, cols = softmax_tile(b, n, 0.125, t1, m, w1)
                got.append((k1, t1, x3, cols))
                bank[b] = [x3]
                run(conv_steps, 2)
            at_tok[n_] = got
            if i == 3:
                dq_free[p] = m

        def join_d(n_):
            n = 128 * (n_ % 4 + 1)
            (k1, t1, e1, s1), (k2, t2, e2, s2) = at_tok[n_]
            r1, c1 = softmax_sum(e1, s1)
            r2, c2 = softmax_sum(e2, s2)
            n1 = lambda: t1[:, 0:n]
            n2 = lambda: t2[:, 0:n]
            x5 = a_fn(n1, n1, ACT.Copy, e1, r1, scale=c1)
            x6 = ts(dve, c2, c2, lambda: sm[:, 24:25], None, ALU.mult, None, r2, t_nl)
            x7 = stt(n2, n2, c2, n1, ALU.mult, ALU.add, x6, x5, e2)
            tmps.give(k1, x7)
            at_tok[n_] = (k2, t2, x7)

        def turn_d(n_):
            i = n_ % 4
            k2, t2, x7 = at_tok[n_]
            o = 128 * (i % 2)
            m, a, l = turn(6, i + 1, t2, lambda: ATh[:, 0:i + 1, o:o + 128], lambda: ATl[:, 0:i + 1, o:o + 128],
                           [x7], at_free[0])
            tmps.give(k2, m)
            at_tok[n_] = (a, l)

        def pv_d(s):
            h, half = s // 2, s % 2
            b = 7
            js = 2 * half + 2
            for j in range(js):
                o0 = max(0, 128 * j - 256 * half)
                o = lambda o0=o0: PS[b][:, o0:256]
                w = [list(at_tok[2 * s + 1]), list(at_tok[2 * s]), list(v2[j]), bank[b]]
                m = mm3(o, lambda j=j: V2h[:, j, h * 128:(h + 1) * 128], lambda j=j: V2l[:, j, h * 128:(h + 1) * 128],
                        lambda j=j, o0=o0: ATh[:, j, o0:256], lambda j=j, o0=o0: ATl[:, j, o0:256],
                        j == 0, j == js - 1, wh=w, sig=j == js - 1)
            at_free[0] = m
            x = a_fn(lambda: YF[:, h, 256 * half:256 * half + 256], lambda: PS[b][:, 0:256], ACT.Copy, m, x_new, t_rb)
            bank[b] = [x]
            yf_tok[s] = x
            return m

        yc_tok = {}
        ln = {}

        def ln_mean(j):
            hi, lo = split_sb(lambda: SQh[0][:, :], lambda: SQl[0][:, :], lambda: AC[:, j, :],
                              conv_last[j], sq_free[0])
            mm(lambda: PS[0][:, :], lambda: con_r("o512"), lambda: SQh[0][:, :], j == 0, False, hi,
               bank[0] if j == 0 else None)
            ln["m"] = sq_free[0] = mm(lambda: PS[0][:, :], lambda: con_r("o512"), lambda: SQl[0][:, :], False, j == 3,
                                      lo, sig=True)

        def ln_diff(j):
            ln[j] = tt(dve, lambda: AC[:, j, :], lambda: PS[0][:, :], lambda: AC[:, j, :], ALU.subtract, ln["m"])
            bank[0] = [ln[j]]
            sq_n[0] = 0
            _, add = square(lambda: AC[:, j, :], ln[j])
            ln["v"] = add(1, "o512", j == 0, j == 3)

        def ln_root():
            r_, c_ = root_cols(1, ln["v"])
            ln["s"] = spread(1, c_, r_)

        def ln_out(j):
            k1, t1, w1 = late_t.take()
            s1 = lambda: t1[:, :]
            x1 = stt(s1, lambda: AC[:, j, :], -1.0, lambda: PS[1][:, :], ALU.mult, ALU.mult, ln["s"], ln[j], w1)
            x2 = a_fn(s1, s1, ACT.Silu, x1, t_par, scale=lambda: pcol("cv_ln_g_2", j),
                      bias=lambda: pcol("cv_ln_b_2", j))
            yc_tok[j] = split_sb(lambda: YCh[:, j, :], lambda: YCl[:, j, :], s1, x2, [conv_last[x] for x in range(4)],
                                 lo=pool)
            bank[1] = [x1]
            late_t.give(k1, *yc_tok[j])

        yd_tok = {}
        sub = {}

        def sub_sum(h, b):
            sq_n[0] = 0
            _, add = square(lambda: YF[:, h, :], yf_tok[2 * h], yf_tok[2 * h + 1])
            sub[h] = root_cols(b, add(b, "o128", True, True))

        def sub_out(h, b):
            r_, c_ = sub[h]
            m = spread(b, c_, r_)
            k1, t1, w1 = late_t.take()
            s1 = lambda: t1[:, :]
            x1 = stt(s1, lambda: YF[:, h, :], lambda: sm[:, 25:26], lambda: PS[b][:, :], ALU.mult, ALU.mult, m,
                     t_sg, w1)
            bank[b] = [x1]
            yd_tok[h] = split_sb(lambda: YDh[:, h, :], lambda: YDl[:, h, :], s1, x1, dq_free[0], lo=pool)
            late_t.give(k1, *yd_tok[h])

        for f in d_steps(0):
            f()
            run(conv_steps, 6)
        steps = d_steps(1)
        qk_d(0)
        run(steps, 2)
        qk_d(1)
        join_d(0)
        late = [lambda: ln_mean(0), lambda: ln_mean(1), lambda: ln_mean(2), lambda: ln_mean(3),
                lambda: ln_diff(0), lambda: ln_diff(1), lambda: ln_diff(2), lambda: ln_diff(3),
                ln_root, lambda: ln_out(0), lambda: ln_out(1), lambda: ln_out(2), lambda: ln_out(3),
                lambda: sub_sum(0, 0), lambda: sub_sum(1, 1), lambda: sub_out(0, 0), lambda: sub_out(1, 1),
                lambda: sub_sum(2, 0), lambda: sub_out(2, 0)]
        for n in range(16):
            h = n // 4
            if n % 4 == 2 and h < 2:
                steps = d_steps(h + 2)
            run(steps, 1)
            run(conv_steps, 3)
            if n < 14:
                qk_d(n + 2)
            if n > 0 and n % 2 == 0:
                pv_d(n // 2 - 1)
            turn_d(n)
            run(conv_steps, 3)
            if n < 15:
                join_d(n + 1)
            if n == 15:
                m = pv_d(7)
            if n == 10:
                run(conv_steps, 999)
                sq_free[1] = [sq_free[1], *cv_free_]
                scr[0] = late_t
                late_t.last = [rt_free[0], rt_free[0]]
            if n > 10:
                run(late, 4)
        sub_late = [lambda: sub_sum(3, 4), lambda: sub_out(3, 4)]
        att_done = m
        for f in sub_late:
            f()
        run(late, 99)
        scr[0] = tmps
        h_read[0] = (pe, pe.n)
        st_tok = out_proj("wo2", lambda k: YDh[:, k, :] if k < 4 else YCh[:, k - 4, :],
                          lambda k: YDl[:, k, :] if k < 4 else YCl[:, k - 4, :],
                          lambda k: yd_tok[k] if k < 4 else yc_tok[k - 4], "norm_cross_g_2",
                          ks=(4, 5, 6, 7, 0, 1, 2, 3), lead=4)
        a, t_rb = root(rb, 7, st_tok)
        free2 = st_tok

        mem_tok = {}
        t_mem = None
        if not plan_only:
            t_mem = sp.dma(l_mem, lambda e: e.dma_start(MEMT[:, :, :], memin), free2)
        for k in range(KC):
            _, add = square(lambda k=k: MEMT[:, k, :], t_mem, n=M)
            s_ = add(6, "o1024", k == 0, k == KC - 1)
        a, r_ = root(lambda: MRB[:, :], 6, s_, n=M)
        m_tok = [None] * KC
        for k in range(KC):
            k1, t1, w1 = tmps.take()
            s1 = lambda t1=t1: t1[:, 0:M]
            x1 = stt(s1, lambda k=k: MEMT[:, k, :], lambda k=k: pcol("norm_mem_g_2", k), lambda: MRB[:, :],
                     ALU.mult, ALU.mult, r_, w1)
            m_tok[k] = split_sb(lambda k=k: MTh[:, k, :], lambda k=k: MTl[:, k, :], s1, x1, free2)
            tmps.give(k1, m_tok[k][1])
        mem_read = x1

        cq_tok, ck_tok, cv_tok = {}, {}, {}
        ck_free = [free2, free2]
        cv_free = [free2, free2]
        m_r = (lambda k: MTh[:, k, :], lambda k: MTl[:, k, :])

        def c_steps(h):
            p = h % 2
            out_ = []
            for g in range(2):
                f = 2 * h + g
                ch = Chunk(("ck", f), g, *m_r, rtok=lambda k: m_tok[k], n=M)

                def fin(f=f, g=g, ch=ch):
                    m = ch.half(1)
                    ck_tok[f] = split_ps(lambda: CKh[p][:, g, :], lambda: CKl[p][:, g, :],
                                         lambda: PS[g][:, 0:M], m, ck_free[p])
                    bank[g] = list(ck_tok[f])
                out_ += [lambda ch=ch: ch.half(0), fin]

            def vals():
                for u in range(2):
                    s, ta, tb, j = use(("cv", h, u))
                    for mt in range(2):
                        if u == 0:
                            pe.wait(bank[mt])
                        for kk in range(4):
                            k = 4 * u + kk
                            o = lambda mt=mt: PS[mt][:, 0:256]
                            lh = lambda k=k, mt=mt: MTh[:, k, mt * 128:(mt + 1) * 128]
                            ll = lambda k=k, mt=mt: MTl[:, k, mt * 128:(mt + 1) * 128]
                            rh = lambda s=s, kk=kk: WH[s][:, kk * 256:(kk + 1) * 256]
                            rl = lambda s=s, kk=kk: WL[s][:, kk * 256:(kk + 1) * 256]
                            mm(o, lh, rh, k == 0, False, ta, list(m_tok[k]))
                            mm(o, lh, rl, False, False, tb)
                            tok = mm(o, ll, rh, False, k == 7, sig=kk == 3)
                        if u == 1:
                            cv_tok[h, mt] = split_ps(lambda mt=mt: CVh[p][:, mt, :], lambda mt=mt: CVl[p][:, mt, :],
                                                     lambda mt=mt: PS[mt][:, 0:256], tok, cv_free[p])
                            bank[mt] = list(cv_tok[h, mt])
                    used(j, tok)
            out_.append(vals)
            for g in range(2):
                f = 2 * h + g
                ch = hproj(("cq", f), g)

                def fin(f=f, g=g, ch=ch):
                    m = ch.half(1)
                    k1, t1, w1 = tmps.take()
                    x = tt(dve, lambda: t1[:, :], lambda: PS[g][:, :], rb, ALU.mult, m, t_rb, w1)
                    bank[g] = [x]
                    cq_tok[f] = split_sb(lambda: Oh[:, f, :], lambda: Ol[:, f, :], lambda: t1[:, :], x, free2,
                                         mem_read)
                    tmps.give(k1, cq_tok[f][1])
                out_ += [lambda ch=ch: ch.half(0), fin]
            return out_

        cp_free = [free2]
        ct_tok, ct2 = {}, {}

        def qk_c(h):
            p = h % 2
            later = []
            for i in range(4):
                b = 2 + i
                for g in range(2):
                    f = 2 * h + g
                    m = mm3(lambda b=b: PS[b][:, 0:M], lambda f=f, i=i: Oh[:, f, 128 * i:128 * i + 128],
                            lambda f=f, i=i: Ol[:, f, 128 * i:128 * i + 128],
                            lambda g=g: CKh[p][:, g, :], lambda g=g: CKl[p][:, g, :], g == 0, g == 1,
                            wh=[list(cq_tok[f]), list(ck_tok[f]), bank[b]], sig=g == 1)
                k1, t1, w1 = tmps.take()
                x3, cols = softmax_tile(b, M, 1.0 / 16, t1, m, w1)
                bank[b] = [x3]
                later.append((i, k1, t1, x3, cols))
            for i, k1, t1, x3, cols in later:
                x4, rc = softmax_sum(x3, cols)
                x5 = ts(dve, lambda t1=t1: t1[:, 0:M], lambda t1=t1: t1[:, 0:M], rc, None, ALU.mult, None, x4, x3)
                ct_tok[i] = (k1, t1, x5)
            ck_free[p] = m
            qk_c.last = m

        def mid_c(h):
            for i in range(4):
                k1, t1, x5 = ct_tok[i]
                m, a, l = turn(2 + i, 2, t1, lambda i=i: CPh[:, :, 128 * i:128 * i + 128],
                               lambda i=i: CPl[:, :, 128 * i:128 * i + 128], [x5], cp_free[0])
                tmps.give(k1, m)
                ct2[i] = (a, l)

        o_tok = {}

        def pv_c(h, q_done):
            p = h % 2
            for g in range(2):
                f, b = 2 * h + g, 6 + g
                for mt in range(2):
                    m = mm3(lambda b=b: PS[b][:, :], lambda mt=mt, g=g: CVh[p][:, mt, 128 * g:128 * g + 128],
                            lambda mt=mt, g=g: CVl[p][:, mt, 128 * g:128 * g + 128],
                            lambda mt=mt: CPh[:, mt, :], lambda mt=mt: CPl[:, mt, :], mt == 0, mt == 1,
                            wh=[[list(ct2[i]) for i in range(4)], list(cv_tok[h, mt]), bank[b]], sig=mt == 1)
                o_tok[f] = split_ps(lambda f=f: Oh[:, f, :], lambda f=f: Ol[:, f, :], lambda b=b: PS[b][:, :], m,
                                    q_done)
                bank[b] = list(o_tok[f])
            cp_free[0] = m
            cv_free[p] = m

        for f in c_steps(0):
            f()
        qk_c(0)
        steps = []
        for h in range(4):
            if h < 3:
                steps += c_steps(h + 1)
            run(steps, 3)
            q_done = qk_c.last
            mid_c(h)
            run(steps, 3)
            if h < 3:
                run(steps, 99)
                qk_c(h + 1)
            pv_c(h, q_done)
        h_read[0] = (pe, pe.n)
        st_tok = out_proj("co", lambda k: Oh[:, k, :], lambda k: Ol[:, k, :], lambda k: o_tok[k], "norm_ffn_g_2")
        a, t_rb = root(rb, 7, st_tok)
        free3 = st_tok

        cb_tok = [pool(lambda e, i=i: e.memset(CB[i][:, 0:2], 0.0), free3) for i in range(4)]
        cb_n = [0]
        cb_free = [None] * 4
        z_tok, z_free = {}, {}

        def conv3(f, b):
            tok = hproj(("up", f), b).both()
            q = cb_n[0] % 4
            cb_n[0] += 1
            x1 = tt(dve, lambda: CB[q][:, 2:2 + T], lambda: PS[b][:, :], rb, ALU.mult, tok, t_rb, cb_free[q], free3)
            bank[b] = [x1]
            k1, t1, w1 = tmps.take()
            s1 = lambda: t1[:, :]
            x2 = a_fn(s1, lambda: CB[q][:, 2:2 + T], ACT.Copy, x1, w1, scale=lambda: pcol("ffn_dw_w_2", 88 + f))
            x3 = stt(s1, lambda: CB[q][:, 1:1 + T], lambda: pcol("ffn_dw_w_2", 44 + f), s1, ALU.mult, ALU.add, x2,
                     cb_tok[q])
            x4 = stt(s1, lambda: CB[q][:, 0:T], lambda: pcol("ffn_dw_w_2", f), s1, ALU.mult, ALU.add, x3)
            cb_free[q] = x4
            return k1, t1, x4

        def up(n):
            s = n % NZ
            k1, t1, x1 = conv3(n, 2 * (n % 2))
            g = a_fn(lambda: t1[:, :], lambda: t1[:, :], ACT.Silu, x1)
            k2, t2, x2 = conv3(22 + n, 2 * (n % 2) + 1)
            z = tt(dve, lambda: t2[:, :], lambda: t2[:, :], lambda: t1[:, :], ALU.mult, g, x2)
            z_tok[n] = split_sb(lambda: ZH[:, s, :], lambda: ZL[:, s, :], lambda: t2[:, :], z, z_free.get(s), free3,
                                lo=pool)
            tmps.give(k1, z)
            tmps.give(k2, *z_tok[n])

        def down(g, last):
            add = None
            nk = min(8, 22 - 8 * g)
            for f in range(KC):
                b = 4 + f % 2
                zz = [(8 * g + k) % NZ for k in range(nk)]
                tok = Chunk(("down", g, f), b, lambda k: ZH[:, zz[k], :], lambda k: ZL[:, zz[k], :], nk=nk,
                            rtok=lambda k: z_tok[8 * g + k]).both()
                if last:
                    if add:
                        add(7, "o1024", f == 1, False)
                    add = residual(f, b, tok, None)
                else:
                    xf = lambda f=f: X[:, f, :]
                    x = tt(dve, xf, lambda b=b: PS[b][:, :], xf, ALU.add, tok, x_rd[f])
                    bank[b] = [x]
                    x_rd[f] = [x]
            for s in zz:
                z_free[s] = tok
            return add(7, "o1024", False, True) if last else None

        for n in range(9):
            up(n)
        down(0, False)
        for n in range(9, 17):
            up(n)
        down(1, False)
        for n in range(17, 22):
            up(n)
        st_tok = down(2, True)
        a, t_rb = root(rb, 7, st_tok)
        for f in range(KC):
            x = stt(lambda f=f: X[:, f, :], lambda f=f: X[:, f, :], lambda f=f: pcol("norm_final_g_2", f), rb,
                    ALU.mult, ALU.mult, t_rb, x_rd[f])
            if not plan_only:
                t_out = sp.dma(l_out, lambda e, f=f: e.dma_start(out[f * 128:(f + 1) * 128, :], X[:, f, :]), x)
        if plan_only:
            return names
        sp.wait(t_out)
        assert state["use"] == len(order) and state["dma"] == len(order), state

        for q in (pe, act, dve, pool, sp):
            q.sem = st.enter_context(nc.semaphore("s_" + q.name))
        for l in lines:
            l.sem = st.enter_context(nc.semaphore(l.name))
        with nc.Block() as block:
            block.tensor(lambda e: pe.emit(e))
            block.scalar(lambda e: act.emit(e))
            block.vector(lambda e: dve.emit(e))
            block.gpsimd(lambda e: pool.emit(e))
            block.sync(lambda e: sp.emit(e))
    return names


def pack_units(order, w):
    def cols(a, c0, n=128, k0=0, nk=8):
        blk = a[128 * k0:128 * (k0 + nk), c0:c0 + n]
        if blk.shape[1] < n:
            blk = np.concatenate([blk, np.zeros((blk.shape[0], n - blk.shape[1]), blk.dtype)], axis=1)
        return blk.reshape(nk, 128, n).transpose(1, 0, 2).reshape(128, nk * n)

    win, wada, wsb, wfox, wout = w["w_in"][0], w["w_ada"][0], w["w_o_sb"][0], w["w_o_fox"][0], w["w_out"][0]
    win2, wout2, wcq, wckv, wco = w["w_in_2"][0], w["w_out_2"][0], w["w_cq_2"][0], w["w_ckv_2"][0], w["w_co_2"][0]
    wup, wdown = w["w_up_2"][0], w["w_down_2"][0]
    res = np.zeros((len(order), 128, U), np.float32)
    for n, u in enumerate(order):
        k = u[0]
        if k == "ada":
            b = wada[128 * u[2]:128 * u[2] + 128, 1024 * u[1]:1024 * u[1] + 1024]
        elif k in ("aq", "ak", "az", "bq", "bk", "bz"):
            o = {"aq": 0, "ak": 512, "az": 1536, "bq": 2048, "bk": 2560, "bz": 3584}[k]
            b = cols(win, o + 128 * u[1])
        elif k in ("av", "bv"):
            b = cols(win, 1024 if k == "av" else 3072, 512, 2 * u[1], 2)
        elif k == "f":
            b = cols(win[:, 4096:4104], 0)
        elif k == "g":
            b = cols(win, 4104 + 128 * u[1])
        elif k in ("oa", "ob"):
            b = cols(wsb if k == "oa" else wfox, 256 * u[1], 256, 0, 4)
        elif k == "wo":
            b = cols(wout, 128 * u[1])
        elif k == "u":
            b = cols(win2, 1536 + 128 * u[1])
        elif k == "dq":
            b = cols(win2, 128 * u[1])
        elif k == "dk":
            b = cols(win2, 512 + 128 * u[1])
        elif k == "dv":
            b = cols(win2, 1024, 512, 2 * u[1], 2)
        elif k == "wo2":
            b = cols(wout2, 128 * u[1])
        elif k == "cq":
            b = cols(wcq, 128 * u[1])
        elif k == "ck":
            b = cols(wckv, 128 * u[1])
        elif k == "cv":
            b = cols(wckv, 1024 + 256 * u[1], 256, 4 * u[2], 4)
        elif k == "co":
            b = cols(wco, 128 * u[1])
        elif k == "up":
            b = cols(wup, 128 * u[1])
        elif k == "down":
            b = cols(wdown, 128 * u[2], 128, 8 * u[1], min(8, 22 - 8 * u[1]))
        res[n, :, 0:b.shape[1]] = b
    return res


def pack_params(w):
    res = np.zeros((128, NPAR), np.float32)
    for name, n in PARAMS:
        a = np.asarray(w[name])
        o = POFF[name]
        if name == "b_forget":
            res[0:8, o] = a.reshape(8)
        elif name == "cv_dw_w_2":
            res[:, o:o + n] = a.reshape(31, 4, 128).transpose(2, 0, 1).reshape(128, n)
        elif name == "ffn_dw_w_2":
            res[:, o:o + n] = a.reshape(3, 44, 128).transpose(2, 0, 1).reshape(128, n)
        else:
            res[:, o:o + n] = a.reshape(n, 128).T
    return res


def kernel(**inputs):
    import concourse.bacc as bacc
    from concourse.bass_utils import run_bass_kernel_spmd

    w = {k: np.asarray(v) for k, v in inputs.items()}
    order = build(None, None)
    arrays = {
        "units": pack_units(order, w),
        "par": pack_params(w),
        "con": constants(),
        "msk": masks(),
        "xin": np.ascontiguousarray(w["x"][0].T.reshape(KC, 128, T).transpose(1, 0, 2)),
        "memin": np.ascontiguousarray(w["mem_2"][0].T.reshape(KC, 128, M).transpose(1, 0, 2)),
        "posin": np.ascontiguousarray(np.broadcast_to(w["positions_2"][0], (128, T))),
        "lamin": np.ascontiguousarray(np.broadcast_to(np.concatenate(
            [w[n][0] for n in ("lam_q1_2", "lam_k1_2", "lam_q2_2", "lam_k2_2")]), (128, 256))),
    }
    nc = bacc.Bacc("TRN2", target_bir_lowering=False, num_devices=1)
    args = [nc.dram_tensor(n, a.shape, mybir.dt.from_np(a.dtype), kind="ExternalInput").ap()
            for n, a in arrays.items()]
    args.append(nc.dram_tensor("out", (D, T), F32, kind="ExternalOutput").ap())
    build(nc, args, order)
    r = run_bass_kernel_spmd(nc, [arrays], core_ids=[0])
    return np.ascontiguousarray(r.results[0]["out"].T).reshape(1, T, D)
```

```python
from contextlib import ExitStack

import numpy as np

import concourse.bass as bass
from concourse import mybir

F32 = mybir.dt.float32
F32R = mybir.dt.float32r
BF16 = mybir.dt.bfloat16
I32 = mybir.dt.int32
ALU = mybir.AluOpType
ACT = mybir.ActivationFunctionType
AX_X = mybir.AxisListType.X

P = 128
T = 512
D = 1024
KC = 8
M = 256
EPS = 1e-6
NEG = -1e30
LAM_INIT = 0.2
U = 1024

PARAMS = [("norm_g", 8), ("b_ada", 24), ("b_gate", 16), ("norm_mix_g_2", 8), ("norm_cross_g_2", 8),
          ("norm_mem_g_2", 8), ("norm_ffn_g_2", 8), ("norm_final_g_2", 8), ("final_g", 8), ("subln_g_2", 1),
          ("cv_dw_b_2", 4), ("cv_ln_g_2", 4), ("cv_ln_b_2", 4), ("c", 8), ("cv_dw_w_2", 124),
          ("ffn_dw_w_2", 132), ("b_forget", 1)]
POFF = {}
_o = 0
for _n, _w in PARAMS:
    POFF[_n] = _o
    _o += _w
NPAR = _o

CONSTS = ["ident", "tri8", "m8", "o1024", "o128", "o512", "rot", "triu", "one"]
NCON = len(CONSTS) * 128 + 16


def constants():
    i = np.arange(128)
    c = {
        "ident": np.eye(128),
        "tri8": np.where(i[:, None] >= i[None, :], -8.0, 0.0),
        "m8": np.full((128, 128), -8.0),
        "o1024": np.full((128, 128), 2.0 ** -10),
        "o128": np.full((128, 128), 2.0 ** -7),
        "o512": np.full((128, 128), 2.0 ** -9),
        "triu": np.where(i[:, None] <= i[None, :], 1.0, 0.0),
        "one": np.ones((128, 128)),
    }
    rot = np.zeros((128, 128))
    for g in (0, 64):
        for j in range(8):
            rot[g + 8 + j, g + j] = -1.0
            rot[g + j, g + 8 + j] = 1.0
    c["rot"] = rot
    out = np.zeros((128, NCON), np.float32)
    for n, name in enumerate(CONSTS):
        out[:, n * 128:(n + 1) * 128] = c[name]
    o = len(CONSTS) * 128
    for h in range(8):
        out[h, o + h] = 1.0
        out[32 + h, o + h] = 1.0
        out[64 + h, o + h] = 1.0
        out[96 + h, o + h] = 1.0
    inv = np.power(np.float32(500000.0), -(np.arange(0, 16, 2, dtype=np.float32) / np.float32(16)))
    for g in (0, 64):
        out[g:g + 8, o + 8] = inv
        out[g + 8:g + 16, o + 8] = inv
    out[:, o + 9] = EPS
    return out


def masks():
    k = np.arange(128) % 64
    i = np.arange(128)
    out = np.zeros((128, 1024), np.float32)
    for g in range(2):
        row = (k + 64 * g)[:, None]
        out[:, g * 128:g * 128 + 128] = row == i[None, :]
        out[:, 256 + g * 128:384 + g * 128] = np.where(row >= i[None, :], NEG, 0.0)
        out[:, 512 + g * 128:640 + g * 128] = np.where(i[None, :] > row, NEG, 0.0)
    return out


class Queue:

    def __init__(self, name):
        self.name, self.n, self.items, self.seen, self.sem = name, 0, [], {}, None

    def __call__(self, f, *waits, sig=True):
        self.wait(*waits)
        self.items.append((f, self if sig else None, 1))
        if sig:
            self.n += 1
        return (self, self.n)

    def wait(self, *waits):
        for w in waits:
            if w is None:
                continue
            if isinstance(w, list):
                self.wait(*w)
                continue
            src, n = w
            if self.seen.get(src.name, 0) < n:
                self.seen[src.name] = n
                self.items.append((None, src, n))

    def dma(self, line, f, *waits):
        self.wait(*waits)
        line.n += 16
        self.items.append((f, line, 16))
        return (line, line.n)

    def emit(self, eng):
        for f, src, n in self.items:
            if f is None:
                eng.wait_ge(src.sem, n)
            else:
                ins = f(eng)
                if src is not None:
                    ins.then_inc(src.sem, n)


class Line:

    def __init__(self, name):
        self.name, self.n, self.sem = name, 0, None


class Temps:

    def __init__(self, tiles):
        self.tiles, self.i, self.last, self.held = tiles, 0, [None] * len(tiles), set()

    def take(self):
        k = self.i % len(self.tiles)
        self.i += 1
        assert k not in self.held
        self.held.add(k)
        return k, self.tiles[k], self.last[k]

    def give(self, k, *tokens):
        self.last[k] = list(tokens)
        self.held.discard(k)


def build(nc, args, order=None):
    names = []
    plan_only = order is None
    raw_n = 4
    spl_n = 4
    if not plan_only:
        units, gate_w, par, con, msk, xin, memin, posin, lamin, out = args
    st = ExitStack()

    off = [16512]

    def at(name, shape, dt, offset=None):
        if plan_only:
            return None
        nb = int(np.prod(shape[1:])) * (2 if dt == BF16 else 4)
        if offset is None:
            offset = off[0]
            off[0] += (nb + 31) // 32 * 32
        assert offset + nb <= 229344, (name, offset + nb)
        return nc.alloc_sbuf_tensor_at(name, list(shape), dt, offset=offset)

    with st:
        RAW = [at(f"raw{i}", [P, U], F32) for i in range(raw_n)]
        WH = [at(f"wh{i}", [P, U], F32R) for i in range(spl_n)]
        WL = [at(f"wl{i}", [P, U], F32R) for i in range(spl_n)]
        HH = at("hh", [P, KC, T], F32R)
        HL = at("hl", [P, KC, T], F32R)
        n_tmp = 7
        TM = [at(f"tm{i}", [P, T], F32) for i in range(n_tmp)]
        con_raw = at("con_raw", [P, NCON], F32)
        conr = at("conr", [P, NCON], F32R)
        MK = at("mk", [P, 768], BF16)
        par_sb = at("par_sb", [P, NPAR], F32)
        sm = at("sm", [P, 96], F32)
        stat = at("stat", [P, 64], F32)
        nrm = at("nrm", [P, 96], F32)
        sq0 = off[0]
        CV = [at(f"cvt{i}", [P, T], F32, sq0 + 2048 + 4096 * i) for i in range(2)]
        SQh = [at(f"sqh{i}", [P, T], F32R) for i in range(2)]
        SQl = [at(f"sql{i}", [P, T], F32R) for i in range(2)]
        base = off[0]
        X = at("x", [P, KC, T], F32)
        a1 = off[0]
        off[0] = base
        SPh = at("sph", [P, 1280], F32R)
        SPl = at("spl", [P, 1280], F32R)
        EWh = at("ewh", [P, 1280], F32R)
        EWl = at("ewl", [P, 1280], F32R)
        PTh = at("pth", [P, 4, T], F32R, base)
        PTl = at("ptl", [P, 4, T], F32R, base + 8192)
        VAh = at("vah", [P, 4, T], F32R)
        VAl = at("val", [P, 4, T], F32R)
        VBh = at("vbh", [P, 4, T], F32R)
        VBl = at("vbl", [P, 4, T], F32R)
        MKR = at("mkr", [P, 1024], F32, off[0])
        YAh = at("yah", [P, 4, T], F32R)
        YAl = at("yal", [P, 4, T], F32R)
        qk0 = off[0]
        Qh = [at(f"qh{i}", [P, T], F32R) for i in range(2)]
        Ql = [at(f"ql{i}", [P, T], F32R) for i in range(2)]
        Kh = [at(f"kh{i}", [P, T], F32R) for i in range(2)]
        Kl = [at(f"kl{i}", [P, T], F32R) for i in range(2)]
        MG2h = at("mg2h", [P, 4, T], F32R, qk0)
        MG2l = at("mg2l", [P, 4, T], F32R, qk0 + 8192)
        SZ = [at(f"sz{i}", [P, T], F32) for i in range(2)]
        FT = at("ft", [104, T], F32R)
        MA = at("ma", [P, U], F32, a1)
        MA2 = at("ma2", [P, U], F32, a1 + 4096)
        off[0] = a1
        RB = at("rb", [P, T], F32)
        b2 = off[0]
        CT = at("ct", [P, T], F32)
        STb = at("stb", [P, T], F32)
        cp0 = off[0]
        CP = at("cp", [P, 4, T + 30], F32)
        ac0 = off[0]
        AC = at("ac", [P, 4, T], F32)
        v20 = off[0]
        V2h = at("v2h", [P, 4, T], F32R)
        V2l = at("v2l", [P, 4, T], F32R)
        dq0 = off[0]
        DQh, DQl, DKh, DKl = ([None] * 2 for _ in range(4))
        for i in range(2):
            DQh[i], DQl[i] = at(f"dqh{i}", [P, T], F32R), at(f"dql{i}", [P, T], F32R)
            DKh[i], DKl[i] = at(f"dkh{i}", [P, T], F32R), at(f"dkl{i}", [P, T], F32R)
        yf0 = off[0]
        YF = at("yf", [P, 4, T], F32)
        ATh = at("ath", [P, 4, 256], F32R)
        ATl = at("atl", [P, 4, 256], F32R)
        RT = [at(f"rt{i}", [P, T], F32, off[0] + 2048 * i) for i in range(2)]
        RTh = at("rth", [P, T], F32R)
        RTl = at("rtl", [P, T], F32R)
        YDh = at("ydh", [P, 4, T], F32R, dq0)
        YDl = at("ydl", [P, 4, T], F32R, yf0)
        YCh = at("ych", [P, 4, T], F32R, cp0)
        YCl = at("ycl", [P, 4, T], F32R, ac0)
        off[0] = b2
        Oh = at("oh", [P, KC, T], F32R)
        CPh = at("cph", [P, 2, T], F32R)
        Ol = at("ol", [P, KC, T], F32R, dq0)
        MTh = at("mth", [P, KC, M], F32R, v20)
        MTl = at("mtl", [P, KC, M], F32R, v20 + 8192)
        off[0] = yf0
        CKh = [at(f"ckh{i}", [P, 2, M], F32R) for i in range(2)]
        CKl = [at(f"ckl{i}", [P, 2, M], F32R) for i in range(2)]
        MEMT = at("memt", [P, KC, M], F32, off[0])
        CVh = [at(f"cvh{i}", [P, 2, M], F32R) for i in range(2)]
        CVl = [at(f"cvl{i}", [P, 2, M], F32R) for i in range(2)]
        CPl = at("cpl", [P, 2, T], F32R)
        MRB = at("mrb", [P, M], F32)
        off[0] = b2
        NZ = 10
        ZH = at("zh", [P, NZ, T], F32R)
        ZL = at("zl", [P, NZ, T], F32R)
        CB = [at(f"cb{i}", [P, T + 2], F32) for i in range(4)]

        if not plan_only:
            PS = [nc.alloc_psum_tensor(f"ps{i}", [P, T], F32) for i in range(8)]

        pe, act, dve, pool, sp = (Queue(n) for n in ("pe", "act", "dve", "pool", "sp"))
        l_raw = [Line(f"l_raw{i}") for i in range(raw_n)]
        l_msk, l_x, l_xb, l_x2, l_g0, l_g1, l_mem, l_con, l_par, l_pos, l_lam, l_out = (
            Line(n) for n in ("l_msk", "l_x", "l_xb", "l_x2", "l_g0", "l_g1", "l_mem", "l_con", "l_par", "l_pos", "l_lam", "l_out"))
        lines = l_raw + [l_msk, l_x, l_xb, l_x2, l_g0, l_g1, l_mem, l_con, l_par, l_pos, l_lam, l_out]

        def con_f(name, w=128):
            o = CONSTS.index(name) * 128
            return con_raw[:, o:o + w]

        def con_r(name):
            o = CONSTS.index(name) * 128
            return conr[:, o:o + 128]

        CO = len(CONSTS) * 128

        def pcol(name, j=0, rows=P):
            return par_sb[0:rows, POFF[name] + j:POFF[name] + j + 1]

        def a_fn(o, i, func, *w, scale=1.0, bias=None, accum=None):
            def f(e):
                k = {} if accum is None else {"accum_out": accum()}
                k["scale"] = scale() if callable(scale) else scale
                if bias is not None:
                    k["bias"] = bias() if callable(bias) else bias
                return e.activation(o(), i(), func, **k)
            return act(f, *w)

        def tt(q, o, a, b, op, *w):
            return q(lambda e: e.tensor_tensor(o(), a(), b(), op), *w)

        def stt(o, a, s, b, op0, op1, *w):
            return dve(lambda e: e.scalar_tensor_tensor(
                o(), a(), s() if callable(s) else s, b(), op0, op1), *w)

        def ts(q, o, a, s1, s2, op0, op1, *w):
            def f(e):
                x1 = s1() if callable(s1) else s1
                x2 = s2() if callable(s2) else s2
                if op1 is None:
                    return e.tensor_scalar(o(), a(), x1, None, op0)
                return e.tensor_scalar(o(), a(), x1, x2, op0, op1)
            return q(f, *w)

        def cp(q, o, i, *w):
            return q(lambda e: e.tensor_copy(o(), i()), *w)

        def as32(f):
            return lambda: f().bitcast(F32)

        def split_ps(h, l, src, *w, scale=None):
            if scale is None:
                a = a_fn(h, src, ACT.Copy, *w)
                b = tt(dve, l, src, as32(h), ALU.subtract, a, *w)
            else:
                a = a_fn(h, src, ACT.Copy, *w, scale=scale)
                b = stt(l, src, scale, as32(h), ALU.mult, ALU.subtract, a, *w)
            return a, b

        def split_sb(h, l, src, *w, lo=None):
            a = cp(dve, h, src, *w)
            b = tt(lo or dve, l, src, as32(h), ALU.subtract, a, *w)
            return a, b

        state = {"dma": 0, "split": 0, "use": 0}
        raw_free = [None] * raw_n
        wh_ready = {}
        spl_free = {}
        raw_tok = {}

        def send(j):
            s = j % raw_n
            raw_tok[j] = sp.dma(l_raw[s], lambda e, s=s, j=j: e.dma_start(RAW[s][:, :], units[j]),
                                raw_free[s])

        slot_of = {}
        split_users = []

        read = set()

        def pump(j):
            read.add(j)
            while state["dma"] < len(order) and state["dma"] - raw_n in read:
                send(state["dma"])
                state["dma"] += 1

        def ahead():
            while state["split"] < len(order):
                j = state["split"]
                if order[j][0] == "ada":
                    state["split"] += 1
                    continue
                if len(split_users) >= spl_n and split_users[-spl_n] not in spl_free:
                    break
                if j > state["use"] + spl_n - 1:
                    break
                if j >= state["dma"]:
                    break
                s = len(split_users) % spl_n
                w = spl_free[split_users[-spl_n]] if len(split_users) >= spl_n else None
                r = j % raw_n
                a = act(lambda e, s=s, r=r: e.activation(WH[s][:, :], RAW[r][:, :], ACT.Copy), raw_tok[j], w)
                b = pool(lambda e, s=s, r=r: e.tensor_tensor(WL[s][:, :], RAW[r][:, :],
                                                             WH[s][:, :].bitcast(F32), ALU.subtract),
                         raw_tok[j], a, w)
                wh_ready[j] = (s, a, b)
                raw_free[r] = [a, b]
                split_users.append(j)
                state["split"] += 1
                pump(j)

        def use(name):
            if plan_only:
                names.append(name)
                return 0, None, None, len(names) - 1
            j = state["use"]
            assert order[j] == name, (order[j], name)
            ahead()
            assert j in wh_ready, (j, name, state)
            s, a, b = wh_ready[j]
            state["use"] += 1
            return s, a, b, j

        def used(j, tok):
            spl_free[j] = tok
            if not plan_only:
                ahead()

        def use_raw(name):
            if plan_only:
                names.append(name)
                return 0, None, 0
            j = state["use"]
            assert order[j] == name, (order[j], name)
            state["use"] += 1
            return j % raw_n, raw_tok[j], j

        def used_raw(j, tok):
            if plan_only:
                return
            raw_free[j % raw_n] = [tok]
            pump(j)
            ahead()

        def mm(o, l, r, start, stop, *w, sig=False, skip=False):
            return pe(lambda e: e.matmul(o(), l(), r(), start=start, stop=stop, skip_group_check=skip),
                      *w, sig=sig)

        def mm3(o, lh, ll, rh, rl, first, last, wh=(), wl=(), sig=False):
            mm(o, lh, rh, first, False, *wh)
            mm(o, lh, rl, False, False, *wl)
            return mm(o, ll, rh, False, last, sig=sig)

        bank = [None] * 8

        class Chunk:

            def __init__(self, name, b, rh, rl, n=T, nk=KC, rtok=None, ks=None):
                self.a = (name, b, rh, rl, n, nk, rtok, ks or tuple(range(nk)))

            def half(self, part):
                name, b, rh, rl, n, nk, rtok, order_k = self.a
                if part == 0:
                    self.u = use(name)
                    s, ta, tb, j = self.u
                    pe.wait(bank[b])
                s, ta, tb, j = self.u
                ks = order_k[:nk // 2] if part == 0 else order_k[nk // 2:]
                tok = None
                for k in ks:
                    lh = lambda k=k, s=s: WH[s][:, k * 128:(k + 1) * 128]
                    ll = lambda k=k, s=s: WL[s][:, k * 128:(k + 1) * 128]
                    rt = rtok(k) if rtok else (None, None)
                    o = lambda b=b, n=n: PS[b][:, 0:n]
                    mm(o, lh, lambda k=k: rh(k), k == order_k[0], False, ta, rt[0])
                    mm(o, lh, lambda k=k: rl(k), False, False, rt[1])
                    tok = mm(o, ll, lambda k=k: rh(k), False, k == order_k[-1], tb, sig=k == order_k[-1])
                if part == 1:
                    used(j, tok)
                    self.tok = tok
                return tok

            def both(self):
                self.half(0)
                return self.half(1)

        h_r = (lambda k: HH[:, k, :], lambda k: HL[:, k, :])
        h_tok = [(None, None)] * KC
        h_read = [None]

        def hproj(name, b, **kw):
            return Chunk(name, b, *h_r, rtok=lambda k: h_tok[k], **kw)

        if not plan_only:
            t_par = sp.dma(l_par, lambda e: e.dma_start(par_sb[:, :], par))
            t_x = [sp.dma(l_x, lambda e: e.dma_start(X[:, 0:4, :], xin[:, 0:4, :])), None]
            send(0)
            t_x[1] = sp.dma(l_xb, lambda e: e.dma_start(X[:, 4:8, :], xin[:, 4:8, :]))
            t_con = sp.dma(l_con, lambda e: e.dma_start(con_raw[:, :], con))
            for j in range(1, raw_n):
                send(j)
            t_msk = sp.dma(l_msk, lambda e: e.dma_start(MKR[:, :], msk))
            state["dma"] = raw_n
        else:
            t_con = t_par = t_msk = None
            t_x = [None, None]
        t_conr = cp(dve, lambda: conr[:, :], lambda: con_raw[:, :], t_con)
        tmps = Temps(TM)
        late_t = Temps(RT if not plan_only else [None] * 2)
        scr = [tmps]
        t_mk = []

        def mask(b, c0, r, which):
            o = lambda: PS[b][:, c0:c0 + 128]
            m0 = 256 if which == "s" else 512
            mm(o, lambda: MK[r:r + 64, 0:128], lambda: MK[r:r + 64, m0:m0 + 128], False, False, *t_mk)
            return mm(o, lambda: MK[r:r + 64, 128:256], lambda: MK[r:r + 64, m0 + 128:m0 + 256], False, True,
                      sig=True)

        def eps():
            return con_raw[:, CO + 9:CO + 10]

        sq_n = [0]
        sq_free = [None, None]

        def square(src, *w, n=T, scale=1.0, q=None):
            ring = scr[0]
            i, t, lw = ring.take()
            p = sq_n[0] % 2
            sq_n[0] += 1
            a = a_fn(lambda: t[:, 0:n], src, ACT.Square, lw, *w, scale=scale)
            if q is None:
                h = cp(dve, lambda: SQh[p][:, 0:n], lambda: t[:, 0:n], a, sq_free[p])
            else:
                h = a_fn(lambda: SQh[p][:, 0:n], lambda: t[:, 0:n], ACT.Copy, a, sq_free[p])
            l = tt(q or dve, lambda: SQl[p][:, 0:n], lambda: t[:, 0:n], lambda: SQh[p][:, 0:n].bitcast(F32),
                   ALU.subtract, h, sq_free[p])
            ring.give(i, l)

            def add(b, ones, first, last):
                out_ = lambda: PS[b][:, 0:n]
                mm(out_, lambda: con_r(ones), lambda: SQh[p][:, 0:n], first, False, h, t_conr,
                   bank[b] if first else None)
                tok = mm(out_, lambda: con_r(ones), lambda: SQl[p][:, 0:n], False, last, l, sig=True)
                sq_free[p] = tok
                return tok

            return a, add

        nrm_n = [0]

        def warm(func):
            a_fn(lambda: sm[:, 60:61], lambda: con_raw[:, 0:1], func, t_con, (act, act.n))

        def root_cols(b, *w, n=T, raw=False):
            k = 8 * (nrm_n[0] % 8)
            nrm_n[0] += 1
            m = n // 128
            ring = scr[0]
            i, t, lw = ring.take()
            v = lambda: t[:, 0:n].rearrange("p (m j) -> p m j", m=m)
            c = lambda: nrm[:, k:k + m]
            d = dve(lambda e: e.tensor_tensor(
                v(), PS[b][:, 0:n].rearrange("p (m j) -> p m j", m=m),
                con_f("ident").unsqueeze(1).to_broadcast([P, m, 128]), ALU.mult), lw, t_con, *w)
            bank[b] = [d]
            d = dve(lambda e: e.tensor_reduce(c(), v(), AX_X, ALU.add), d)
            ring.give(i, d)
            if raw:
                return d, c
            a = a_fn(c, c, ACT.Sqrt, d, bias=eps)
            return dve(lambda e: e.reciprocal(c(), c()), a), c

        def spread(b, cols, *w, n=T):
            ring = scr[0]
            i, t, lw = ring.take()
            m = n // 128
            d = dve(lambda e: e.tensor_tensor(
                t[:, 0:n].rearrange("p (m j) -> p m j", m=m),
                con_f("ident").unsqueeze(1).to_broadcast([P, m, 128]),
                cols()[:, 0:m].unsqueeze(2).to_broadcast([P, m, 128]), ALU.mult), lw, *w, t_con)
            tok = mm(lambda: PS[b][:, 0:n], lambda: con_f("one"), lambda: t[:, 0:n], True, True, d, bank[b], sig=True)
            ring.give(i, tok)
            return tok

        def root(dst, b, *w, n=T, ahead_=None):
            r, c = root_cols(b, *w, n=n)
            if ahead_:
                ahead_()
            m = spread(b, c, r, n=n)
            x = cp(dve, dst, lambda: PS[b][:, 0:n], m, *w)
            bank[b] = [x]
            return x, x

        def mod_step(part, k, tok, ma=MA):
            r, tr, j = use_raw(("ada", part, k))
            if k == 0:
                tok = ts(dve, lambda: ma[:, :], lambda: RAW[r][:, :], lambda: pcol("c", k), None,
                         ALU.mult, None, tr, t_par, tok)
            else:
                tok = stt(lambda: ma[:, :], lambda: RAW[r][:, :], lambda: pcol("c", k),
                          lambda: ma[:, :], ALU.mult, ALU.add, tr, tok)
            used_raw(j, tok)
            return tok

        def mod_end(part, tok, b, ma=MA):
            for f in range(8):
                m = mm(lambda f=f: PS[b][:, f:f + 1], lambda f=f: ma[:, f * 128:(f + 1) * 128],
                       lambda: con_f("one", 1), True, True, tok, t_con, bank[b], sig=True)
            a = tt(dve, lambda: sm[:, part * 8:part * 8 + 8], lambda: PS[b][:, 0:8],
                   lambda: par_sb[:, POFF["b_ada"] + part * 8:POFF["b_ada"] + part * 8 + 8], ALU.add, m, t_par)
            bank[b] = [a]
            return a, m

        for k in range(KC):
            _, add = square(lambda k=k: X[:, k, :], t_x[k // 4], q=pool)
            st_tok = add(7, "o1024", k == 0, k == KC - 1)
        RB1 = lambda: SZ[1][:, :]
        tok1 = tok = None
        for k in range(KC):
            tok1 = mod_step(1, k, tok1)
        for k in range(KC):
            tok = mod_step(0, k, tok, MA2)
            if k == 1:
                t_sc, _ = mod_end(1, tok1, 0)
                r_, c_ = root_cols(7, st_tok)
            if k == 3:
                m = spread(7, c_, r_)
            if k == 4:
                t_rb = cp(dve, RB1, lambda: PS[7][:, :], m)
                bank[7] = [t_rb]
        for c0, w in ((0, 512), (512, 256)):
            t_mk.append(cp(dve, lambda c0=c0, w=w: MK[:, c0:c0 + w], lambda c0=c0, w=w: MKR[:, c0:c0 + w], t_msk))
        t_g1 = ts(dve, lambda: sm[:, 8:16], lambda: sm[:, 8:16], 1.0, None, ALU.add, None, t_sc)
        t_gs = tt(dve, lambda: sm[:, 8:16], lambda: sm[:, 8:16],
                  lambda: par_sb[:, POFF["norm_g"]:POFF["norm_g"] + 8], ALU.mult, t_g1, t_par)
        t_sh, _ = mod_end(0, tok, 1, MA2)
        for k in range(KC):
            i, t, lw = tmps.take()
            a = stt(lambda t=t: t[:, :], lambda k=k: X[:, k, :], lambda k=k: sm[:, 8 + k:9 + k], RB1,
                    ALU.mult, ALU.mult, lw, t_gs, t_rb)
            hi = a_fn(lambda k=k: HH[:, k, :], lambda t=t: t[:, :], ACT.Identity, a, t_sh,
                      bias=lambda k=k: sm[:, k:k + 1])
            lo = stt(lambda k=k: HL[:, k, :], lambda t=t: t[:, :], lambda k=k: sm[:, k:k + 1],
                     lambda k=k: HH[:, k, :].bitcast(F32), ALU.add, ALU.subtract, hi)
            tmps.give(i, lo)
            h_tok[k] = (hi, lo)
        x_read = h_tok[KC - 1][1]

        def vproj(name, dh, dl, wfree, scale=None, stok=None, between=None):
            toks = []
            for u in range(4):
                s, ta, tb, j = use((name, u))
                for t in range(4):
                    if u == 0:
                        pe.wait(bank[2 + t])
                    for kk in range(2):
                        k = 2 * u + kk
                        o = lambda t=t: PS[2 + t][:, :]
                        wh = lambda s=s, kk=kk: WH[s][:, kk * T:(kk + 1) * T]
                        wl = lambda s=s, kk=kk: WL[s][:, kk * T:(kk + 1) * T]
                        hh = lambda k=k, t=t: HH[:, k, t * 128:(t + 1) * 128]
                        hl = lambda k=k, t=t: HL[:, k, t * 128:(t + 1) * 128]
                        mm(o, hh, wh, k == 0, False, ta, h_tok[k][0])
                        mm(o, hh, wl, False, False, tb)
                        tok = mm(o, hl, wh, False, k == KC - 1, h_tok[k][1], sig=kk == 1)
                    if u == 3:
                        a, b = split_ps(lambda t=t: dh[:, t, :], lambda t=t: dl[:, t, :],
                                        lambda t=t: PS[2 + t][:, :], tok, wfree, stok,
                                        scale=None if scale is None else scale(t))
                        bank[2 + t] = [a, b]
                        toks.append((a, b))
                used(j, tok)
                if between:
                    between()
            return toks

        q_tok, k_tok, z_tok = {}, {}, {}
        q_free, z_free = [None, None], [x_read, x_read]
        zf = {}

        def q_steps(br, c):
            p = c % 2
            qc = Chunk((br + "q", c), 0, *h_r, rtok=lambda k: h_tok[k])
            kc = Chunk((br + "k", c), 1, *h_r, rtok=lambda k: h_tok[k])
            zc = Chunk((br + "z", c), 0, *h_r, rtok=lambda k: h_tok[k])

            def fin_q():
                m = qc.half(1)
                q_tok[c] = split_ps(lambda: Qh[p][:, :], lambda: Ql[p][:, :], lambda: PS[0][:, :], m, q_free[p])
                bank[0] = list(q_tok[c])

            def fin_k():
                m = kc.half(1)
                k_tok[c] = split_ps(lambda: Kh[p][:, :], lambda: Kl[p][:, :], lambda: PS[1][:, :], m, q_free[p])
                bank[1] = list(k_tok[c])

            def fin_z():
                m = zc.half(1)
                z_tok[c] = a_fn(lambda: SZ[p][:, :], lambda: PS[0][:, :], ACT.Silu, m, z_free[p])
                bank[0] = [z_tok[c]]

            return [lambda: qc.half(0), fin_q, lambda: kc.half(0), fin_k, lambda: zc.half(0), fin_z]

        OFF = [0, 512, 896, 1152]

        def run(steps, n):
            for _ in range(n):
                if steps:
                    steps.pop(0)()

        y_part = {}

        def gate_y(h, m, dh, dl, wfree):
            c, r = h // 2, 64 * (h % 2)
            z = lambda: SZ[c % 2][r:r + 64, :]
            b = 6 + h % 2
            a = tt(dve, z, lambda: PS[b][r:r + 64, :], z, ALU.mult, m, z_tok[c])
            bank[b] = [a]
            if h % 2 == 0:
                y_part["a"] = a
                return None
            hi, lo = split_sb(lambda: dh[:, c, :], lambda: dl[:, c, :], lambda: SZ[c % 2][:, :], a, y_part["a"],
                              wfree)
            z_free[c % 2] = lo
            return hi, lo

        va = vproj("av", VAh, VAl, None)
        for f in q_steps("a", 0):
            f()
        ew_free = [None]
        sp_free = [x_read]
        sp_tok, ew_tok = {}, {}

        def qk_a(h):
            c, r, p = h // 2, 64 * (h % 2), (h // 2) % 2
            later = []
            for i in (3, 2, 1, 0):
                b, n = 2 + i, T - 128 * i
                o = lambda b=b, n=n: PS[b][:, 0:n]
                lh = lambda i=i: Kh[p][r:r + 64, i * 128:(i + 1) * 128]
                ll = lambda i=i: Kl[p][r:r + 64, i * 128:(i + 1) * 128]
                rh = lambda i=i: Qh[p][r:r + 64, i * 128:T]
                rl = lambda i=i: Ql[p][r:r + 64, i * 128:T]
                mm3(o, lh, ll, rh, rl, True, False, wh=[k_tok[c], q_tok[c], bank[b]] and
                    [list(k_tok[c]), list(q_tok[c]), bank[b]])
                m = mask(b, 0, r, "s")
                o2 = OFF[i]
                if i != 1:
                    pair = (tmps.take(), tmps.take())
                    if i == 3:
                        pair3 = pair
                (k1, t1, w1), (k2, t2, w2) = pair3 if i == 1 else pair
                c0 = 128 if i == 1 else 0
                s1 = lambda t1=t1, n=n, c0=c0: t1[:, c0:c0 + n]
                s2 = lambda t2=t2, n=n, c0=c0: t2[:, c0:c0 + n]
                x4 = ts(dve, s2, o, 0.125, 0.0, ALU.mult, ALU.max, m, w2)
                x1 = stt(s1, s2, -16.0, o, ALU.mult, ALU.add, x4, w1)
                x2 = a_fn(s1, s1, ACT.Exp, x1, scale=0.125)
                bank[b] = [x1, x4]
                later.append((i, n, o2, s1, s2, x2, x4, k1, k2))
            for i, n, o2, s1, s2, x2, x4, k1, k2 in later:
                x3 = a_fn(s1, s1, ACT.Ln, x2, bias=1.0)
                x5 = tt(dve, s2, s2, s1, ALU.add, x3, x4)
                hi, lo = split_sb(lambda o2=o2, n=n: SPh[:, o2:o2 + n], lambda o2=o2, n=n: SPl[:, o2:o2 + n],
                                  s2, x5, sp_free[0])
                tmps.give(k1, x5)
                tmps.give(k2, lo)
                sp_tok[i] = (hi, lo)
            q_free[p] = m

        def mid_a(h):
            for i in (3, 2, 1, 0):
                b, n = 2 + i, T - 128 * i
                for j in range(3, i - 1, -1):
                    nj = T - 128 * j
                    o = lambda b=b, i=i, j=j, n=n: PS[b][:, 128 * (j - i):n]
                    w = lambda i=i, j=j: con_r("tri8" if i == j else "m8")
                    mm(o, w, lambda j=j, nj=nj: SPh[:, OFF[j]:OFF[j] + nj], False, False, sp_tok[j][0], bank[b],
                       t_conr, skip=True)
                    m = mm(o, w, lambda j=j, nj=nj: SPl[:, OFF[j]:OFF[j] + nj], False, j == i, sp_tok[j][1],
                           skip=True, sig=j == i)
                k1, t1, w1 = tmps.take()
                s1 = lambda t1=t1, n=n: t1[:, 0:n]
                x = a_fn(s1, lambda b=b, n=n: PS[b][:, 0:n], ACT.Exp, m, w1, scale=0.125)
                hi, lo = split_sb(lambda i=i, n=n: EWh[:, OFF[i]:OFF[i] + n],
                                  lambda i=i, n=n: EWl[:, OFF[i]:OFF[i] + n], s1, x, ew_free[0])
                tmps.give(k1, lo)
                ew_tok[i] = (hi, lo)
                bank[b] = [x]
            sp_free[0] = m

        def pv_a(h):
            c = h // 2
            b = 6 + h % 2
            for j in range(4):
                nj = T - 128 * j
                o = lambda j=j: PS[b][:, 128 * j:T]
                lh = lambda j=j: VAh[:, j, c * 128:(c + 1) * 128]
                ll = lambda j=j: VAl[:, j, c * 128:(c + 1) * 128]
                rh = lambda j=j, nj=nj: EWh[:, OFF[j]:OFF[j] + nj]
                rl = lambda j=j, nj=nj: EWl[:, OFF[j]:OFF[j] + nj]
                m = mm3(o, lh, ll, rh, rl, j == 0, j == 3, wh=[ew_tok[j][0], va[j][0], va[j][1], bank[b]],
                        wl=[ew_tok[j][1]], sig=j == 3)
            ew_free[0] = m
            return m

        ya_tok = {}
        qk_a(0)
        steps = []
        f_tok = {}

        def f_steps():
            fc = Chunk(("f", 0), 1, *h_r, rtok=lambda k: h_tok[k])

            def fin():
                m = fc.half(1)
                k1, t1, w1 = tmps.take()
                k2, t2, w2 = tmps.take()
                s1 = lambda: t1[0:8, :]
                s2 = lambda: t2[0:8, :]
                x0 = ts(dve, s2, lambda: PS[1][0:8, :], lambda: pcol("b_forget", 0, 8), None, ALU.add, None,
                        m, w2, t_par)
                bank[1] = [x0]
                x1 = a_fn(s1, s2, ACT.Abs, x0, w1)
                x2 = a_fn(s1, s1, ACT.Exp, x1, scale=-1.0)
                x3 = a_fn(s1, s1, ACT.Ln, x2, bias=1.0)
                x4 = ts(dve, s2, s2, 0.0, None, ALU.min, None, x1)
                x5 = tt(dve, s2, s2, s1, ALU.subtract, x3, x4)
                for n in range(4):
                    m = pe(lambda e, n=n: e.transpose(PS[1][:, 8 * n:8 * n + 8], t2[0:8, 128 * n:128 * n + 128],
                                                      con_raw[0:8, 0:8]), x5, bank[1], t_con)
                x6 = cp(dve, lambda: t1[:, 0:32], lambda: PS[1][:, 0:32], m, x5)
                bank[1] = [x6]
                for n in range(4):
                    for b in range(n + 1):
                        m = mm(lambda n=n: PS[1][0:8, 128 * n:128 * n + 128], lambda b=b: t1[:, 8 * b:8 * b + 8],
                               lambda b=b, n=n: con_f("triu" if b == n else "one"), b == 0, b == n, x6, sig=True)
                x7 = ts(dve, s2, lambda: PS[1][0:8, :], -8.0, None, ALU.mult, None, m)
                x8 = cp(dve, lambda: FT[0:8, :], s2, x7, t_fz)
                x9 = tt(dve, s1, s2, lambda: FT[0:8, :].bitcast(F32), ALU.subtract, x8, m)
                x10 = cp(dve, lambda: FT[32:40, :], s1, x9)
                cp(dve, lambda: FT[64:72, :], lambda: FT[0:8, :].bitcast(F32), x8)
                x10 = cp(dve, lambda: FT[96:104, :], lambda: FT[32:40, :].bitcast(F32), x10)
                tmps.give(k1, x10)
                tmps.give(k2, x9)
                bank[1] = [x7]
                f_tok[0] = x10

            return [lambda: fc.half(0), fin]

        t_fz = pool(lambda e: e.memset(FT[:, :].bitcast(F32), 0.0))
        for h in range(8):
            c = h // 2
            if h % 2 == 0:
                steps += q_steps("a", c + 1) if c < 3 else (q_steps("b", 0)[0:4] + f_steps())
            mid_a(h)
            run(steps, 1)
            if h < 7:
                if h % 2 == 1:
                    run(steps, max(0, len(steps) - 2))
                qk_a(h + 1)
            m = pv_a(h)
            t = gate_y(h, m, YAh, YAl, t_mk)
            if t:
                ya_tok[c] = t
            run(steps, 2 if h % 2 == 0 else 9)

        pv_done = m
        vb = vproj("bv", VBh, VBl, None)
        for f in q_steps("b", 0)[4:]:
            f()
        pt_free = [pv_done]

        def softmax_tile(b, n, scale, t, w, tw):
            k = softmax_tile.n % 8
            softmax_tile.n += 1
            cm, cb, cs, cr = (4 * k + x for x in range(4))
            col = lambda x: (lambda: stat[:, x:x + 1])
            x1 = dve(lambda e: e.tensor_reduce(col(cm)(), PS[b][:, 0:n], AX_X, ALU.max, negate=True), w, tw)
            x2 = ts(dve, col(cb), col(cm), scale, None, ALU.mult, None, x1)
            x3 = a_fn(lambda: t[:, 0:n], lambda: PS[b][:, 0:n], ACT.Exp, x2, tw, scale=scale, bias=col(cb),
                      accum=col(cs))
            return x3, (col(cs), col(cr))
        softmax_tile.n = 0

        def softmax_sum(x3, cols):
            cs, cr = cols
            return dve(lambda e: e.reciprocal(cr(), cs()), x3), cr

        pt_tok, pt2 = {}, {}

        def turn(b, nj, t, dh, dl, ready, wfree):
            for j in range(nj):
                m = pe(lambda e, j=j: e.transpose(PS[b][:, 128 * j:128 * j + 128], t[:, 128 * j:128 * j + 128],
                                                  con_f("ident")), ready, t_con, bank[b])
            src = lambda: PS[b][:, 0:128 * nj].rearrange("p (j t) -> p j t", j=nj)
            a, l = split_ps(dh, dl, src, m, wfree)
            bank[b] = [a, l]
            return m, a, l

        def sel(h):
            r = 64 * (h % 2)
            return conr[r:r + 40, CO + h:CO + h + 1].to_broadcast([40, 128])

        def qk_b(h):
            c, r, p = h // 2, 64 * (h % 2), (h // 2) % 2
            later = []
            for i in (3, 2, 1, 0):
                b, n = 2 + i, 128 * (i + 1)
                o = lambda b=b, n=n: PS[b][:, 0:n]
                lh = lambda i=i: Qh[p][r:r + 64, i * 128:(i + 1) * 128]
                ll = lambda i=i: Ql[p][r:r + 64, i * 128:(i + 1) * 128]
                mm3(o, lh, ll, lambda n=n: Kh[p][r:r + 64, 0:n], lambda n=n: Kl[p][r:r + 64, 0:n], True, False,
                    wh=[list(k_tok[c]), list(q_tok[c]), bank[b]])
                mm(o, lambda: sel(h), lambda n=n: FT[r:r + 40, 0:n], False, False, f_tok[0], t_conr)
                m = mask(b, 128 * i, r, "f")
                k1, t1, w1 = tmps.take()
                x3, cols = softmax_tile(b, n, 0.125, t1, m, w1)
                later.append((i, n, k1, t1, x3, cols))
            for i, n, k1, t1, x3, cols in later:
                x4, rc = softmax_sum(x3, cols)
                x5 = a_fn(lambda t1=t1, n=n: t1[:, 0:n], lambda t1=t1, n=n: t1[:, 0:n], ACT.Copy, x4, scale=rc)
                pt_tok[i] = (k1, t1, x3, x5)
            q_free[p] = m

        def mid_b(h):
            for i in (3, 2, 1, 0):
                k1, t1, x3, x5 = pt_tok[i]
                m, a, l = turn(2 + i, i + 1, t1, lambda i=i: PTh[:, 0:i + 1, 128 * i:128 * i + 128],
                               lambda i=i: PTl[:, 0:i + 1, 128 * i:128 * i + 128], [x5, x3], pt_free[0])
                tmps.give(k1, m)
                pt2[i] = (a, l)

        def pv_b(h):
            c = h // 2
            b = 6 + h % 2
            for j in range(4):
                o = lambda j=j: PS[b][:, 128 * j:T]
                lh = lambda j=j: VBh[:, j, c * 128:(c + 1) * 128]
                ll = lambda j=j: VBl[:, j, c * 128:(c + 1) * 128]
                w = [[list(pt2[i]) for i in range(4)], list(vb[j]), bank[b]]
                m = mm3(o, lh, ll, lambda j=j: PTh[:, j, 128 * j:T], lambda j=j: PTl[:, j, 128 * j:T],
                        j == 0, j == 3, wh=w, sig=j == 3)
            pt_free[0] = m
            return m

        yb_tok = {}
        gate_tok = pv_done

        def gate_load(k, tok):
            got = []
            for x, line in enumerate((l_g0, l_g1)):
                k1, t1, w1 = tmps.take()
                tr = None
                if not plan_only:
                    tr = sp.dma(line, lambda e, t1=t1, x=x: e.dma_start(t1[:, :], gate_w[k, :, T * x:T * x + T]), w1, tok)
                got.append((k1, t1, tr))
            return got

        def gate_add(k, got, tok):
            for x, (k1, t1, tr) in enumerate(got):
                o = lambda x=x: MA[:, T * x:T * x + T]
                i = lambda t1=t1: t1[:, :]
                if k == 0:
                    tok = ts(dve, o, i, lambda: pcol("c", k), None, ALU.mult, None, tr, tok)
                else:
                    tok = stt(o, i, lambda: pcol("c", k), o, ALU.mult, ALU.add, tr, tok)
                tmps.give(k1, tok)
            return tok

        qk_b(0)
        steps = []
        for h in range(8):
            c = h // 2
            if h % 2 == 0:
                steps += q_steps("b", c + 1) if c < 3 else []
            mid_b(h)
            got = gate_load(h, gate_tok)
            run(steps, 1)
            if h < 7:
                if h % 2 == 1:
                    run(steps, max(0, len(steps) - 2))
                qk_b(h + 1)
            m = pv_b(h)
            t = gate_y(h, m, VAh, VAl, pv_done)
            if t:
                yb_tok[c] = t
            run(steps, 2 if h % 2 == 0 else 9)
            gate_tok = gate_add(h, got, gate_tok)
        pv_done = m

        t_xr = None
        if not plan_only:
            t_xr = sp.dma(l_x2, lambda e: e.dma_start(X[:, :, :], xin), pv_done)

        def half_unit(name, b0, rh, rl, rtok, n=T):
            s, ta, tb, j = use(name)
            toks = []
            for g in range(2):
                pe.wait(bank[b0 + g])
                for k in range(4):
                    lh = lambda k=k, g=g, s=s: WH[s][:, k * 256 + g * 128:k * 256 + g * 128 + 128]
                    ll = lambda k=k, g=g, s=s: WL[s][:, k * 256 + g * 128:k * 256 + g * 128 + 128]
                    o = lambda g=g: PS[b0 + g][:, :]
                    tok = mm3(o, lh, ll, lambda k=k: rh(k), lambda k=k: rl(k), k == 0, k == 3,
                              wh=[ta, rtok(k)[0]], wl=[tb, rtok(k)[1]], sig=k == 3)
                toks.append(tok)
            used(j, tok)
            return toks

        mg_tok = {}

        def mgh(k):
            return VBh[:, k, :] if k < 4 else MG2h[:, k - 4, :]

        def mgl(k):
            return VBl[:, k, :] if k < 4 else MG2l[:, k - 4, :]

        for u in range(4):
            ta = half_unit(("oa", u), 0, lambda k: YAh[:, k, :], lambda k: YAl[:, k, :], lambda k: ya_tok[k])
            tb = half_unit(("ob", u), 2, lambda k: VAh[:, k, :], lambda k: VAl[:, k, :], lambda k: yb_tok[k])
            for g in range(2):
                f = 2 * u + g
                ms = []
                for x in range(2):
                    b = 4 + 2 * g + x
                    tok = hproj(("g", 8 * x + f), b).both()
                    h_read[0] = tok
                    k1, t1, w1 = tmps.take()
                    sg = a_fn(lambda t1=t1: t1[:, :], lambda b=b: PS[b][:, :], ACT.Sigmoid, tok, w1, t_par,
                              bias=lambda x=x, f=f: pcol("b_gate", 8 * x + f))
                    bank[b] = [sg]
                    yb_, ty = (g, ta[g]) if x == 0 else (2 + g, tb[g])
                    pr = tt(dve, lambda t1=t1: t1[:, :], lambda t1=t1: t1[:, :], lambda yb_=yb_: PS[yb_][:, :],
                            ALU.mult, sg, ty)
                    bank[yb_] = [pr]
                    ms.append((k1, t1, pr))
                (k1, t1, p1), (k2, t2, p2) = ms
                s_ = tt(dve, lambda t1=t1: t1[:, :], lambda t1=t1: t1[:, :], lambda t2=t2: t2[:, :], ALU.add,
                        p1, p2)
                hi, lo = split_sb(lambda f=f: mgh(f), lambda f=f: mgl(f), lambda t1=t1: t1[:, :], s_, pv_done,
                                  lo=pool)
                tmps.give(k1, hi, lo)
                tmps.give(k2, s_)
                mg_tok[f] = (hi, lo)
            if u == 1:
                t_gate, _ = mod_end(2, gate_tok, 0)

        x_rd = [None] * KC
        x_tok = [None] * KC

        def residual(f, b, tok, gname, gate=None, wx=None, both=False):
            if gate is None:
                x = tt(dve, lambda: X[:, f, :], lambda: PS[b][:, :], lambda: X[:, f, :], ALU.add, tok, wx,
                       x_rd[f])
            else:
                x = stt(lambda: X[:, f, :], lambda: PS[b][:, :], gate, lambda: X[:, f, :], ALU.mult, ALU.add,
                        tok, wx)
            bank[b] = [x]
            if gname:
                g = (lambda: sm[:, 40 + f:41 + f]) if both else (lambda: pcol(gname, f))
                hi = a_fn(lambda: HH[:, f, :], lambda: X[:, f, :], ACT.Copy, x, h_read[0], scale=g)
                lo = stt(lambda: HL[:, f, :], lambda: X[:, f, :], g, lambda: HH[:, f, :].bitcast(F32),
                         ALU.mult, ALU.subtract, hi)
                h_tok[f] = (hi, lo)
            sq, add = square(lambda: X[:, f, :], x)
            x_rd[f] = [sq, hi] if gname else [sq]
            x_tok[f] = x
            if both:
                sq2, add2 = square(lambda: X[:, f, :], x, scale=lambda: pcol("final_g", f))
                x_rd[f].append(sq2)

                def adds(b_, ones, first, last):
                    add(b_, ones, first, last)
                    return add2(6, ones, first, last)
                return adds
            return add

        def out_chunks(name, rh, rl, rtok, banks, ks=None):
            return [Chunk((name, f), banks[f % len(banks)], rh, rl, rtok=rtok, ks=ks) for f in range(KC)]

        def out_proj(chunks, gname, gate=None, wx=None, both=False, lead=0, hook=None):
            add = None
            for f in range(KC):
                tok = chunks[f].half(1) if f < lead else chunks[f].both()
                if add:
                    add(7, "o1024", f == 1, False)
                add = residual(f, chunks[f].a[1], tok, gname, gate=(lambda f=f: gate(f)) if gate else None, wx=wx,
                               both=both)
                if hook and f > 0:
                    hook.pop(0)()
            warm(ACT.Sqrt)
            return add(7, "o1024", False, True)

        mg_read = (pe, pe.n)
        lam = lambda a, b: CP[:, 3, 100 + a:100 + b]
        if plan_only:
            t_pos = t_lam = None
        else:
            t_pos = sp.dma(l_pos, lambda e: e.dma_start(CT[:, :].bitcast(I32), posin), mg_read)
            t_lam = sp.dma(l_lam, lambda e: e.dma_start(lam(0, 256), lamin), mg_read)
        tb = {}

        def tables_steps():
            C1 = 6.28125
            C2 = float(np.float32(np.round((2 * np.pi - C1) * 2 ** 20) / 2 ** 20))
            C3 = float(2 * np.pi - C1 - C2)
            MAGIC = 12582912.0
            ang, kr = lambda: STb[:, :], lambda: CT[:, :]

            def s0():
                x = cp(dve, ang, lambda: CT[:, :].bitcast(I32), t_pos, mg_read)
                x = ts(dve, ang, ang, lambda: con_raw[:, CO + 8:CO + 9], None, ALU.mult, None, x, t_con)
                x = ts(dve, kr, ang, float(1 / (2 * np.pi)), MAGIC, ALU.mult, ALU.add, x)
                tb["x"] = ts(dve, kr, kr, MAGIC, None, ALU.subtract, None, x)

            def s1():
                x = stt(ang, kr, -C1, ang, ALU.mult, ALU.add, tb["x"])
                tb["x"] = stt(ang, kr, -C2, ang, ALU.mult, ALU.add, x)

            def s2():
                x = stt(ang, kr, -C3, ang, ALU.mult, ALU.add, tb["x"])
                x = ts(dve, ang, ang, -3.1415925, 3.1415925, ALU.max, ALU.min, x)
                tb["x"] = a_fn(kr, ang, ACT.Abs, x)
                x = tt(dve, lambda: lam(256, 320), lambda: lam(0, 64), lambda: lam(64, 128), ALU.mult, t_lam)
                y = tt(dve, lambda: lam(320, 384), lambda: lam(128, 192), lambda: lam(192, 256), ALU.mult, t_lam)
                tb["l"] = dve(lambda e: e.tensor_reduce(
                    sm[:, 26:28], lam(256, 384).rearrange("p (a b) -> p a b", a=2), AX_X, ALU.add), x, y)

            def s3():
                x = ts(dve, kr, kr, -1.0, float(np.pi / 2), ALU.mult, ALU.add, tb["x"])
                tb["s"] = a_fn(ang, ang, ACT.Sin, tb["x"])
                tb["c"] = a_fn(kr, kr, ACT.Sin, x)

            def s4():
                x = a_fn(lambda: sm[:, 28:30], lambda: sm[:, 26:28], ACT.Exp, tb["l"])
                x = tt(dve, lambda: sm[:, 30:31], lambda: sm[:, 29:30], lambda: sm[:, 28:29], ALU.subtract, x)
                tb["nl"] = ts(dve, lambda: sm[:, 24:25], lambda: sm[:, 30:31], -LAM_INIT, None, ALU.add, None, x)
                tb["sg"] = ts(dve, lambda: sm[:, 25:26], lambda: pcol("subln_g_2"), 1.0 - LAM_INIT, None, ALU.mult,
                              None, t_par)

            return [s0, s1, s2, s3, s4]

        t_fm = tt(dve, lambda: sm[:, 40:48], lambda: par_sb[:, POFF["final_g"]:POFF["final_g"] + 8],
                  lambda: par_sb[:, POFF["norm_mix_g_2"]:POFF["norm_mix_g_2"] + 8], ALU.mult, t_par)
        st_tok = out_proj(out_chunks("wo", mgh, mgl, lambda k: mg_tok[k], (0, 1, 2)), "norm_mix_g_2",
                          gate=lambda f: sm[:, 16 + f:17 + f], wx=[t_xr, t_gate, t_fm], both=True, hook=tables_steps())
        x8, x11, t_nl, t_sg = tb["s"], tb["c"], tb["nl"], tb["sg"]
        rb = lambda: RB[:, :]
        r1 = lambda: YF[:, 0, :]
        x1, c1_ = root_cols(7, st_tok)
        x2_, c2_ = root_cols(6, st_tok, raw=True)
        rc2 = lambda: sm[:, 64:68]
        x2 = tt(dve, rc2, c1_, c1_, ALU.mult, x1)
        x2 = tt(dve, rc2, rc2, c2_, ALU.mult, x2, x2_)
        x3 = a_fn(rc2, rc2, ACT.Sqrt, x2, bias=eps)
        x3 = dve(lambda e: e.reciprocal(rc2(), rc2()), x3)
        t_rc = tt(dve, rc2, rc2, c1_, ALU.mult, x3)
        pre = [hproj(("u", 0), 0).both(), hproj(("u", 4), 1).both()]
        m = spread(7, rc2, t_rc)
        t_rb = cp(dve, rb, lambda: PS[7][:, :], m)
        bank[7] = [t_rb]
        m = spread(6, c1_, x1)
        t_r1 = cp(dve, r1, lambda: PS[6][:, :], m)
        bank[6] = [t_r1]
        for f in range(KC):
            xf = lambda f=f: X[:, f, :]
            x_new = stt(xf, xf, lambda f=f: pcol("final_g", f), r1, ALU.mult, ALU.mult, t_r1, x_rd[f])
        free1 = st_tok

        t_c2 = tt(dve, lambda: CT[:, :], lambda: CT[:, :], rb, ALU.mult, x11, t_rb)
        t_s2 = tt(dve, lambda: STb[:, :], lambda: STb[:, :], rb, ALU.mult, x8, t_rb)
        t_pad = pool(lambda e: e.memset(CP[:, :, 0:30], 0.0), free1)
        cp_tok = {}
        conv_last = {}
        cv_free_ = [sq_free[1], sq_free[1]]
        cv_n = [0]
        conv_steps = []

        def tap(j, x):
            w = lambda: pcol("cv_dw_w_2", 4 * x + j)
            o = lambda: AC[:, j, :]
            i = lambda: CP[:, j, x:x + T]
            if x == 0:
                conv_last[j] = ts(dve, o, i, w, lambda: pcol("cv_dw_b_2", j), ALU.mult, ALU.add, cp_tok[j], t_pad,
                                  free1, t_par)
            else:
                if j % 2 == 0:
                    conv_last[j] = stt(o, i, w, o, ALU.mult, ALU.add, conv_last[j])
                else:
                    v = cv_n[0] % 2
                    cv_n[0] += 1
                    a = a_fn(lambda: CV[v][:, :], i, ACT.Copy, cv_free_[v], cp_tok[j], t_pad, scale=w)
                    conv_last[j] = tt(pool, o, o, lambda: CV[v][:, :], ALU.add, a, conv_last[j])
                    cv_free_[v] = conv_last[j]

        for j0 in (0, 2):
            for x in range(31):
                for j in (j0, j0 + 1):
                    conv_steps.append(lambda j=j, x=x: tap(j, x))

        for j in range(4):
            b0, b1 = ((0, 1), (2, 3), (4, 5), (0, 1))[j]
            ua = pre[0] if j == 0 else hproj(("u", j), b0).both()
            k1, t1, w1 = tmps.take()
            xa = tt(dve, lambda t1=t1: t1[:, :], lambda b0=b0: PS[b0][:, :], rb, ALU.mult, ua, w1, t_rb)
            bank[b0] = [xa]
            ub = pre[1] if j == 0 else hproj(("u", 4 + j), b1).both()
            k2, t2, w2 = tmps.take()
            xb = tt(dve, lambda t2=t2: t2[:, :], lambda b1=b1: PS[b1][:, :], rb, ALU.mult, ub, w2, t_rb)
            bank[b1] = [xb]
            xc = a_fn(lambda t2=t2: t2[:, :], lambda t2=t2: t2[:, :], ACT.Sigmoid, xb)
            xd = tt(dve, lambda j=j: CP[:, j, 30:30 + T], lambda t1=t1: t1[:, :], lambda t2=t2: t2[:, :],
                    ALU.mult, xa, xc, free1, tb["l"])
            tmps.give(k1, xd)
            tmps.give(k2, xd)
            cp_tok[j] = xd
            if j > 0:
                run(conv_steps, 8)
        v2 = vproj("dv", V2h, V2l, free1, scale=lambda t: (lambda: sm[:, 64 + t:65 + t]), stok=t_rc, between=lambda: run(conv_steps, 4))
        dq_tok, dk_tok = {}, {}
        dq_free = [free1, free1]
        rt_free = [free1]

        dq_last = [None]
        rots = []

        def d_steps(h):
            p = h % 2
            out_ = []
            for b, nm, dh, dl, dt in ((0, "dq", DQh, DQl, dq_tok), (1, "dk", DKh, DKl, dk_tok)):
                ch = Chunk((nm, h), b, *h_r, rtok=lambda k: h_tok[k])

                def second(b=b, ch=ch, dh=dh, dl=dl, dt=dt):
                    m = ch.half(1)
                    dq_last[0] = m
                    ps = lambda: PS[b][:, :]
                    hi, lo = split_ps(lambda: RTh[:, :], lambda: RTl[:, :], ps, m, rt_free[0])
                    k1, t1, w1 = tmps.take()
                    x1 = tt(dve, lambda: t1[:, :], ps, lambda: CT[:, :], ALU.mult, m, w1, t_c2)

                    def third():
                        mm(ps, lambda: con_r("rot"), lambda: RTh[:, :], True, False, hi, lo, x1, t_conr)
                        m2 = mm(ps, lambda: con_r("rot"), lambda: RTl[:, :], False, True, lo, sig=True)
                        rt_free[0] = m2
                        k2, t2, w2 = tmps.take()
                        x2 = tt(dve, lambda: t2[:, :], ps, lambda: STb[:, :], ALU.mult, m2, w2, t_s2)
                        bank[b] = [x2]
                        x3 = tt(dve, lambda: t2[:, :], lambda: t2[:, :], lambda: t1[:, :], ALU.add, x2, x1)
                        dt[h] = split_sb(lambda: dh[p][:, :], lambda: dl[p][:, :], lambda: t2[:, :], x3, dq_free[p])
                        tmps.give(k1, x3)
                        tmps.give(k2, dt[h][1])

                    rots.append(third)

                out_ += [lambda ch=ch: ch.half(0), second]
            return out_

        at_tok = {}
        at_free = [free1]
        yf_tok = {}

        def qk_d(n_):
            h, i = n_ // 4, n_ % 4
            p, n = h % 2, 128 * (i + 1)
            got = []
            for c in range(2):
                b = 2 + 2 * (n_ % 2) + c
                r = 64 * c
                o = lambda b=b: PS[b][:, 0:n]
                mm3(o, lambda r=r: DQh[p][r:r + 64, 128 * i:128 * i + 128],
                    lambda r=r: DQl[p][r:r + 64, 128 * i:128 * i + 128],
                    lambda r=r: DKh[p][r:r + 64, 0:n], lambda r=r: DKl[p][r:r + 64, 0:n], True, False,
                    wh=[list(dq_tok[h]), list(dk_tok[h]), bank[b]])
                m = mask(b, 128 * i, r, "f")
                k1, t1, w1 = tmps.take()
                x3, cols = softmax_tile(b, n, 0.125, t1, m, w1)
                got.append((k1, t1, x3, cols))
                bank[b] = [x3]
                run(conv_steps, 1)
            at_tok[n_] = got
            if i == 3:
                dq_free[p] = m

        def join_d(n_):
            n = 128 * (n_ % 4 + 1)
            (k1, t1, e1, s1), (k2, t2, e2, s2) = at_tok[n_]
            r1, c1 = softmax_sum(e1, s1)
            r2, c2 = softmax_sum(e2, s2)
            n1 = lambda: t1[:, 0:n]
            n2 = lambda: t2[:, 0:n]
            x5 = a_fn(n1, n1, ACT.Copy, e1, r1, scale=c1)
            x6 = ts(dve, c2, c2, lambda: sm[:, 24:25], None, ALU.mult, None, r2, t_nl)
            x7 = stt(n2, n2, c2, n1, ALU.mult, ALU.add, x6, x5, e2)
            tmps.give(k1, x7)
            at_tok[n_] = (k2, t2, x7)

        def turn_d(n_):
            i = n_ % 4
            k2, t2, x7 = at_tok[n_]
            o = 128 * (i % 2)
            m, a, l = turn(6, i + 1, t2, lambda: ATh[:, 0:i + 1, o:o + 128], lambda: ATl[:, 0:i + 1, o:o + 128],
                           [x7], at_free[0])
            tmps.give(k2, m)
            at_tok[n_] = (a, l)

        def pv_d(s):
            h, half = s // 2, s % 2
            b = 7
            js = 2 * half + 2
            for j in range(js):
                o0 = max(0, 128 * j - 256 * half)
                o = lambda o0=o0: PS[b][:, o0:256]
                w = [list(at_tok[2 * s + 1]), list(at_tok[2 * s]), list(v2[j]), bank[b]]
                m = mm3(o, lambda j=j: V2h[:, j, h * 128:(h + 1) * 128], lambda j=j: V2l[:, j, h * 128:(h + 1) * 128],
                        lambda j=j, o0=o0: ATh[:, j, o0:256], lambda j=j, o0=o0: ATl[:, j, o0:256],
                        j == 0, j == js - 1, wh=w, sig=j == js - 1)
            at_free[0] = m
            x = a_fn(lambda: YF[:, h, 256 * half:256 * half + 256], lambda: PS[b][:, 0:256], ACT.Copy, m, x_new, t_rb)
            bank[b] = [x]
            yf_tok[s] = x
            return m

        yc_tok = {}
        ln = {}

        def ln_mean(j):
            p = j % 2
            hi, lo = split_sb(lambda: SQh[p][:, :], lambda: SQl[p][:, :], lambda: AC[:, j, :],
                              conv_last[j], sq_free[p])
            mm(lambda: PS[0][:, :], lambda: con_r("o512"), lambda: SQh[p][:, :], j == 0, False, hi,
               bank[0] if j == 0 else None)
            ln["m"] = sq_free[p] = mm(lambda: PS[0][:, :], lambda: con_r("o512"), lambda: SQl[p][:, :], False, j == 3,
                                      lo, sig=True)

        def ln_diff(j):
            ln[j] = tt(dve, lambda: AC[:, j, :], lambda: PS[0][:, :], lambda: AC[:, j, :], ALU.subtract, ln["m"])
            bank[0] = [ln[j]]

        def ln_sq(j):
            _, add = square(lambda: AC[:, j, :], ln[j])
            ln["v"] = add(1, "o512", j == 0, j == 3)

        def ln_root():
            r_, c_ = root_cols(1, ln["v"])
            ln["s"] = spread(1, c_, r_)

        def ln_out(j):
            k1, t1, w1 = late_t.take()
            s1 = lambda: t1[:, :]
            x1 = stt(s1, lambda: AC[:, j, :], -1.0, lambda: PS[1][:, :], ALU.mult, ALU.mult, ln["s"], ln[j], w1)
            x2 = a_fn(s1, s1, ACT.Silu, x1, t_par, scale=lambda: pcol("cv_ln_g_2", j),
                      bias=lambda: pcol("cv_ln_b_2", j))
            yc_tok[j] = split_sb(lambda: YCh[:, j, :], lambda: YCl[:, j, :], s1, x2, [conv_last[x] for x in range(4)],
                                 lo=pool)
            bank[1] = [x1]
            late_t.give(k1, *yc_tok[j])

        yd_tok = {}
        sub = {}

        def sub_sum(h, b):
            if h < 2:
                sq_n[0] = 0
            _, add = square(lambda: YF[:, h, :], yf_tok[2 * h], yf_tok[2 * h + 1])
            sub[h] = root_cols(b, add(b, "o128", True, True))

        def sub_out(h, b):
            r_, c_ = sub[h]
            m = spread(b, c_, r_)
            k1, t1, w1 = late_t.take()
            s1 = lambda: t1[:, :]
            x1 = stt(s1, lambda: YF[:, h, :], lambda: sm[:, 25:26], lambda: PS[b][:, :], ALU.mult, ALU.mult, m,
                     t_sg, w1)
            bank[b] = [x1]
            yd_tok[h] = split_sb(lambda: YDh[:, h, :], lambda: YDl[:, h, :], s1, x1, dq_free[0], lo=pool)
            late_t.give(k1, *yd_tok[h])

        wo2 = out_chunks("wo2", lambda k: YDh[:, k, :] if k < 4 else YCh[:, k - 4, :],
                         lambda k: YDl[:, k, :] if k < 4 else YCl[:, k - 4, :],
                         lambda k: yd_tok[k] if k < 4 else yc_tok[k - 4], (2, 3, 4, 5), (4, 5, 6, 7, 0, 1, 2, 3))
        for f in d_steps(0):
            f()
            run(conv_steps, 4)
            run(rots, 1)
        steps = d_steps(1)
        qk_d(0)
        run(steps, 2)
        qk_d(1)
        run(rots, 1)
        join_d(0)
        late = {10: [lambda: sub_sum(0, 0), lambda: sub_sum(1, 1), lambda: sub_out(0, 0), lambda: sub_out(1, 1)],
                11: [lambda: ln_mean(0), lambda: ln_mean(1), lambda: ln_mean(2), lambda: ln_mean(3)],
                12: [lambda: ln_diff(0), lambda: ln_diff(1), lambda: ln_diff(2), lambda: ln_diff(3),
                     lambda: ln_sq(0), lambda: ln_sq(1), lambda: ln_sq(2), lambda: ln_sq(3)],
                13: [ln_root, lambda: ln_out(0), lambda: ln_out(1), lambda: ln_out(2), lambda: ln_out(3)],
                14: [lambda: sub_sum(2, 0), lambda: wo2[0].half(0), lambda: sub_out(2, 0), lambda: wo2[1].half(0)],
                15: [lambda: wo2[2].half(0), lambda: wo2[3].half(0)]}
        for n in range(16):
            h = n // 4
            if n % 4 == 2 and h < 2:
                steps = d_steps(h + 2)
            if n == 10:
                scr[0] = late_t
                late_t.last = [rt_free[0], rt_free[0]]
            more = late.get(n, [])
            run(steps, 1)
            run(conv_steps, 3)
            if n < 14:
                qk_d(n + 2)
            if n > 0 and n % 2 == 0:
                pv_d(n // 2 - 1)
            turn_d(n)
            run(rots, 1)
            run(conv_steps, 2)
            if n < 15:
                join_d(n + 1)
            run(more, 99)
            if n == 10:
                run(conv_steps, 999)
                sq_free[1] = [sq_free[1], *cv_free_]
            if n == 15:
                m = pv_d(7)
        h_read[0] = dq_last[0]
        att_done = m
        t_mem = None
        if not plan_only:
            t_mem = sp.dma(l_mem, lambda e: e.dma_start(MEMT[:, :, :], memin), att_done)
        m_tok = [None] * KC
        mm_ = {}

        def mem_steps():
            def squares(k0):
                for k in range(k0, k0 + 4):
                    k1, t1, w1 = tmps.take()
                    x = a_fn(lambda t1=t1: t1[:, 0:M], lambda k=k: MEMT[:, k, :], ACT.Square, t_mem, w1)
                    h = a_fn(lambda k=k: MTh[:, k, :], lambda t1=t1: t1[:, 0:M], ACT.Copy, x, att_done)
                    l = tt(pool, lambda k=k: MTl[:, k, :], lambda t1=t1: t1[:, 0:M],
                           lambda k=k: MTh[:, k, :].bitcast(F32), ALU.subtract, h, att_done)
                    tmps.give(k1, l)
                    m_tok[k] = (h, l)

            def sums():
                for k in range(KC):
                    for x, op in enumerate((MTh, MTl)):
                        mm_["s"] = mm(lambda: PS[6][:, 0:M], lambda: con_r("o1024"),
                                      lambda op=op, k=k: op[:, k, :], k == 0 and x == 0, k == 7 and x == 1,
                                      m_tok[k][x], bank[6] if k == 0 else None, sig=True)

            def last():
                r, c = root_cols(6, mm_["s"], n=M)
                m = spread(6, c, r, n=M)
                mm_["r"] = cp(dve, lambda: MRB[:, :], lambda: PS[6][:, 0:M], m)
                bank[6] = [mm_["r"]]

            def out(k0):
                for k in range(k0, k0 + 4):
                    k1, t1, w1 = tmps.take()
                    s1 = lambda t1=t1: t1[:, 0:M]
                    x1 = stt(s1, lambda k=k: MEMT[:, k, :], lambda k=k: pcol("norm_mem_g_2", k), lambda: MRB[:, :],
                             ALU.mult, ALU.mult, mm_["r"], w1)
                    m_tok[k] = split_sb(lambda k=k: MTh[:, k, :], lambda k=k: MTl[:, k, :], s1, x1, att_done, lo=pool)
                    tmps.give(k1, *m_tok[k])
                mm_["e"] = x1

            return [lambda: squares(0), lambda: squares(4), sums, last, lambda: out(0), lambda: out(4)]

        sub_late = [lambda: sub_sum(3, 0), lambda: sub_out(3, 0)]
        for f in sub_late:
            f()
        scr[0] = tmps
        st_tok = out_proj(wo2, "norm_cross_g_2", lead=4, hook=mem_steps())
        mem_read = mm_["e"]
        cq_pre = {}

        def cq_first():
            for f in (0, 1):
                cq_pre[f] = hproj(("cq", f), f).both()

        a, t_rb = root(rb, 7, st_tok, ahead_=cq_first)
        free2 = st_tok

        cq_tok, ck_tok, cv_tok = {}, {}, {}
        ck_free = [free2, free2]
        cv_free = [[free2, mem_read], [free2, mem_read]]
        m_r = (lambda k: MTh[:, k, :], lambda k: MTl[:, k, :])

        def c_steps(h):
            p = h % 2
            out_ = []
            for g in range(2):
                f = 2 * h + g
                ch = Chunk(("ck", f), g, *m_r, rtok=lambda k: m_tok[k], n=M)

                def fin(f=f, g=g, ch=ch):
                    m = ch.half(1)
                    ck_tok[f] = split_ps(lambda: CKh[p][:, g, :], lambda: CKl[p][:, g, :],
                                         lambda: PS[g][:, 0:M], m, ck_free[p])
                    bank[g] = list(ck_tok[f])
                out_ += [lambda ch=ch: ch.half(0), fin]

            def vals():
                for u in range(2):
                    s, ta, tb, j = use(("cv", h, u))
                    for mt in range(2):
                        if u == 0:
                            pe.wait(bank[mt])
                        for kk in range(4):
                            k = 4 * u + kk
                            o = lambda mt=mt: PS[mt][:, 0:256]
                            lh = lambda k=k, mt=mt: MTh[:, k, mt * 128:(mt + 1) * 128]
                            ll = lambda k=k, mt=mt: MTl[:, k, mt * 128:(mt + 1) * 128]
                            rh = lambda s=s, kk=kk: WH[s][:, kk * 256:(kk + 1) * 256]
                            rl = lambda s=s, kk=kk: WL[s][:, kk * 256:(kk + 1) * 256]
                            mm(o, lh, rh, k == 0, False, ta, list(m_tok[k]))
                            mm(o, lh, rl, False, False, tb)
                            tok = mm(o, ll, rh, False, k == 7, sig=kk == 3)
                        if u == 1:
                            cv_tok[h, mt] = split_ps(lambda mt=mt: CVh[p][:, mt, :], lambda mt=mt: CVl[p][:, mt, :],
                                                     lambda mt=mt: PS[mt][:, 0:256], tok, cv_free[p])
                            bank[mt] = list(cv_tok[h, mt])
                    used(j, tok)
            out_.append(vals)
            q_out = []
            for g in range(2):
                f = 2 * h + g
                ch = None if f in cq_pre else hproj(("cq", f), g)

                def fin(f=f, g=g, ch=ch):
                    m = ch.half(1) if ch else cq_pre[f]
                    k1, t1, w1 = tmps.take()
                    x = tt(dve, lambda: t1[:, :], lambda: PS[g][:, :], rb, ALU.mult, m, t_rb, w1)
                    bank[g] = [x]
                    cq_tok[f] = split_sb(lambda: Oh[:, f, :], lambda: Ol[:, f, :], lambda: t1[:, :], x, free2,
                                         mem_read)
                    tmps.give(k1, cq_tok[f][1])
                q_out += ([lambda ch=ch: ch.half(0)] if ch else []) + [fin]
            out_ = out_ + q_out if h else q_out + out_
            return out_

        cp_free = [free2]
        ct_tok, ct2 = {}, {}

        def qk_c(h):
            p = h % 2
            later = []
            for i in range(4):
                b = 2 + i
                for g in range(2):
                    f = 2 * h + g
                    m = mm3(lambda b=b: PS[b][:, 0:M], lambda f=f, i=i: Oh[:, f, 128 * i:128 * i + 128],
                            lambda f=f, i=i: Ol[:, f, 128 * i:128 * i + 128],
                            lambda g=g: CKh[p][:, g, :], lambda g=g: CKl[p][:, g, :], g == 0, g == 1,
                            wh=[list(cq_tok[f]), list(ck_tok[f]), bank[b]], sig=g == 1)
                k1, t1, w1 = tmps.take()
                x3, cols = softmax_tile(b, M, 1.0 / 16, t1, m, w1)
                bank[b] = [x3]
                later.append((i, k1, t1, x3, cols))
            for i, k1, t1, x3, cols in later:
                x4, rc = softmax_sum(x3, cols)
                x5 = ts(dve, lambda t1=t1: t1[:, 0:M], lambda t1=t1: t1[:, 0:M], rc, None, ALU.mult, None, x4, x3)
                ct_tok[i] = (k1, t1, x5)
            ck_free[p] = m
            qk_c.last = m

        def mid_c(h):
            for i in range(4):
                k1, t1, x5 = ct_tok[i]
                m, a, l = turn(2 + i, 2, t1, lambda i=i: CPh[:, :, 128 * i:128 * i + 128],
                               lambda i=i: CPl[:, :, 128 * i:128 * i + 128], [x5], cp_free[0])
                tmps.give(k1, m)
                ct2[i] = (a, l)

        o_tok = {}

        def pv_c(h, q_done):
            p = h % 2
            for g in range(2):
                f, b = 2 * h + g, 6 + g
                for mt in range(2):
                    m = mm3(lambda b=b: PS[b][:, :], lambda mt=mt, g=g: CVh[p][:, mt, 128 * g:128 * g + 128],
                            lambda mt=mt, g=g: CVl[p][:, mt, 128 * g:128 * g + 128],
                            lambda mt=mt: CPh[:, mt, :], lambda mt=mt: CPl[:, mt, :], mt == 0, mt == 1,
                            wh=[[list(ct2[i]) for i in range(4)], list(cv_tok[h, mt]), bank[b]], sig=mt == 1)
                o_tok[f] = split_ps(lambda f=f: Oh[:, f, :], lambda f=f: Ol[:, f, :], lambda b=b: PS[b][:, :], m,
                                    q_done)
                bank[b] = list(o_tok[f])
            cp_free[0] = m
            cv_free[p] = m

        for f in c_steps(0):
            f()
        qk_c(0)
        steps = []
        for h in range(4):
            if h < 3:
                steps += c_steps(h + 1)
            run(steps, 3)
            q_done = qk_c.last
            mid_c(h)
            run(steps, 3)
            if h < 3:
                run(steps, 99)
                qk_c(h + 1)
            pv_c(h, q_done)
        h_read[0] = (pe, pe.n)
        st_tok = out_proj(out_chunks("co", lambda k: Oh[:, k, :], lambda k: Ol[:, k, :], lambda k: o_tok[k], (0, 1, 2)),
                          "norm_ffn_g_2")
        up_pre = {}

        def up_first():
            for f, b in ((0, 0), (22, 1), (1, 2), (23, 3)):
                up_pre[f] = hproj(("up", f), b).both()

        a, t_rb = root(rb, 7, st_tok, ahead_=up_first)
        free3 = st_tok

        cb_tok = [pool(lambda e, i=i: e.memset(CB[i][:, 0:2], 0.0), free3) for i in range(4)]
        cb_n = [0]
        cb_free = [None] * 4
        z_tok, z_free = {}, {}

        def conv3(f, b):
            tok = up_pre.pop(f) if f in up_pre else hproj(("up", f), b).both()
            q = cb_n[0] % 4
            cb_n[0] += 1
            x1 = tt(dve, lambda: CB[q][:, 2:2 + T], lambda: PS[b][:, :], rb, ALU.mult, tok, t_rb, cb_free[q], free3)
            bank[b] = [x1]
            k1, t1, w1 = tmps.take()
            s1 = lambda: t1[:, :]
            x2 = a_fn(s1, lambda: CB[q][:, 2:2 + T], ACT.Copy, x1, w1, scale=lambda: pcol("ffn_dw_w_2", 88 + f))
            x3 = stt(s1, lambda: CB[q][:, 1:1 + T], lambda: pcol("ffn_dw_w_2", 44 + f), s1, ALU.mult, ALU.add, x2,
                     cb_tok[q])
            x4 = stt(s1, lambda: CB[q][:, 0:T], lambda: pcol("ffn_dw_w_2", f), s1, ALU.mult, ALU.add, x3)
            cb_free[q] = x4
            return k1, t1, x4

        def up(n):
            s = n % NZ
            k1, t1, x1 = conv3(n, 2 * (n % 2))
            g = a_fn(lambda: t1[:, :], lambda: t1[:, :], ACT.Silu, x1)
            k2, t2, x2 = conv3(22 + n, 2 * (n % 2) + 1)
            z = tt(dve, lambda: t2[:, :], lambda: t2[:, :], lambda: t1[:, :], ALU.mult, g, x2)
            z_tok[n] = split_sb(lambda: ZH[:, s, :], lambda: ZL[:, s, :], lambda: t2[:, :], z, z_free.get(s), free3,
                                lo=pool)
            tmps.give(k1, z)
            tmps.give(k2, *z_tok[n])

        def down(g, last):
            add = None
            nk = min(8, 22 - 8 * g)
            for f in range(KC):
                b = 4 + f % 2
                zz = [(8 * g + k) % NZ for k in range(nk)]
                tok = Chunk(("down", g, f), b, lambda k: ZH[:, zz[k], :], lambda k: ZL[:, zz[k], :], nk=nk,
                            rtok=lambda k: z_tok[8 * g + k]).both()
                if last:
                    if add:
                        add(7, "o1024", f == 1, False)
                    add = residual(f, b, tok, None)
                else:
                    xf = lambda f=f: X[:, f, :]
                    x = tt(dve, xf, lambda b=b: PS[b][:, :], xf, ALU.add, tok, x_rd[f])
                    bank[b] = [x]
                    x_rd[f] = [x]
            for s in zz:
                z_free[s] = tok
            return add(7, "o1024", False, True) if last else None

        for n in range(9):
            up(n)
        down(0, False)
        for n in range(9, 17):
            up(n)
        down(1, False)
        for n in range(17, 22):
            up(n)
        st_tok = down(2, True)
        a, t_rb = root(rb, 7, st_tok)
        for f in range(KC):
            x = stt(lambda f=f: X[:, f, :], lambda f=f: X[:, f, :], lambda f=f: pcol("norm_final_g_2", f), rb,
                    ALU.mult, ALU.mult, t_rb, x_rd[f])
            if not plan_only:
                t_out = sp.dma(l_out, lambda e, f=f: e.dma_start(out[f * 128:(f + 1) * 128, :], X[:, f, :]), x)
        if plan_only:
            return names
        sp.wait(t_out)
        assert state["use"] == len(order) and state["dma"] == len(order), state

        for q in (pe, act, dve, pool, sp):
            q.sem = st.enter_context(nc.semaphore("s_" + q.name))
        for l in lines:
            l.sem = st.enter_context(nc.semaphore(l.name))
        with nc.Block() as block:
            block.tensor(lambda e: pe.emit(e))
            block.scalar(lambda e: act.emit(e))
            block.vector(lambda e: dve.emit(e))
            block.gpsimd(lambda e: pool.emit(e))
            block.sync(lambda e: sp.emit(e))
    return names


def pack_units(order, w):
    def cols(a, c0, n=128, k0=0, nk=8):
        blk = a[128 * k0:128 * (k0 + nk), c0:c0 + n]
        if blk.shape[1] < n:
            blk = np.concatenate([blk, np.zeros((blk.shape[0], n - blk.shape[1]), blk.dtype)], axis=1)
        return blk.reshape(nk, 128, n).transpose(1, 0, 2).reshape(128, nk * n)

    win, wada, wsb, wfox, wout = w["w_in"][0], w["w_ada"][0], w["w_o_sb"][0], w["w_o_fox"][0], w["w_out"][0]
    win2, wout2, wcq, wckv, wco = w["w_in_2"][0], w["w_out_2"][0], w["w_cq_2"][0], w["w_ckv_2"][0], w["w_co_2"][0]
    wup, wdown = w["w_up_2"][0], w["w_down_2"][0]
    res = np.zeros((len(order), 128, U), np.float32)
    for n, u in enumerate(order):
        k = u[0]
        if k == "ada":
            b = wada[128 * u[2]:128 * u[2] + 128, 1024 * u[1]:1024 * u[1] + 1024]
        elif k in ("aq", "ak", "az", "bq", "bk", "bz"):
            o = {"aq": 0, "ak": 512, "az": 1536, "bq": 2048, "bk": 2560, "bz": 3584}[k]
            b = cols(win, o + 128 * u[1])
        elif k in ("av", "bv"):
            b = cols(win, 1024 if k == "av" else 3072, 512, 2 * u[1], 2)
        elif k == "f":
            b = cols(win[:, 4096:4104], 0)
        elif k == "g":
            b = cols(win, 4104 + 128 * u[1])
        elif k in ("oa", "ob"):
            b = cols(wsb if k == "oa" else wfox, 256 * u[1], 256, 0, 4)
        elif k == "wo":
            b = cols(wout, 128 * u[1])
        elif k == "u":
            b = cols(win2, 1536 + 128 * u[1])
        elif k == "dq":
            b = cols(win2, 128 * u[1])
        elif k == "dk":
            b = cols(win2, 512 + 128 * u[1])
        elif k == "dv":
            b = cols(win2, 1024, 512, 2 * u[1], 2)
        elif k == "wo2":
            b = cols(wout2, 128 * u[1])
        elif k == "cq":
            b = cols(wcq, 128 * u[1])
        elif k == "ck":
            b = cols(wckv, 128 * u[1])
        elif k == "cv":
            b = cols(wckv, 1024 + 256 * u[1], 256, 4 * u[2], 4)
        elif k == "co":
            b = cols(wco, 128 * u[1])
        elif k == "up":
            b = cols(wup, 128 * u[1])
        elif k == "down":
            b = cols(wdown, 128 * u[2], 128, 8 * u[1], min(8, 22 - 8 * u[1]))
        res[n, :, 0:b.shape[1]] = b
    return res


def pack_params(w):
    res = np.zeros((128, NPAR), np.float32)
    for name, n in PARAMS:
        a = np.asarray(w[name])
        o = POFF[name]
        if name == "b_forget":
            res[0:8, o] = a.reshape(8)
        elif name == "cv_dw_w_2":
            res[:, o:o + n] = a.reshape(31, 4, 128).transpose(2, 0, 1).reshape(128, n)
        elif name == "ffn_dw_w_2":
            res[:, o:o + n] = a.reshape(3, 44, 128).transpose(2, 0, 1).reshape(128, n)
        else:
            res[:, o:o + n] = a.reshape(n, 128).T
    return res


def kernel(**inputs):
    import concourse.bacc as bacc
    from concourse.bass_utils import run_bass_kernel_spmd

    w = {k: np.asarray(v) for k, v in inputs.items()}
    order = build(None, None)
    arrays = {
        "units": pack_units(order, w),
        "gate_w": np.ascontiguousarray(w["w_ada"][0][:, 2048:3072].reshape(KC, 128, 1024)),
        "par": pack_params(w),
        "con": constants(),
        "msk": masks(),
        "xin": np.ascontiguousarray(w["x"][0].T.reshape(KC, 128, T).transpose(1, 0, 2)),
        "memin": np.ascontiguousarray(w["mem_2"][0].T.reshape(KC, 128, M).transpose(1, 0, 2)),
        "posin": np.ascontiguousarray(np.broadcast_to(w["positions_2"][0], (128, T))),
        "lamin": np.ascontiguousarray(np.broadcast_to(np.concatenate(
            [w[n][0] for n in ("lam_q1_2", "lam_k1_2", "lam_q2_2", "lam_k2_2")]), (128, 256))),
    }
    nc = bacc.Bacc("TRN2", target_bir_lowering=False, num_devices=1)
    args = [nc.dram_tensor(n, a.shape, mybir.dt.from_np(a.dtype), kind="ExternalInput").ap()
            for n, a in arrays.items()]
    args.append(nc.dram_tensor("out", (D, T), F32, kind="ExternalOutput").ap())
    build(nc, args, order)
    r = run_bass_kernel_spmd(nc, [arrays], core_ids=[0])
    return np.ascontiguousarray(r.results[0]["out"].T).reshape(1, T, D)
```
